# Optimizing a Trainium2 kernel written in Bass

```python
import jax, jax.numpy as jnp
from jax import lax
import numpy as np
import jax
import jax.numpy as jnp

D_MODEL = 2048
BATCH = 1
SEQ = 256
DEPTH = 1

HEAD_DIM = 128
N_HEADS_A = 8
N_HEADS_B = 8
D_A = N_HEADS_A * HEAD_DIM
D_B = N_HEADS_B * HEAD_DIM
D_MIX = D_A + D_B
IDX_HEADS = 16
IDX_DIM = 64
DSA_TOPK_MAX = 256
MOBA_BLOCK = 256
MOBA_TOPK_MAX = 3
DSA_Q_CHUNK = 64
MOBA_Q_CHUNK = 16
RMS_EPS = 1e-6
NEG_INF = -1e30

COL_WIDTHS = [D_A, D_A, D_A, D_A,
              IDX_HEADS * IDX_DIM, IDX_DIM, IDX_HEADS,
              D_B, D_B, D_B, D_B]
D_IN = sum(COL_WIDTHS)
COL_SPLITS = [int(s) for s in np.cumsum(COL_WIDTHS)[:-1]]


def _rms_norm(x, g):
    xf = x.astype(jnp.float32)
    y = xf * lax.rsqrt(jnp.mean(xf * xf, axis=-1, keepdims=True) + RMS_EPS)
    return (y * g.astype(jnp.float32)).astype(x.dtype)

def _alibi_slopes(n):
    return jnp.asarray(2.0 ** (-8.0 * np.arange(1, n + 1) / n), dtype=jnp.float32)

def _dsa_attention(q, k, v, q_idx, k_idx, w_idx, slopes):
    B, L, H, Dh = q.shape
    top_k = min(DSA_TOPK_MAX, L // 4)
    n_chunks = L // DSA_Q_CHUNK
    key_pos = jnp.arange(L)
    gather = jax.vmap(lambda t, i: t[i])

    def to_chunks(t):
        return jnp.swapaxes(t.reshape((B, n_chunks, DSA_Q_CHUNK) + t.shape[2:]), 0, 1)

    def chunk_fn(args):
        start, qc, qic, wc = args
        q_pos = start + jnp.arange(DSA_Q_CHUNK)
        logits = jnp.einsum('bqhd,bsd->bqhs', qic, k_idx).astype(jnp.float32) * IDX_DIM ** -0.5
        score = jnp.einsum('bqh,bqhs->bqs', wc.astype(jnp.float32), jax.nn.relu(logits)) * IDX_HEADS ** -0.5
        causal = key_pos[None, :] <= q_pos[:, None]
        score = jnp.where(causal[None], score, NEG_INF)
        _, sel = lax.top_k(score, top_k)
        valid = sel <= q_pos[None, :, None]
        k_sel = gather(k, sel)
        v_sel = gather(v, sel)
        s = jnp.einsum('bqhd,bqkhd->bqhk', qc, k_sel).astype(jnp.float32) * Dh ** -0.5
        dist = (q_pos[None, :, None] - sel).astype(jnp.float32)
        s = s - slopes[None, None, :, None] * dist[:, :, None, :]
        s = jnp.where(valid[:, :, None, :], s, NEG_INF)
        p = jax.nn.softmax(s, axis=-1).astype(v.dtype)
        return jnp.einsum('bqhk,bqkhd->bqhd', p, v_sel)

    starts = jnp.arange(n_chunks) * DSA_Q_CHUNK
    out = lax.map(chunk_fn, (starts, to_chunks(q), to_chunks(q_idx), to_chunks(w_idx)))
    return jnp.swapaxes(out, 0, 1).reshape(B, L, H, Dh)

def _moba_attention(q, k, v, slopes):
    B, L, H, Dh = q.shape
    nb = -(-L // MOBA_BLOCK)
    Lp = nb * MOBA_BLOCK
    pad = ((0, 0), (0, Lp - L), (0, 0), (0, 0))
    kp = jnp.pad(k, pad)
    vp = jnp.pad(v, pad)
    qp = jnp.pad(q, pad)
    scale = Dh ** -0.5
    offs = jnp.arange(MOBA_BLOCK)
    qb = qp.reshape(B, nb, MOBA_BLOCK, H, Dh)
    kb = kp.reshape(B, nb, MOBA_BLOCK, H, Dh)
    vb = vp.reshape(B, nb, MOBA_BLOCK, H, Dh)

    s_self = jnp.einsum('bnqhd,bnshd->bnhqs', qb, kb).astype(jnp.float32) * scale
    rel = offs[:, None] - offs[None, :]
    s_self = s_self - slopes[:, None, None] * rel.astype(jnp.float32)
    s_self = jnp.where(rel >= 0, s_self, NEG_INF)
    lse_self = jax.nn.logsumexp(s_self, axis=-1)
    p_self = jnp.exp(s_self - lse_self[..., None]).astype(v.dtype)
    o_self = jnp.einsum('bnhqs,bnshd->bnqhd', p_self, vb).reshape(B, Lp, H, Dh)[:, :L]
    lse_self = jnp.swapaxes(lse_self, 2, 3).reshape(B, Lp, H)[:, :L]

    top_k = min(MOBA_TOPK_MAX, nb - 1)
    if top_k == 0:
        return o_self.astype(q.dtype)

    k_mean = jnp.mean(kb.astype(jnp.float32), axis=2)
    gate = jnp.einsum('bthd,bnhd->bthn', q.astype(jnp.float32), k_mean)
    q_blk = jnp.arange(L) // MOBA_BLOCK
    past = jnp.arange(nb)[None, :] < q_blk[:, None]
    gate = jnp.where(past[None, :, None, :], gate, NEG_INF)
    _, sel = lax.top_k(gate, top_k)

    k_bh = jnp.transpose(kb, (0, 3, 1, 2, 4))
    v_bh = jnp.transpose(vb, (0, 3, 1, 2, 4))
    bi = jnp.arange(B)[:, None, None, None]
    hi = jnp.arange(H)[None, None, :, None]
    n_chunks = L // MOBA_Q_CHUNK

    def to_chunks(t):
        return jnp.swapaxes(t.reshape((B, n_chunks, MOBA_Q_CHUNK) + t.shape[2:]), 0, 1)

    def chunk_fn(args):
        start, qc, sc = args
        q_pos = start + jnp.arange(MOBA_Q_CHUNK)
        valid = sc < (q_pos // MOBA_BLOCK)[None, :, None, None]
        k_g = k_bh[bi, hi, sc]
        v_g = v_bh[bi, hi, sc]
        s = jnp.einsum('bqhd,bqhjsd->bqhjs', qc, k_g).astype(jnp.float32) * scale
        key_pos = sc[..., None] * MOBA_BLOCK + offs
        dist = (q_pos[None, :, None, None, None] - key_pos).astype(jnp.float32)
        s = s - slopes[None, None, :, None, None] * dist
        s = jnp.where(valid[..., None], s, NEG_INF)
        s = s.reshape(B, MOBA_Q_CHUNK, H, top_k * MOBA_BLOCK)
        lse = jax.nn.logsumexp(s, axis=-1)
        p = jnp.exp(s - lse[..., None]).astype(v.dtype).reshape(B, MOBA_Q_CHUNK, H, top_k, MOBA_BLOCK)
        o = jnp.einsum('bqhjs,bqhjsd->bqhd', p, v_g)
        return o, lse

    starts = jnp.arange(n_chunks) * MOBA_Q_CHUNK
    o_hist, lse_hist = lax.map(chunk_fn, (starts, to_chunks(q), to_chunks(sel)))
    o_hist = jnp.swapaxes(o_hist, 0, 1).reshape(B, L, H, Dh)
    lse_hist = jnp.swapaxes(lse_hist, 0, 1).reshape(B, L, H)

    lse = jnp.logaddexp(lse_self, lse_hist)
    w_self = jnp.exp(lse_self - lse)[..., None]
    w_hist = jnp.exp(lse_hist - lse)[..., None]
    return (o_self * w_self + o_hist * w_hist).astype(q.dtype)

def _hybrid_layer(x, c, w_ada, b_ada, g_norm, w_in, q_norm_a, k_norm_a, k_norm_idx,
                  q_norm_b, k_norm_b, w_out):
    B, L, _ = x.shape
    mod = jax.nn.silu(c) @ w_ada + b_ada
    shift, scale, gate = jnp.split(mod, 3, axis=-1)
    h = _rms_norm(x, g_norm) * (1.0 + scale[:, None, :]) + shift[:, None, :]

    proj = h @ w_in
    qa, ka, va, za, q_idx, k_idx, w_idx, qb, kb, vb, zb = jnp.split(proj, COL_SPLITS, axis=-1)

    heads_a = (B, L, N_HEADS_A, HEAD_DIM)
    heads_b = (B, L, N_HEADS_B, HEAD_DIM)
    qa = _rms_norm(qa.reshape(heads_a), q_norm_a)
    ka = _rms_norm(ka.reshape(heads_a), k_norm_a)
    va = va.reshape(heads_a)
    q_idx = q_idx.reshape(B, L, IDX_HEADS, IDX_DIM)
    k_idx = _rms_norm(k_idx, k_norm_idx)
    qb = _rms_norm(qb.reshape(heads_b), q_norm_b)
    kb = _rms_norm(kb.reshape(heads_b), k_norm_b)
    vb = vb.reshape(heads_b)

    ya = _dsa_attention(qa, ka, va, q_idx, k_idx, w_idx, _alibi_slopes(N_HEADS_A))
    yb = _moba_attention(qb, kb, vb, _alibi_slopes(N_HEADS_B))

    ya = ya.reshape(B, L, D_A) * jax.nn.silu(za)
    yb = yb.reshape(B, L, D_B) * jax.nn.silu(zb)
    y = jnp.concatenate([ya, yb], axis=-1) @ w_out
    return x + gate[:, None, :] * y

def first_inputs(seed: int = 0) -> dict:
    key = jax.random.key(seed)
    ks = jax.random.split(key, 12)
    nrm = jax.random.normal
    x = nrm(ks[0], (BATCH, SEQ, D_MODEL), jnp.float32)
    c = nrm(ks[1], (BATCH, D_MODEL), jnp.float32)
    w_ada = nrm(ks[2], (DEPTH, D_MODEL, 3 * D_MODEL), jnp.float32) * (0.5 * D_MODEL ** -0.5)
    b_ada = 0.01 * nrm(ks[3], (DEPTH, 3 * D_MODEL), jnp.float32)
    g_norm = 1.0 + 0.02 * nrm(ks[4], (DEPTH, D_MODEL), jnp.float32)
    w_in = nrm(ks[5], (DEPTH, D_MODEL, D_IN), jnp.float32) * D_MODEL ** -0.5
    q_norm_a = 1.0 + 0.02 * nrm(ks[6], (DEPTH, HEAD_DIM), jnp.float32)
    k_norm_a = 1.0 + 0.02 * nrm(ks[7], (DEPTH, HEAD_DIM), jnp.float32)
    k_norm_idx = 1.0 + 0.02 * nrm(ks[8], (DEPTH, IDX_DIM), jnp.float32)
    q_norm_b = 1.0 + 0.02 * nrm(ks[9], (DEPTH, HEAD_DIM), jnp.float32)
    k_norm_b = 1.0 + 0.02 * nrm(ks[10], (DEPTH, HEAD_DIM), jnp.float32)
    w_out = nrm(ks[11], (DEPTH, D_MIX, D_MODEL), jnp.float32) * D_MIX ** -0.5
    return {"x": x, "c": c, "w_ada": w_ada, "b_ada": b_ada, "g_norm": g_norm, "w_in": w_in,
            "q_norm_a": q_norm_a, "k_norm_a": k_norm_a, "k_norm_idx": k_norm_idx,
            "q_norm_b": q_norm_b, "k_norm_b": k_norm_b, "w_out": w_out}

def first_block(x, c, w_ada, b_ada, g_norm, w_in, q_norm_a, k_norm_a, k_norm_idx,
              q_norm_b, k_norm_b, w_out):
    for i in range(DEPTH):
        x = _hybrid_layer(x, c, w_ada[i], b_ada[i], g_norm[i], w_in[i], q_norm_a[i], k_norm_a[i],
                          k_norm_idx[i], q_norm_b[i], k_norm_b[i], w_out[i])
    return x


D_MIX_2 = D_MODEL
RWKV_HEAD = 64
RWKV_WIDTH = D_MIX_2 // 2
RWKV_HEADS = RWKV_WIDTH // RWKV_HEAD
DECAY_LORA = 64
AAA_LORA = 64
GATE_LORA = 160
GN_EPS = 64e-5
QK_NOPE = 128
QK_ROPE = 64
V_HEAD = 128
MLA_WIDTH = D_MIX_2 - RWKV_WIDTH
MLA_HEADS = MLA_WIDTH // V_HEAD
Q_LORA = 512
KV_LORA = 512
ROPE_THETA = 10000.0
Q_BLOCK = 128
D_FF = 5632
CONV_W = 3
NORM_EPS = 1e-6
NEG_INF_2 = -1e30

IN_SPLITS = (RWKV_WIDTH, RWKV_WIDTH, RWKV_WIDTH, DECAY_LORA, AAA_LORA, GATE_LORA,
             Q_LORA, KV_LORA, QK_ROPE)
D_IN_2 = sum(IN_SPLITS)
RWKV_SHIFT_DIM = 3 * RWKV_WIDTH + DECAY_LORA + AAA_LORA + GATE_LORA


def _split(t, sizes):
    idx = np.cumsum(sizes)[:-1].tolist()
    return jnp.split(t, idx, axis=-1)

def rms_norm(x, g):
    xf = x.astype(jnp.float32)
    y = xf * lax.rsqrt(jnp.mean(xf * xf, axis=-1, keepdims=True) + NORM_EPS)
    return (y * g.astype(jnp.float32)).astype(x.dtype)

def token_shift(h, mu):
    prev = jnp.pad(h, ((0, 0), (1, 0), (0, 0)))[:, :-1]
    return h + (prev - h) * mu

def apply_rope(t, positions):
    half = t.shape[-1] // 2
    inv_freq = ROPE_THETA ** (-jnp.arange(half, dtype=jnp.float32) / half)
    ang = positions.astype(jnp.float32)[..., None] * inv_freq
    ang = ang.reshape(ang.shape[:2] + (1,) * (t.ndim - 3) + (half,))
    cos, sin = jnp.cos(ang), jnp.sin(ang)
    tf = t.astype(jnp.float32)
    t1, t2 = tf[..., :half], tf[..., half:]
    return jnp.concatenate([t1 * cos - t2 * sin, t2 * cos + t1 * sin], axis=-1).astype(t.dtype)

def rwkv7_scan(r, w, k, v, a, b):
    bsz, _, h, n = r.shape

    def step(state, inp):
        r_t, w_t, k_t, v_t, a_t, b_t = inp
        sa = jnp.einsum('bhvk,bhk->bhv', state, a_t)
        state = (state * w_t[:, :, None, :]
                 + sa[..., None] * b_t[:, :, None, :]
                 + v_t[..., None] * k_t[:, :, None, :])
        return state, jnp.einsum('bhvk,bhk->bhv', state, r_t)

    init = jnp.zeros((bsz, h, n, n), jnp.float32)
    xs = tuple(jnp.moveaxis(t, 1, 0) for t in (r, w, k, v, a, b))
    _, out = lax.scan(step, init, xs)
    return jnp.moveaxis(out, 0, 1)

def rwkv7_mixer(h_r, h_k, h_v, h_w, h_a, h_g, w0, w2, a0, a2, g2, k_k, k_a, r_k, gn_w, gn_b):
    f32 = jnp.float32
    bsz, s, c = h_r.shape
    hd = (bsz, s, RWKV_HEADS, RWKV_HEAD)
    r = h_r.astype(f32)
    k = h_k.astype(f32)
    v = h_v.astype(f32)
    w_log = -jax.nn.softplus(-(w0.astype(f32) + jnp.tanh(h_w.astype(f32)) @ w2.astype(f32))) - 0.5
    decay = jnp.exp(-jnp.exp(w_log))
    a = jax.nn.sigmoid(a0.astype(f32) + h_a.astype(f32) @ a2.astype(f32))
    g = jax.nn.sigmoid(h_g.astype(f32)) @ g2.astype(f32)
    kk = (k * k_k).reshape(hd)
    kk = kk * lax.rsqrt(jnp.maximum(jnp.sum(kk * kk, axis=-1, keepdims=True), 1e-24))
    k = k * (1.0 + (a - 1.0) * k_a)
    r, k, v, decay, a = (t.reshape(hd) for t in (r, k, v, decay, a))
    y = rwkv7_scan(r, decay, k, v, -kk, kk * a)
    mu = jnp.mean(y, axis=-1, keepdims=True)
    var = jnp.mean(jnp.square(y - mu), axis=-1, keepdims=True)
    y = ((y - mu) * lax.rsqrt(var + GN_EPS)).reshape(bsz, s, c) * gn_w + gn_b
    bonus = jnp.sum(r * k * r_k, axis=-1, keepdims=True) * v
    return (y + bonus.reshape(bsz, s, c)) * g

def mla_mixer(c_q, c_kv, k_pe, positions, q_norm_g, w_uq, kv_norm_g, w_ukv):
    f32 = jnp.float32
    bsz, s, _ = c_q.shape
    q = (rms_norm(c_q, q_norm_g) @ w_uq).reshape(bsz, s, MLA_HEADS, QK_NOPE + QK_ROPE)
    q_nope = q[..., :QK_NOPE]
    q_pe = apply_rope(q[..., QK_NOPE:], positions)
    kv = (rms_norm(c_kv, kv_norm_g) @ w_ukv).reshape(bsz, s, MLA_HEADS, QK_NOPE + V_HEAD)
    k_nope, v = kv[..., :QK_NOPE], kv[..., QK_NOPE:]
    k_pe = apply_rope(k_pe, positions)
    scale = (QK_NOPE + QK_ROPE) ** -0.5
    outs = []
    for i in range(s // Q_BLOCK):
        q0, q1 = i * Q_BLOCK, (i + 1) * Q_BLOCK
        sc = (jnp.einsum('bqhd,bkhd->bhqk', q_nope[:, q0:q1], k_nope[:, :q1])
              + jnp.einsum('bqhr,bkr->bhqk', q_pe[:, q0:q1], k_pe[:, :q1])).astype(f32) * scale
        causal = (q0 + jnp.arange(Q_BLOCK))[:, None] >= jnp.arange(q1)[None, :]
        p = jax.nn.softmax(jnp.where(causal, sc, NEG_INF_2), axis=-1)
        outs.append(jnp.einsum('bhqk,bkhd->bqhd', p.astype(v.dtype), v[:, :q1]))
    return jnp.concatenate(outs, axis=1).reshape(bsz, s, MLA_WIDTH)

def conv_glu_ffn(h, w_gate, w_up, conv_w, conv_b, w_down):
    gate = h @ w_gate
    gate = lax.conv_general_dilated(
        gate, conv_w[:, None, :].astype(gate.dtype), window_strides=(1,),
        padding=[(CONV_W - 1, 0)], dimension_numbers=('NWC', 'WIO', 'NWC'),
        feature_group_count=D_FF) + conv_b
    return (jax.nn.silu(gate) * (h @ w_up)) @ w_down

def second_inputs(seed: int = 0) -> dict:
    key = jax.random.key(seed)
    ks = jax.random.split(key, 32)
    L = DEPTH

    def nrm(k, shape, scale):
        return jax.random.normal(k, shape, jnp.float32) * scale

    def gain(k, shape):
        return 1.0 + nrm(k, shape, 0.05)

    x = nrm(ks[0], (BATCH, SEQ, D_MODEL), 1.0)
    offset = jax.random.randint(ks[1], (BATCH, 1), 0, 4096, dtype=jnp.int32)
    positions = offset + jnp.arange(SEQ, dtype=jnp.int32)[None, :]
    return {
        'x': x,
        'positions': positions,
        'attn_norm_g': gain(ks[2], (L, D_MODEL)),
        'w_in': nrm(ks[3], (L, D_MODEL, D_IN_2), D_MODEL ** -0.5),
        'rwkv_mu': jax.random.uniform(ks[4], (L, RWKV_SHIFT_DIM), jnp.float32),
        'rwkv_w0': jax.random.uniform(ks[5], (L, RWKV_WIDTH), jnp.float32, -6.0, -1.0),
        'rwkv_w2': nrm(ks[6], (L, DECAY_LORA, RWKV_WIDTH), 0.1 * DECAY_LORA ** -0.5),
        'rwkv_a0': nrm(ks[7], (L, RWKV_WIDTH), 0.5),
        'rwkv_a2': nrm(ks[8], (L, AAA_LORA, RWKV_WIDTH), 0.5 * AAA_LORA ** -0.5),
        'rwkv_g2': nrm(ks[9], (L, GATE_LORA, RWKV_WIDTH), GATE_LORA ** -0.5),
        'rwkv_k_k': 0.85 + nrm(ks[10], (L, RWKV_WIDTH), 0.05),
        'rwkv_k_a': gain(ks[11], (L, RWKV_WIDTH)),
        'rwkv_r_k': nrm(ks[12], (L, RWKV_HEADS, RWKV_HEAD), 0.1),
        'rwkv_gn_w': gain(ks[13], (L, RWKV_WIDTH)),
        'rwkv_gn_b': nrm(ks[14], (L, RWKV_WIDTH), 0.02),
        'mla_q_norm_g': gain(ks[15], (L, Q_LORA)),
        'mla_w_uq': nrm(ks[16], (L, Q_LORA, MLA_HEADS * (QK_NOPE + QK_ROPE)), Q_LORA ** -0.5),
        'mla_kv_norm_g': gain(ks[17], (L, KV_LORA)),
        'mla_w_ukv': nrm(ks[18], (L, KV_LORA, MLA_HEADS * (QK_NOPE + V_HEAD)), KV_LORA ** -0.5),
        'w_out': nrm(ks[19], (L, D_MIX_2, D_MODEL), D_MIX_2 ** -0.5),
        'ffn_norm_g': gain(ks[20], (L, D_MODEL)),
        'ffn_w_gate': nrm(ks[21], (L, D_MODEL, D_FF), D_MODEL ** -0.5),
        'ffn_w_up': nrm(ks[22], (L, D_MODEL, D_FF), D_MODEL ** -0.5),
        'ffn_conv_w': nrm(ks[23], (L, CONV_W, D_FF), CONV_W ** -0.5),
        'ffn_conv_b': nrm(ks[24], (L, D_FF), 0.02),
        'ffn_w_down': nrm(ks[25], (L, D_FF, D_MODEL), D_FF ** -0.5),
        'final_norm_g': gain(ks[26], (D_MODEL,)),
    }

def second_block(x, positions, attn_norm_g, w_in, rwkv_mu, rwkv_w0, rwkv_w2, rwkv_a0, rwkv_a2,
              rwkv_g2, rwkv_k_k, rwkv_k_a, rwkv_r_k, rwkv_gn_w, rwkv_gn_b, mla_q_norm_g,
              mla_w_uq, mla_kv_norm_g, mla_w_ukv, w_out, ffn_norm_g, ffn_w_gate, ffn_w_up,
              ffn_conv_w, ffn_conv_b, ffn_w_down, final_norm_g):
    for l in range(DEPTH):
        h = rms_norm(x, attn_norm_g[l])
        proj = h @ w_in[l]
        shifted = token_shift(proj[..., :RWKV_SHIFT_DIM], rwkv_mu[l])
        h_r, h_k, h_v, h_w, h_a, h_g = _split(shifted, IN_SPLITS[:6])
        c_q, c_kv, k_pe = _split(proj[..., RWKV_SHIFT_DIM:], IN_SPLITS[6:])
        y_rwkv = rwkv7_mixer(h_r, h_k, h_v, h_w, h_a, h_g, rwkv_w0[l], rwkv_w2[l], rwkv_a0[l],
                             rwkv_a2[l], rwkv_g2[l], rwkv_k_k[l], rwkv_k_a[l], rwkv_r_k[l],
                             rwkv_gn_w[l], rwkv_gn_b[l])
        y_mla = mla_mixer(c_q, c_kv, k_pe, positions, mla_q_norm_g[l], mla_w_uq[l],
                          mla_kv_norm_g[l], mla_w_ukv[l])
        y = jnp.concatenate([y_rwkv.astype(x.dtype), y_mla.astype(x.dtype)], axis=-1)
        x = x + y @ w_out[l]
        h = rms_norm(x, ffn_norm_g[l])
        x = x + conv_glu_ffn(h, ffn_w_gate[l], ffn_w_up[l], ffn_conv_w[l], ffn_conv_b[l],
                             ffn_w_down[l]).astype(x.dtype)
    return rms_norm(x, final_norm_g)


def setup_inputs(seed=0):
    out = dict(first_inputs(seed))
    for name, value in second_inputs(seed + 1).items():
        if name != "x":
            out[name + "_2"] = value
    return out


def reference(
    x, c, w_ada, b_ada, g_norm, w_in, q_norm_a, k_norm_a, k_norm_idx, q_norm_b, k_norm_b, w_out,
    positions_2, attn_norm_g_2, w_in_2, rwkv_mu_2, rwkv_w0_2, rwkv_w2_2, rwkv_a0_2, rwkv_a2_2,
    rwkv_g2_2, rwkv_k_k_2, rwkv_k_a_2, rwkv_r_k_2, rwkv_gn_w_2, rwkv_gn_b_2, mla_q_norm_g_2,
    mla_w_uq_2, mla_kv_norm_g_2, mla_w_ukv_2, w_out_2, ffn_norm_g_2, ffn_w_gate_2, ffn_w_up_2,
    ffn_conv_w_2, ffn_conv_b_2, ffn_w_down_2, final_norm_g_2,
):
    x = first_block(
        x, c, w_ada, b_ada, g_norm, w_in, q_norm_a, k_norm_a, k_norm_idx, q_norm_b, k_norm_b,
        w_out,
    )
    return second_block(
        x, positions_2, attn_norm_g_2, w_in_2, rwkv_mu_2, rwkv_w0_2, rwkv_w2_2, rwkv_a0_2,
        rwkv_a2_2, rwkv_g2_2, rwkv_k_k_2, rwkv_k_a_2, rwkv_r_k_2, rwkv_gn_w_2, rwkv_gn_b_2,
        mla_q_norm_g_2, mla_w_uq_2, mla_kv_norm_g_2, mla_w_ukv_2, w_out_2, ffn_norm_g_2,
        ffn_w_gate_2, ffn_w_up_2, ffn_conv_w_2, ffn_conv_b_2, ffn_w_down_2, final_norm_g_2,
    )


_drawn_inputs = setup_inputs


def setup_inputs(seed=0):
    import zlib

    import numpy as np

    out = dict(_drawn_inputs(seed))
    spreads = {}
    factors = {'b_ada': 5.589,
     'g_norm': 4.218,
     'q_norm_a': 8.0,
     'k_norm_a': 8.0,
     'k_norm_idx': 5.782,
     'q_norm_b': 8.0,
     'k_norm_b': 8.0,
     'rwkv_w2_2': 64.0,
     'rwkv_k_k_2': 27.481,
     'rwkv_gn_w_2': 16.184,
     'rwkv_gn_b_2': 45.61,
     'mla_q_norm_g_2': 8.0,
     'mla_kv_norm_g_2': 5.574,
     'ffn_conv_b_2': 27.61,
     'rwkv_k_a_2': 5.085,
     'rwkv_r_k_2': 3.729,
     'ffn_norm_g_2': 7.636}
    for name, (base, spread) in spreads.items():
        noise = np.random.default_rng([zlib.crc32(name.encode()), seed]).standard_normal(out[name].shape)
        drawn = base * np.exp(spread * noise) if base else spread * noise
        out[name] = jnp.asarray(drawn.astype(out[name].dtype))
    for name, factor in factors.items():
        out[name] = (out[name] * factor).astype(out[name].dtype)
    return out
```

```python
from contextlib import ExitStack

import numpy as np
import concourse.bass as bass
from concourse import mybir

F32 = mybir.dt.float32
I32 = mybir.dt.int32
ALU = mybir.AluOpType
ACT = mybir.ActivationFunctionType
AX_X = mybir.AxisListType.X
ds = bass.ds

P = 128
L = 256
TT = L // P
D = 2048
KT = D // P
DH = 128
HEADS = 8
D_A = HEADS * DH
IDX_HEADS, IDX_DIM, TOPK = 16, 64, 64
IDX_COL = 4 * D_A
KW_COL = IDX_COL + IDX_HEADS * IDX_DIM
KW = IDX_DIM + IDX_HEADS
B_COL = KW_COL + KW
EPS = 1e-6
NEG = -1e30
SPAN = P + L

NSLOT = 4
HALF = 8
CH = 512

RW = 1024
NP_ = 8
N = 64
C = 64
NCH = L // C
WAG_COL = 3 * RW
WAG_TILES = [(0, 64), (64, 64), (128, 128), (256, 32)]
WAG = 64 + 64 + 160
CQ_COL = WAG_COL + WAG
KPE_COL = CQ_COL + 1024
LORA = 512
ROPE = 64
MLA_W = HEADS * (DH + ROPE)
FF = 5632
FT = FF // P
GN_EPS = 64e-5

VEC = {}


def _place():
    groups = [
        [("c", 16), ("b_ada", 48), ("g_norm", 16), ("attn_norm_g_2", 16), ("ffn_norm_g_2", 16),
         ("q_norm_a", 1), ("k_norm_a", 1), ("q_norm_b", 1), ("k_norm_b", 1),
         ("mla_q_norm_g_2", 4), ("mla_kv_norm_g_2", 4)],
        [("rwkv_mu_2", 28), ("rwkv_w0_2", 8), ("rwkv_a0_2", 8), ("rwkv_k_k_2", 8), ("rwkv_k_a_2", 8),
         ("rwkv_r_k_2", 8), ("rwkv_gn_w_2", 8), ("rwkv_gn_b_2", 8), ("ffn_conv_b_2", 44)],
        [("conv0", 44), ("conv1", 44)],
        [("conv2", 44)],
    ]
    for g, names in enumerate(groups):
        row = 0
        for name, rows in names:
            VEC[name] = (g, row, rows)
            row += rows
    return [sum(r for _, r in names) for names in groups]


GROUP_ROWS = _place()


class Chain:

    def __init__(self, eng, sem):
        self.eng, self.sem, self.n, self.i, self.per = eng, sem, 0, None, 0

    def value(self):
        return self.n if self.i is None else self.i * self.per + self.n

    def mark(self, ins):
        ins.then_inc(self.sem, 1)
        self.n += 1
        return ins

    def wait(self):
        self.eng.wait_ge(self.sem, self.value())

    def link(self, ins):
        self.mark(ins)
        self.wait()

    def enter(self, i, per):
        self.i, self.per, self.start = i, per, self.n

    def leave(self, times):
        assert self.n - self.start == self.per, (self.n - self.start, self.per)
        self.n, self.i = self.start + self.per * times, None


class Steps:

    def __init__(self, sem, names):
        self.sem, self.names, self.at = sem, names, 0

    def mark(self, ins, name):
        assert self.names[self.at % len(self.names)] == name, (self.names[self.at % len(self.names)], name)
        self.at += 1
        ins.then_inc(self.sem, 1)

    def wait(self, eng, name, step):
        eng.wait_ge(self.sem, step * len(self.names) + (self.names.index(name) + 1))


def build(nc, a, out):
    ctx = ExitStack()
    with ctx:
        def sb(name, *shape, dt=F32):
            return ctx.enter_context(nc.sbuf_tensor(name, [P, *shape], dt))

        def sem(name):
            return ctx.enter_context(nc.semaphore(name))

        BANK = [ctx.enter_context(nc.psum_tensor(f"bank{i}", [P, 512], F32)) for i in range(8)]

        ring = sb("ring", NSLOT, HALF * CH)
        X = sb("X", TT, D)
        HT = sb("HT", KT, L)
        cols = sb("cols", 4 * P)
        ident = sb("ident", P)
        ones = sb("ones", P)
        small = sb("small", 512)
        masks = sb("masks", 1216)
        causal_dist = masks[:, 0:SPAN]
        causal_mask = masks[:, SPAN:2 * SPAN]
        bias_a = masks[:, 2 * SPAN:3 * SPAN]
        slope = sb("slope", 2 * HEADS)
        ARENA = 25600
        arena = sb("arena", ARENA)

        used = [0]

        def at(off, *shape):
            n = int(np.prod(shape))
            assert off + n <= ARENA, (off, n)
            v = arena[:, off:off + n]
            used[0] = off + n
            if len(shape) == 1:
                return v
            names = "abcd"[:len(shape)]
            return v.rearrange(f"p ({' '.join(names)}) -> p {' '.join(names)}",
                               **{m: s for m, s in zip(names[1:], shape[1:])})

        def col(name, j=0, n=1):
            g, row, _ = VEC[name]
            return cols[:, g * P + row + j:g * P + row + j + n]

        mod = small[:, 0:48]
        cs = small[:, 48:64]
        gs = small[:, 64:80]
        qgain = small[:, 80:84]
        ss = small[:, 84:86]
        rstd = small[:, 86:88]
        sgc = small[:, 88:104]
        nmax = small[:, 104:104 + 32]
        rowsum = small[:, 136:136 + 32]
        rsum_inv = small[:, 168:168 + 32]
        hss = small[:, 200:216]
        hrstd = small[:, 216:232]
        top8 = small[:, 232:248].rearrange("p (t e) -> p t e", t=TT)
        cnt = small[:, 248:250]
        need = small[:, 250:252]
        kss = small[:, 252:254]
        krstd = small[:, 254:256]

        V1 = at(0, 2, TT, D_A)
        Z1 = at(4096, 2, TT, D_A)
        QT = at(8192, 2, HEADS, L)
        KTT = at(12288, 2, HEADS, L)
        XN = at(8192, TT, D)
        rows = at(16384, 4, P)
        stage = at(16896, 2, TT, CH)
        square = at(18944, TT, CH)
        QI = at(19968, 8, L)
        S_sb = at(16896, 2, SPAN)
        Pr = at(17664, 2, SPAN)
        PTs = at(18432, 2, SPAN)
        KI = at(22016, TT, KW)
        KIX = at(22176, TT, 2, P)
        KB = at(22688, 2, L)
        relu = at(23200, 2, CH)
        score = at(24224, SPAN)
        work = at(24608, SPAN)
        kin_g = at(24992, IDX_DIM)
        MROW = at(0, 2 * D)[0:1, :]
        gate_row = at(19968, D)
        cs_wide = HT[:, 0:8, :].rearrange("p a n -> p (a n)").rearrange("p (k n) -> p k n", n=P)
        bgate_row = HT[:, 8:16, :].rearrange("p a n -> p (a n)")
        wo_tmp = at(10752, 2, CH)

        RKV = at(0, 24, L)
        HW, HA, HG0, HG1 = (at(6144 + 256 * i, L) for i in range(4))
        RAW = at(7168, 4, L + 1)
        SH = at(8196, 4, L)
        S2, Pr2, PT2 = at(7168, 2, SPAN), at(7936, 2, SPAN), at(8704, 2, SPAN)
        CQ = at(9472, 4, LORA)
        YM = at(9472, TT, 1024)
        KPE = at(11520, TT, ROPE)
        CT = at(11648, 8, L)
        QN = at(13696, HEADS, L)
        KN = at(15744, HEADS, L)
        VM = at(17792, TT, 1024)
        QPE = at(19840, TT, 512)
        QPR = at(20864, TT, 512)
        QPT = at(21888, 4, L)
        KPX = at(22912, TT, 2, P)
        KPT = at(23424, 2, L)
        ang = at(23936, 2, TT, 32)
        turns = at(24064, 2, TT, 32)
        inv_freq = at(24192, 32)
        rope_tmp = at(24224, 4, 256)
        pos_i = arena[:, 25248:25250].bitcast(I32)
        pos = at(25250, 2)
        XN2 = at(13696, TT, D)
        cstat = small[:, 256:260]
        crstd = small[:, 260:264]

        Lw = at(7168, 8, L)
        El = at(9216, 8, L)
        Bv = at(11264, 8, L)
        KKn = at(13312, 8, L)
        sqk = at(15360, 8, L)
        chunk_start = at(17408, L)
        kfac = at(17664, 8, L)
        w4 = [at(15360 + 512 * i, 4, P) for i in range(15)]
        a_bd, b_bd, k_bd, r_bd, v_bd, LT, AkT, BrT, KrT, b_tok, k_tok, Xi, Zi, T2, y_bd = w4
        n4 = [at(23040 + 256 * i, 4, N) for i in range(10)]
        P1, Us, Vp, ST, YC, YQ, EX, EN, EXC, DEL = n4
        level = [masks[:, P * i:P * (i + 1)] for i in range(6)]
        below, upto_diag = masks[:, 768:896], masks[:, 896:1024]
        I2 = masks[:, 1024:1088]
        head_ones = masks[:, 1088:1216]
        end_s = small[:, 264:296].rearrange("p (f c) -> p f c", c=NCH)
        mid_s = small[:, 296:328].rearrange("p (f c) -> p f c", c=NCH)
        fac = small[:, 328:360].rearrange("p (f c) -> p f c", c=NCH)
        one_ka = small[:, 360:368]
        gsum, gvar = small[:, 368:372], small[:, 372:376]
        RK2 = at(15360, 8, L)
        BV = at(17408, 8, L)

        AC = at(0, FT, L)
        RAWF = at(11264, 4, L + 2)
        CV = at(12296, 4, L)
        XN3 = at(16384, TT, D)
        fg_row = at(20480, D)

        piece_in = [sem(f"piece_in{s}") for s in range(NSLOT)]
        piece_done = sem("piece_done")
        act_took, dve_took = sem("act_took"), sem("dve_took")
        x_in, params_in, misc_in = sem("x_in"), sem("params_in"), sem("misc_in")
        rows_clear, consts_set = sem("rows_clear"), sem("consts_set")
        pool_chain, dve_chain_s, act_chain_s = sem("pool_chain"), sem("dve_chain"), sem("act_chain")
        colsT_ready, cols_ready = sem("colsT_ready"), sem("cols_ready")
        cs_ready = sem("cs_ready")
        mod_ready = sem("mod_ready")
        ssq_ready, var_ready, rstd_ready, xn_ready = sem("ssq_ready"), sem("var_ready"), sem("rstd_ready"), sem("xn_ready")
        xT_ready, xT_taken = sem("xT_ready"), sem("xT_taken")
        ki_var, ki_rstd, kix_ready, kixT_ready, kb_ready = map(sem, ["ki_var", "ki_rstd", "kix_ready", "kixT_ready", "kb_ready"])
        idx_ready, relu_ready, relu_used = sem("idx_ready"), sem("relu_ready"), sem("relu_used")
        chunk_out, head_var, head_rstd, head_normed, headT_ready, headT_taken = map(
            sem, ["chunk_out", "head_var", "head_rstd", "head_normed", "headT_ready", "headT_taken"])
        scores_ready, scores_biased, max_ready, probs_ready = map(
            sem, ["scores_ready", "scores_biased", "max_ready", "probs_ready"])
        probsT_ready, probsT_taken, out_ready, out_taken = map(
            sem, ["probsT_ready", "probsT_taken", "out_ready", "out_taken"])
        row_took, modT_ready, cs_wide_ready, bgate_in = map(sem, ["row_took", "modT_ready", "cs_wide_ready", "bgate_in"])
        x_updated = sem("x_updated")
        stored = sem("stored")
        shifted, raw_clear, wag_ready = sem("shifted"), sem("raw_clear"), sem("wag_ready")
        pos_in, fg_in = sem("pos_in"), sem("fg_in")
        ang_ready, trig_ready = sem("ang_ready"), sem("trig_ready")
        c_sq, c_var, c_rstd, c_normed, kpx_ready, qpr_ready = map(
            sem, ["c_sq", "c_var", "c_rstd", "c_normed", "kpx_ready", "qpr_ready"])
        lora_ready = sem("lora_ready")
        masks_free, rw_masks, rw_mid = sem("masks_free"), sem("rw_masks"), sem("rw_mid")
        rw_small, rw_small_took, kk_sq, kk_sum, kk_var, kk_rstd = map(
            sem, ["rw_small", "rw_small_took", "kk_sq", "kk_sum", "kk_var", "kk_rstd"])
        prep_ready, fac_raw, fac_ready = sem("prep_ready"), sem("fac_raw"), sem("fac_ready")
        pe_step, act_step, dve_step = sem("pe_step"), sem("act_step"), sem("dve_step")
        rk_ready, bonus_ready, bonus_took, g_ready, g_took = map(
            sem, ["rk_ready", "bonus_ready", "bonus_took", "g_ready", "g_took"])
        conv_ready, gate_act, up_taken = sem("conv_ready"), sem("gate_act"), sem("up_taken")
        fin_ready = sem("fin_ready")

        def attention_pe(pe, heads, base, qk, v, Pr, PTs):
            def scores(h):
                if h >= 2:
                    pe.wait_ge(scores_biased, base + h - 1)
                for t in range(TT):
                    o = BANK[4 + h % 2][:, t * P:t * P + (t + 1) * P]
                    parts = qk(h, t)
                    for n, (q, k) in enumerate(parts):
                        last = pe.matmul(o, q, k, start=(n == 0), stop=(n == len(parts) - 1))
                last.then_inc(scores_ready, 1)

            scores(0)
            scores(1)
            for h in range(heads):
                pe.wait_ge(probs_ready, 2 * (base + h + 1))
                if h >= 2:
                    pe.wait_ge(probsT_taken, base + h - 1)
                for n, c0 in enumerate((0, P, 2 * P)):
                    last = pe.transpose(BANK[2 + h % 2][:, n * P:(n + 1) * P], Pr[:, h % 2, c0:c0 + P], ident[:])
                last.then_inc(probsT_ready, 1)
                if h + 2 < heads:
                    scores(h + 2)
                pe.wait_ge(probsT_taken, base + h + 1)
                if h >= 2:
                    pe.wait_ge(out_taken, 2 * (base + h - 1))
                o = BANK[6 + h % 2]
                pt = PTs[:, h % 2]
                pe.matmul(o[:, 0:DH], pt[:, 0:P], v(h, 0), start=True, stop=True)
                pe.matmul(o[:, DH:2 * DH], pt[:, P:2 * P], v(h, 0), start=True, stop=False)
                pe.matmul(o[:, DH:2 * DH], pt[:, 2 * P:3 * P], v(h, 1), start=False, stop=True) \
                    .then_inc(out_ready, 1)

        def attention_act(act, heads, base, S_sb, Pr, PTs):
            def exps(h):
                act.wait_ge(max_ready, 2 * (base + h + 1))
                if base + h >= 2:
                    act.wait_ge(probsT_ready, base + h - 1)
                for t, (c0, w) in enumerate(((0, P), (P, L))):
                    act.activation(Pr[:, h % 2, c0:c0 + w], S_sb[:, h % 2, c0:c0 + w], ACT.Exp,
                                   bias=nmax[:, 2 * h + t:2 * h + t + 1],
                                   accum_out=rowsum[:, 2 * h + t:2 * h + t + 1]).then_inc(probs_ready, 1)

            def turn(h):
                act.wait_ge(probsT_ready, base + h + 1)
                if base + h >= 2:
                    act.wait_ge(out_ready, base + h - 1)
                act.activation(PTs[:, h % 2, :], BANK[2 + h % 2][:, 0:SPAN], ACT.Copy).then_inc(probsT_taken, 1)

            for h in range(heads):
                exps(h)
                if h >= 1:
                    turn(h - 1)
            turn(heads - 1)

        def attention_dve(dve, own, heads, base, bias, coef, emit, S_sb):
            def maxima(h):
                dve.wait_ge(scores_ready, base + h + 1)
                if base + h >= 2:
                    dve.wait_ge(probs_ready, 2 * (base + h - 1))
                dve.scalar_tensor_tensor(out=S_sb[:, h % 2, :], in0=bias(h), scalar=coef(h),
                                         in1=BANK[4 + h % 2][:, 0:SPAN], op0=ALU.mult,
                                         op1=ALU.add).then_inc(scores_biased, 1)
                dve.wait_ge(scores_biased, base + h + 1)
                for t, (c0, w) in enumerate(((0, P), (P, L))):
                    dve.tensor_reduce(nmax[:, 2 * h + t:2 * h + t + 1], S_sb[:, h % 2, c0:c0 + w], AX_X, ALU.max,
                                      negate=True).then_inc(max_ready, 1)

            def finish(h):
                dve.wait_ge(probs_ready, 2 * (base + h + 1))
                own.link(dve.reciprocal(rsum_inv[:, 2 * h:2 * h + 2], rowsum[:, 2 * h:2 * h + 2]))
                dve.wait_ge(out_ready, base + h + 1)
                for t in range(TT):
                    emit(h, t, BANK[6 + h % 2][:, t * DH:(t + 1) * DH],
                         rsum_inv[:, 2 * h + t:2 * h + t + 1]).then_inc(out_taken, 1)

            for h in range(heads):
                maxima(h)
                if h >= 1:
                    finish(h - 1)
            finish(heads - 1)

        PARAMS = [(n, n) for n in VEC if not n.startswith("conv")]
        PARAM_DMAS = len(PARAMS) + 4 + 3

        block = ctx.enter_context(nc.Block())

        ACT_GATE, ACT_RKV = 38, 42
        NADA = 2 * D // CH
        n_ada = 0
        n_kw = n_ada + 2 * NADA
        n_qi = n_kw + 2
        n_br = n_qi + 4
        n_gate = n_br + 32
        n_wo = n_gate + 8
        n_rkv = n_wo + 8
        n_wag = n_rkv + 12
        n_kpe = n_wag + 2
        n_c = n_kpe + 2
        n_uq = n_c + 4
        n_ukv = n_uq + 2
        n_w2 = n_ukv + 2
        n_wo2 = n_w2 + 4
        n_gu = n_wo2 + 8
        n_dn = n_gu + 44

        LEVELS = 6
        inv = []
        for m in range(LEVELS):
            inv += [f"T{m}"] + ([f"X{m}"] if 0 < m < LEVELS - 1 else []) + [f"Z{m}"]
        pe_names = ["LT", "AkT", "btok", "ktok", "Vp", "BrT", "KrT"] + inv + ["P1", "U", "Y", "S", "YT"]
        act_names = ["EX", "EN", "EXC", "btok", "ktok", "Vp", "P1", "U", "sq", "YT"]
        dve_names = (["DEL"] + [f"{x}{h}" for x in "vbkra" for h in range(2)] + ["LT", "AkT", "BrT", "KrT"]
                     + [f"T{m}" if k == "T" else f"{k}{m}" for m in range(LEVELS)
                        for k in (["T"] + (["X"] if m < LEVELS - 1 else []) + ["Z"])]
                     + ["Ssum", "gs", "yc", "yq", "gv", "ge", "gi", "y0", "y1", "S"])

        def source(w, half, c0, width):
            return w[half * HALF * P:(half + 1) * HALF * P, c0].rearrange("(k p) n -> p k n", p=P) \
                if not isinstance(c0, int) else \
                w[half * HALF * P:(half + 1) * HALF * P, c0:c0 + width].rearrange("(k p) n -> p k n", p=P)

        def slot(n, width, k=HALF):
            return ring[:, n % NSLOT, 0:k * width].rearrange("p (k n) -> p k n", k=k)

        @block.sync
        def _(sp):
            def load(n, src, width, k=HALF, shift=0):
                if n >= NSLOT or not isinstance(shift, int):
                    sp.wait_ge(piece_done, shift + n - NSLOT + 1)
                sp.dma_start(slot(n, width, k), src).then_inc(piece_in[n % NSLOT], 16)

            def chunk(n, w, c0, width, shift=0, n0=None):
                for half in range(2):
                    src = w[half * HALF * P:(half + 1) * HALF * P, ds(c0, width)]
                    load(n + half, src.rearrange("(k p) n -> p k n", p=P), width, shift=shift)

            w_ada, w_in, w_out = a["w_ada"][0], a["w_in"][0], a["w_out"][0]
            for j in range(2):
                chunk(n_ada + 2 * j, w_ada, j * CH, CH)
            with sp.Fori(1, NADA // 2) as i:
                for j in range(2):
                    chunk(n_ada + 2 * j, w_ada, i * 2 * CH + j * CH, CH, shift=i * 4)
            chunk(n_kw, w_in, KW_COL, KW)
            for j in range(2):
                chunk(n_qi + 2 * j, w_in, IDX_COL + j * CH, CH)
            with sp.Fori(0, 2) as i:
                for j in range(8):
                    chunk(n_br + 2 * j, w_in, i * B_COL + j * CH, CH, shift=i * 16)
            with sp.Fori(0, 2) as i:
                for j in range(2):
                    chunk(n_gate + 2 * j, w_ada, i * 2 * CH + (2 * D + j * CH), CH, shift=i * 4)
            with sp.Fori(0, 2) as i:
                for j in range(2):
                    chunk(n_wo + 2 * j, w_out, i * 2 * CH + j * CH, CH, shift=i * 4)
            w_in2, w_uq, w_ukv = a["w_in_2"][0], a["mla_w_uq_2"][0], a["mla_w_ukv_2"][0]
            with sp.Fori(0, 3) as i:
                for j in range(2):
                    chunk(n_rkv + 2 * j, w_in2, i * 2 * CH + j * CH, CH, shift=i * 4)
            chunk(n_wag, w_in2, WAG_COL, WAG)
            chunk(n_kpe, w_in2, KPE_COL, ROPE)
            for j in range(2):
                chunk(n_c + 2 * j, w_in2, CQ_COL + j * CH, CH)
            for j in range(2):
                load(n_uq + j, w_uq[:, j * 768:(j + 1) * 768].rearrange("(k p) n -> p k n", p=P), 768, k=4)
            for j in range(2):
                load(n_ukv + j, w_ukv[:, j * 1024:(j + 1) * 1024].rearrange("(k p) n -> p k n", p=P), 1024, k=4)
            for j, (w, r0, r) in enumerate([("rwkv_w2_2", 0, 64), ("rwkv_a2_2", 0, 64), ("rwkv_g2_2", 0, P),
                                            ("rwkv_g2_2", P, 32)]):
                n = n_w2 + j
                sp.wait_ge(piece_done, n - NSLOT + 1)
                sp.dma_start(ring[0:r, n % NSLOT, 0:RW], a[w][0, r0:r0 + r, :]).then_inc(piece_in[n % NSLOT], 16)
            for c in range(4):
                chunk(n_wo2 + 2 * c, a["w_out_2"][0], c * CH, CH)
            with sp.Fori(0, FF // CH) as i:
                for j, w in enumerate(("ffn_w_gate_2", "ffn_w_up_2")):
                    chunk(n_gu + 2 * j, a[w][0], i * CH, CH, shift=i * 4)
            wd = a["ffn_w_down_2"][0]
            with sp.Fori(0, 2) as i:
                for j in range(2):
                    for q in range(6):
                        k = HALF if q < 5 else 4
                        src = wd[q * HALF * P:(q * HALF + k) * P, ds(i * 2 * CH + j * CH, CH)]
                        load(n_dn + 6 * j + q, src.rearrange("(k p) n -> p k n", p=P), CH, k=k, shift=i * 12)
            sp.wait_ge(fin_ready, 2)
            for t in range(TT):
                sp.dma_start(out[0, t * P:(t + 1) * P, :], XN3[:, t, :]).then_inc(stored, 16)
            sp.wait_ge(stored, 32)

        @block.gpsimd
        def _(pool):
            own = Chain(pool, pool_chain)
            pool.memset(rows[:, :, :], 0.0).then_inc(rows_clear, 1)
            pool.memset(ones[:], 1.0).then_inc(consts_set, 1)
            own.link(pool.memset(ident[:], 0.0))
            pool.affine_select(out=ident[:], in_=ident[:], compare_op=ALU.not_equal, fill=1.0, base=0,
                               pattern=[[-1, P]], channel_multiplier=1).then_inc(consts_set, 1)
            for t, (c0, w) in enumerate(((0, P), (P, L))):
                own.mark(pool.iota(causal_dist[:, c0:c0 + w], pattern=[[1, w]], base=-t * P,
                                   channel_multiplier=-1, allow_small_or_imprecise_dtypes=True))
            own.link(pool.memset(causal_mask, 0.0))
            for t, (c0, w) in enumerate(((0, P), (P, L))):
                for m in (causal_dist, causal_mask):
                    pool.affine_select(out=m[:, c0:c0 + w], in_=m[:, c0:c0 + w], compare_op=ALU.is_ge,
                                       fill=NEG, base=t * P, pattern=[[-1, w]],
                                       channel_multiplier=1).then_inc(consts_set, 1)
            for h in range(2 * HEADS):
                pool.memset(slope[:, h:h + 1], float(np.float32(2.0 ** (-8.0 * (h % HEADS + 1) / HEADS)))) \
                    .then_inc(consts_set, 1)
            pool.memset(KIX[:, :, :, :], 0.0).then_inc(consts_set, 1)
            pool.wait_ge(masks_free, 1)
            own.link(pool.memset(masks[:, 0:768], 0.0))
            own.link(pool.memset(masks[:, 768:1024], 1.0))
            own.link(pool.memset(I2, 0.0))
            own.link(pool.memset(head_ones, 0.0))
            own.link(pool.memset(chunk_start, 1.0))
            for m in range(LEVELS):
                b = 1 << m
                v = level[m].rearrange("p (j two m) -> p j two m", two=2, m=b)[:, :, 0, :]
                nb = P // (2 * b)
                own.link(pool.memset(v, 1.0))
                own.link(pool.affine_select(out=v, in_=v, compare_op=ALU.is_ge, fill=0.0, base=-b,
                                            pattern=[[-2 * b, nb], [0, b]], channel_multiplier=1))
                own.link(pool.affine_select(out=v, in_=v, compare_op=ALU.is_ge, fill=0.0, base=2 * b - 1,
                                            pattern=[[2 * b, nb], [0, b]], channel_multiplier=-1))
            own.link(pool.affine_select(out=below, in_=below, compare_op=ALU.is_gt, fill=0.0, base=0,
                                        pattern=[[1, P]], channel_multiplier=-1))
            own.link(pool.affine_select(out=upto_diag, in_=upto_diag, compare_op=ALU.is_ge, fill=0.0, base=0,
                                        pattern=[[1, P]], channel_multiplier=-1))
            own.link(pool.affine_select(out=I2, in_=I2, compare_op=ALU.not_equal, fill=1.0, base=0,
                                        pattern=[[-1, N]], channel_multiplier=1))
            own.link(pool.affine_select(out=I2, in_=I2, compare_op=ALU.not_equal, fill=1.0, base=-N,
                                        pattern=[[-1, N]], channel_multiplier=1))
            for h in range(2):
                own.link(pool.memset(head_ones[h * N:(h + 1) * N, h * N:(h + 1) * N], 1.0))
            own.link(pool.memset(chunk_start.rearrange("p (c t) -> p c t", t=C)[:, :, 0], 0.0))
            pool.memset(small[:, 511:512], 0.0).then_inc(rw_masks, 1)
        CONSTS = 2 + 4 + 2 * HEADS + 1

        @block.tensor
        def _(pe):
            def arrived(n, more=0):
                pe.wait_ge(piece_in[n % NSLOT], more * 16 + 16 * (n // NSLOT + 1))

            def tok_chunk(n, pair, width, more=0):
                for half in range(2):
                    arrived(n + half, more)
                    w = slot(n + half, width)
                    for k in range(HALF):
                        for t in range(TT):
                            last = pe.matmul(BANK[2 * pair + t][:, 0:width],
                                             HT[:, half * HALF + k, t * P:(t + 1) * P], w[:, k, :],
                                             start=(half + k == 0), stop=(half == 1 and k == HALF - 1))
                    last.then_inc(piece_done, 1)

            def feat_chunk(n, pair, width, more=0, tiles=None):
                arrived(n, more)
                arrived(n + 1, more)
                for f, (f0, m) in enumerate(tiles or [(f * P, P) for f in range(width // P)]):
                    for k in range(KT):
                        w = slot(n + k // HALF, width)
                        last = pe.matmul(BANK[2 * pair + f // 2][0:m, (f % 2) * L:(f % 2 + 1) * L],
                                         w[:, k % HALF, f0:f0 + m], HT[:, k, :],
                                         start=(k == 0), stop=(k == KT - 1))
                last.then_inc(piece_done, 2)

            def ada_chunk(n, bank, stationary, more=0):
                for half in range(2):
                    arrived(n + half, more)
                    w = slot(n + half, CH)
                    for k in range(HALF):
                        last = pe.matmul(bank, stationary(half * HALF + k), w[:, k, :],
                                         start=(half + k == 0), stop=(half == 1 and k == HALF - 1))
                    last.then_inc(piece_done, 1)

            def to_feature(src, kt, first, base):
                for g in range(kt // 2):
                    bank = BANK[first + (base + g) % 2]
                    if base + g >= 2:
                        pe.wait_ge(xT_taken, 2 * (base + g - 1))
                    for f in range(2):
                        for t in range(TT):
                            last = pe.transpose(bank[:, f * L + t * P:f * L + (t + 1) * P],
                                                src[:, t, (2 * g + f) * P:(2 * g + f + 1) * P], ident[:])
                    last.then_inc(xT_ready, 1)

            pe.wait_ge(consts_set, 2)
            pe.wait_ge(params_in, PARAM_DMAS * 16)
            for g, r in enumerate(GROUP_ROWS):
                last = pe.transpose(BANK[6][:, g * P:g * P + r], rows[0:r, g, :], ident[0:r, 0:r])
            last.then_inc(colsT_ready, 1)
            pe.wait_ge(cs_ready, 1)
            for j in range(2):
                ada_chunk(n_ada + 2 * j, BANK[j][0:1, :], lambda k: cs[:, k:k + 1])
            with pe.Fori(1, NADA // 2) as i:
                for j in range(2):
                    pe.wait_ge(row_took, i * 2 + j - 1)
                    ada_chunk(n_ada + 2 * j, BANK[j][0:1, :], lambda k: cs[:, k:k + 1], more=i)
            for j in range(2 * KT):
                pe.wait_ge(row_took, j // 4 + 1)
                last = pe.matmul(BANK[7][:, j:j + 1], MROW[:, j * P:(j + 1) * P], ones[0:1, 0:1],
                                 start=True, stop=True)
            last.then_inc(modT_ready, 1)
            pe.wait_ge(xn_ready, 2)
            to_feature(XN, KT, 4, 0)
            pe.wait_ge(xT_taken, KT)
            tok_chunk(n_kw, 0, KW)
            feat_chunk(n_qi, 1, CH)
            pe.wait_ge(act_took, 2)
            feat_chunk(n_qi + 2, 0, CH)
            pe.wait_ge(kix_ready, 4)
            for lo in range(2):
                for t in range(TT):
                    last = pe.transpose(BANK[6][:, lo * L + t * P:lo * L + (t + 1) * P], KIX[:, t, lo, :], ident[:])
            last.then_inc(kixT_ready, 1)
            pe.wait_ge(kb_ready, 1)
            pe.wait_ge(act_took, 6)
            for j in range(8):
                for t in range(TT):
                    s = 2 * j + t
                    w = (t + 1) * P
                    if s >= 2:
                        pe.wait_ge(relu_ready, s - 1)
                    pe.matmul(BANK[4 + t][:, 0:2 * w].rearrange("p (a n) -> p a n", a=2), QI[:, j, t * P:(t + 1) * P], KB[:, :, 0:w],
                              start=True, stop=True).then_inc(idx_ready, 1)
            with pe.Fori(0, 2) as b:
                for j in range(8):
                    pe.wait_ge(act_took, b * 16 + 6 + 2 * j - 2)
                    tok_chunk(n_br + 2 * j, (j + 1) % 2, CH, more=b * 4)
                    if 1 <= j <= 4:
                        c = j - 1
                        pe.wait_ge(head_normed, b * 4 + c + 1)
                        for g in range(2):
                            for f in range(2):
                                for t in range(TT):
                                    h = 2 * g + f
                                    last = pe.transpose(BANK[4 + 2 * (c % 2) + g][:, f * L + t * P:f * L + (t + 1) * P],
                                                        stage[:, c % 2, t, h * P:(h + 1) * P], ident[:])
                        last.then_inc(headT_ready, 1)
            pe.wait_ge(cs_wide_ready, 1)
            with pe.Fori(0, 2) as i:
                for j in range(2):
                    pe.wait_ge(act_took, i * 2 + (ACT_GATE - 1 + j))
                    ada_chunk(n_gate + 2 * j, BANK[2 * j][:, :], lambda k: cs_wide[:, k, :], more=i)
            attention_pe(pe, 2 * HEADS, 0,
                         lambda h, t: [(QT[:, h // HEADS, h % HEADS, t * P:(t + 1) * P],
                                        KTT[:, h // HEADS, h % HEADS, 0:(t + 1) * P])],
                         lambda h, k: V1[:, h // HEADS, k, (h % HEADS) * DH:(h % HEADS + 1) * DH], Pr, PTs)
            pe.wait_ge(out_taken, 4 * HEADS)
            for bb in range(2):
                to_feature(Z1[:, bb], 8, 4, 8 + 4 * bb)
            pe.wait_ge(xT_taken, 2 * KT)
            pe.wait_ge(act_took, ACT_RKV)
            for c in range(4):
                if c >= 2:
                    pe.wait_ge(x_updated, 2 * (c - 1))
                tok_chunk(n_wo + 2 * c, c % 2, CH)
            pe.wait_ge(xn_ready, 4)
            to_feature(XN2, KT, 4, 16)
            pe.wait_ge(xT_taken, 48)
            with pe.Fori(0, 3) as i:
                for j in range(2):
                    pe.wait_ge(act_took, i * 4 + (ACT_RKV + 2 * j - 2))
                    feat_chunk(n_rkv + 2 * j, j, CH, more=i)
            pe.wait_ge(act_took, ACT_RKV + 2 * 5)
            feat_chunk(n_wag, 0, WAG, tiles=WAG_TILES)
            pe.wait_ge(act_took, ACT_RKV + 2 * 6)
            tok_chunk(n_kpe, 1, ROPE)
            for j in range(2):
                pe.wait_ge(act_took, ACT_RKV + 2 * (7 + j))
                tok_chunk(n_c + 2 * j, j, CH)
            pe.wait_ge(kpx_ready, 4)
            to_feature(KPX.rearrange("p t a n -> p t (a n)"), 2, 4, 24)
            pe.wait_ge(c_normed, 2 * TT)
            for q in range(2):
                to_feature(CQ[:, 2 * q:2 * q + 2, :], 4, 4, 25 + 2 * q)
            pe.wait_ge(xT_taken, 2 * 29)
            for part, (n, stride) in enumerate(((n_uq, 192), (n_uq + 1, 192), (n_ukv, 256), (n_ukv + 1, 256))):
                c0 = 0 if part < 2 else 4
                arrived(n)
                w = slot(n, 4 * stride, 4)
                pe.wait_ge(act_took, ACT_RKV + 2 * (9 + 2 * part))
                for h in range(4):
                    for k in range(4):
                        last = pe.matmul(BANK[h // 2][:, (h % 2) * L:(h % 2 + 1) * L],
                                         w[:, k, h * stride:h * stride + P], CT[:, c0 + k, :],
                                         start=(k == 0), stop=(k == 3))
                last.then_inc(lora_ready, 1)
                pe.wait_ge(act_took, ACT_RKV + 2 * (10 + 2 * part))
                width = stride - P
                for k in range(4):
                    for t in range(TT):
                        last = pe.matmul(BANK[2 + t][:, 0:4 * width].rearrange("p (h n) -> p h n", h=4),
                                         CT[:, c0 + k, t * P:(t + 1) * P],
                                         w[:, k, :].rearrange("p (h n) -> p h n", h=4)[:, :, P:stride],
                                         start=(k == 0), stop=(k == 3))
                last.then_inc(piece_done, 1)
            pe.wait_ge(qpr_ready, 1)
            to_feature(QPR, 4, 4, 29)
            pe.wait_ge(xT_taken, 2 * 31)
            pe.wait_ge(act_took, ACT_RKV + 36)
            attention_pe(pe, HEADS, 2 * HEADS,
                         lambda h, t: [(QN[:, h, t * P:(t + 1) * P], KN[:, h, 0:(t + 1) * P]),
                                       (QPT[:, h // 2, t * P:(t + 1) * P], KPT[:, h % 2, 0:(t + 1) * P])],
                         lambda h, k: VM[:, k, h * DH:(h + 1) * DH], Pr2, PT2)
            pe.wait_ge(out_taken, 6 * HEADS)
            to_feature(YM, 8, 4, 31)
            pe.wait_ge(wag_ready, 4)
            for q, h in enumerate((HW, HA)):
                arrived(n_w2 + q)
                for g in range(4):
                    r = 4 * q + g
                    if r >= 4:
                        pe.wait_ge(rw_small_took, 2 * (r - 3))
                    for f in range(2):
                        last = pe.matmul(BANK[r % 4][:, f * L:(f + 1) * L],
                                         ring[0:64, (n_w2 + q) % NSLOT, (2 * g + f) * P:(2 * g + f + 1) * P],
                                         h[0:64, :], start=True, stop=True)
                    last.then_inc(rw_small, 1)
            pe.wait_ge(rw_masks, 1)
            pe.wait_ge(rw_small_took, 16)
            pe.wait_ge(kk_sq, 1)
            for g in range(4):
                pe.matmul(BANK[g][:, :], head_ones, sqk[:, 2 * g:2 * g + 2, :], start=True, stop=True).then_inc(kk_sum, 1)
            pe.wait_ge(prep_ready, 1)
            P_ = Steps(pe_step, pe_names)
            A_, D_ = Steps(act_step, act_names), Steps(dve_step, dve_names)
            with pe.Fori(0, 2) as g, pe.Fori(0, NCH) as c:
                it = g * NCH + c

                def four(name, bank, lhsT, rhs, width, extra=()):
                    o = BANK[bank][:, 0:4 * width].rearrange("p (q n) -> p q n", q=4)
                    terms = [(lhsT, rhs), *extra]
                    for q in range(4):
                        for n, (x, y) in enumerate(terms):
                            last = pe.matmul(o[:, q, :], x[:, q, :], y[:, q, :] if len(y.shape) == 3 else y,
                                             start=(n == 0), stop=(n == len(terms) - 1))
                    P_.mark(last, name)

                D_.wait(pe, "a1", it)
                four("LT", 0, b_bd, a_bd, P)
                four("AkT", 1, k_bd, a_bd, P)
                for name, bank, src in (("btok", 2, b_bd), ("ktok", 3, k_bd)):
                    for q in range(4):
                        last = pe.transpose(BANK[bank][:, q * P:(q + 1) * P], src[:, q, :], ident[:])
                    P_.mark(last, name)
                four("Vp", 4, v_bd, I2, N)
                four("BrT", 5, b_bd, r_bd, P)
                four("KrT", 6, k_bd, r_bd, P)
                for m in range(LEVELS):
                    if m == 0:
                        D_.wait(pe, "LT", it)
                        four("T0", 7, LT, ident[:], P)
                        D_.wait(pe, "T0", it)
                        four("Z0", 1, T2, ident[:], P)
                        continue
                    D_.wait(pe, f"X{m - 1}", it)
                    four(f"T{m}", 7, LT, Xi, P)
                    D_.wait(pe, f"T{m}", it)
                    if m < LEVELS - 1:
                        four(f"X{m}", 0, Zi, T2, P)
                    four(f"Z{m}", 1, T2, Zi, P)
                A_.wait(pe, "Vp", it)
                D_.wait(pe, "AkT", it)
                four("P1", 4, a_bd, ST, N, [(AkT, Vp)])
                D_.wait(pe, f"Z{LEVELS - 1}", it)
                A_.wait(pe, "P1", it)
                four("U", 2, Zi, P1, N)
                A_.wait(pe, "U", it)
                D_.wait(pe, "KrT", it)
                four("Y", 3, r_bd, ST, N, [(BrT, Us), (KrT, Vp)])
                four("S", 5, b_tok, Us, N, [(k_tok, Vp)])
                D_.wait(pe, "y1", it)
                four("YT", 6, y_bd, I2, N)
            pe.wait_ge(rk_ready, 1)
            for g in range(4):
                pe.matmul(BANK[g][:, :], head_ones, RK2[:, 2 * g:2 * g + 2, :], start=True, stop=True) \
                    .then_inc(bonus_ready, 1)
            arrived(n_w2 + 2)
            arrived(n_w2 + 3)
            for g in range(4):
                pe.wait_ge(bonus_took, g + 1)
                for f in range(2):
                    for n, h in enumerate((HG0, HG1)):
                        r = (P, 32)[n]
                        last = pe.matmul(BANK[g][:, f * L:(f + 1) * L],
                                         ring[0:r, (n_w2 + 2 + n) % NSLOT, (2 * g + f) * P:(2 * g + f + 1) * P],
                                         h[0:r, :], start=(n == 0), stop=(n == 1))
                if g < 3:
                    last.then_inc(g_ready, 1)
                else:
                    last.then_inc(piece_done, 4)
            pe.wait_ge(g_took, 8)
            pe.wait_ge(xT_taken, 2 * 35)
            for c in range(4):
                if c >= 2:
                    pe.wait_ge(x_updated, 8 + 2 * (c - 1))
                tok_chunk(n_wo2 + 2 * c, c % 2, CH)
            pe.wait_ge(xn_ready, 6)
            to_feature(XN3, KT, 4, 35)
            pe.wait_ge(xT_taken, 2 * 43)
            with pe.Fori(0, FF // CH) as i:
                pe.wait_ge(act_took, i * 2 + (ACT_RKV + 36))
                feat_chunk(n_gu, 0, CH, more=i)
                pe.wait_ge(up_taken, i * 2 + 1)
                feat_chunk(n_gu + 2, 1, CH, more=i)
            pe.wait_ge(up_taken, FF // CH * 2 + 1)
            with pe.Fori(0, 2) as i:
                for j in range(2):
                    pe.wait_ge(x_updated, i * 4 + (14 + 2 * j))
                    for q in range(6):
                        n = n_dn + 6 * j + q
                        pe.wait_ge(piece_in[n % NSLOT], i * 48 + 16 * (n // NSLOT + 1))
                        w = slot(n, CH, HALF)
                        for k in range(HALF if q < 5 else 4):
                            kk = q * HALF + k
                            for t in range(TT):
                                last = pe.matmul(BANK[2 * j + t][:, :], AC[:, kk, t * P:(t + 1) * P], w[:, k, :],
                                                 start=(kk == 0), stop=(kk == FT - 1))
                        last.then_inc(piece_done, 1)

        @block.scalar
        def _(act):
            own = Chain(act, act_chain_s)
            for t in range(TT):
                act.dma_start(X[:, t, :], a["x"][0, t * P:(t + 1) * P, :]).then_inc(x_in, 16)
            act.wait_ge(rows_clear, 1)
            for name, _ in PARAMS:
                g, row, r = VEC[name]
                v = a[name]
                if len(v.shape) == 3:
                    v = v.rearrange("o a b -> o (a b)")
                v = v[0]
                if name == "rwkv_mu_2":
                    for r0, rn, c0, w in [(0, 24, 0, P)] + [(24 + i, 1, WAG_COL + b, w)
                                                            for i, (b, w) in enumerate(WAG_TILES)]:
                        act.dma_start(rows[row + r0:row + r0 + rn, g, 0:w],
                                      v[c0:c0 + rn * w].rearrange("(a n) -> a n", a=rn)).then_inc(params_in, 16)
                else:
                    act.dma_start(rows[row:row + r, g, :], v.rearrange("(a n) -> a n", n=P)).then_inc(params_in, 16)
            for tap in range(3):
                g, row, r = VEC[f"conv{tap}"]
                act.dma_start(rows[row:row + r, g, :],
                              a["ffn_conv_w_2"][0, tap, :].rearrange("(a n) -> a n", n=P)).then_inc(params_in, 16)
            act.dma_start(kin_g, a["k_norm_idx"][0:1, :].to_broadcast([P, IDX_DIM])).then_inc(misc_in, 16)

            act.wait_ge(x_in, 32)
            for t in range(TT):
                act.activation(XN[:, t, :], X[:, t, :], ACT.Square, accum_out=ss[:, t:t + 1]).then_inc(ssq_ready, 1)
            act.wait_ge(cols_ready, 1)
            act.activation(cs, col("c", 0, 16), ACT.Silu).then_inc(cs_ready, 1)

            def sqrt_of(dst, src):
                return act.activation(dst, src, ACT.Sqrt)

            act.wait_ge(var_ready, 1)
            sqrt_of(rstd, rstd).then_inc(rstd_ready, 1)

            def read_chunk(n, pair, dsts, func=ACT.Copy, more=0, width=CH, parts=P, signal=None):
                act.wait_ge(piece_done, more + n + 2)
                for t, dst in enumerate(dsts):
                    act.activation(dst, BANK[2 * pair + t][0:parts, 0:width], func).then_inc(act_took, 1)

            for j in range(2):
                act.wait_ge(piece_done, 2 * j + 2)
                act.activation(MROW[:, j * CH:(j + 1) * CH], BANK[j][0:1, :], ACT.Copy).then_inc(row_took, 1)
            with act.Fori(1, NADA // 2) as i:
                for j in range(2):
                    act.wait_ge(piece_done, i * 4 + 2 * j + 2)
                    act.activation(MROW[:, ds(i * 2 * CH + j * CH, CH)], BANK[j][0:1, :],
                                   ACT.Copy).then_inc(row_took, 1)

            act.wait_ge(mod_ready, 1)
            for g in range(KT // 2):
                act.wait_ge(xT_ready, g + 1)
                for f in range(2):
                    k = 2 * g + f
                    act.activation(HT[:, k, :], BANK[4 + g % 2][:, f * L:(f + 1) * L], ACT.Identity,
                                   bias=mod[:, k:k + 1], scale=gs[:, k:k + 1]).then_inc(xT_taken, 1)
            read_chunk(n_kw, 0, [KI[:, t, :] for t in range(TT)], width=KW)
            act.wait_ge(ki_var, 1)
            sqrt_of(krstd, krstd).then_inc(ki_rstd, 1)
            for j in range(2):
                read_chunk(n_qi + 2 * j, (1 + j) % 2, [QI[:, 4 * j + 2 * t:4 * j + 2 * t + 2, :].rearrange(
                    "p a n -> p (a n)") for t in range(TT)])
            act.wait_ge(kixT_ready, 1)
            act.activation(KB.rearrange("p a n -> p (a n)"), BANK[6][:, :], ACT.Copy).then_inc(kb_ready, 1)
            for s in range(16):
                t = s % 2
                w = (t + 1) * 2 * P
                act.wait_ge(idx_ready, s + 1)
                if s >= 2:
                    act.wait_ge(relu_used, s - 1)
                act.activation(relu[:, t, 0:w], BANK[4 + t][:, 0:w], ACT.Relu).then_inc(relu_ready, 1)
            with act.Fori(0, 2) as b:
                for j in range(8):
                    n, pair = n_br + 2 * j, (j + 1) % 2
                    if j < 4:
                        if j >= 2:
                            act.wait_ge(headT_ready, b * 4 + j - 1)
                        read_chunk(n, pair, [stage[:, j % 2, t, :] for t in range(TT)], more=b * 16)
                        act.wait_ge(head_var, b * 4 + j + 1)
                        sqrt_of(hrstd[:, 8 * (j % 2):8 * (j % 2) + 8],
                                hrstd[:, 8 * (j % 2):8 * (j % 2) + 8]).then_inc(head_rstd, 1)
                    elif j < 6:
                        read_chunk(n, pair, [V1[:, ds(b, 1), t, (j - 4) * CH:(j - 3) * CH].rearrange("p o n -> p (o n)") for t in range(TT)],
                                   more=b * 16)
                    else:
                        read_chunk(n, pair, [Z1[:, ds(b, 1), t, (j - 6) * CH:(j - 5) * CH].rearrange("p o n -> p (o n)") for t in range(TT)],
                                   func=ACT.Silu, more=b * 16)
                    if 1 <= j <= 4:
                        c = j - 1
                        act.wait_ge(headT_ready, b * 4 + c + 1)
                        dst = QT if c < 2 else KTT
                        for g in range(2):
                            h = 4 * (c % 2) + 2 * g
                            act.activation(dst[:, ds(b, 1), h:h + 2, :].rearrange("p o a n -> p (o a n)"),
                                           BANK[4 + 2 * (c % 2) + g][:, :], ACT.Copy,
                                           scale=qgain[:, ds(b + (0 if c < 2 else 2), 1)]).then_inc(headT_taken, 1)
            act.wait_ge(piece_done, n_gate)
            act.dma_start(bgate_row, a["b_ada"][0:1, 2 * D:3 * D].to_broadcast([P, D])).then_inc(bgate_in, 16)
            for c in range(4):
                act.wait_ge(piece_done, n_gate + 2 * c + 2)
                act.activation(gate_row[:, c * CH:(c + 1) * CH], BANK[2 * (c % 2)][:, :], ACT.Copy).then_inc(act_took, 1)
            attention_act(act, 2 * HEADS, 0, S_sb, Pr, PTs)
            for g in range(8):
                act.wait_ge(xT_ready, 8 + g + 1)
                act.activation(HT[:, 2 * g:2 * g + 2, :].rearrange("p a n -> p (a n)"),
                               BANK[4 + g % 2][:, :], ACT.Copy).then_inc(xT_taken, 2)
            for t in range(TT):
                act.dma_start(pos_i[:, t:t + 1], a["positions_2"][0, t * P:(t + 1) * P].rearrange("(p o) -> p o", o=1)) \
                   .then_inc(pos_in, 16)

            def norm_act(q, junk, updates, c=None):
                act.wait_ge(x_updated, updates)
                for t in range(TT):
                    act.activation(junk[:, t, :], X[:, t, :], ACT.Square, accum_out=ss[:, t:t + 1]).then_inc(ssq_ready, 1)
                act.wait_ge(var_ready, q + 1)
                sqrt_of(rstd, rstd).then_inc(rstd_ready, 1)

            def take_feature(dsts, base, gains=None):
                for g in range(len(dsts) // 2):
                    act.wait_ge(xT_ready, base + g + 1)
                    for f in range(2):
                        k = 2 * g + f
                        act.activation(dsts[k], BANK[4 + (base + g) % 2][:, f * L:(f + 1) * L], ACT.Copy,
                                       scale=gains[k] if gains else 1.0).then_inc(xT_taken, 1)

            norm_act(1, XN2, 8)
            take_feature([HT[:, k, :] for k in range(KT)], 16, [col("attn_norm_g_2", k) for k in range(KT)])
            act.wait_ge(ang_ready, 1)
            act.activation(ang.rearrange("p s t n -> p (s t n)"), turns.rearrange("p s t n -> p (s t n)"),
                           ACT.Sin).then_inc(trig_ready, 1)
            act.wait_ge(raw_clear, 1)
            with act.Fori(0, 3) as i:
                for j in range(2):
                    act.wait_ge(piece_done, i * 4 + (n_rkv + 2 * j + 2))
                    act.wait_ge(shifted, i * 2 + (j + 1))
                    for t in range(TT):
                        act.activation(RAW[:, 2 * t:2 * t + 2, 1:L + 1],
                                       BANK[2 * j + t][:, :].rearrange("p (f n) -> p f n", f=2),
                                       ACT.Copy).then_inc(act_took, 1)
            act.wait_ge(piece_done, n_wag + 2)
            act.wait_ge(shifted, 7)
            for f, (_, m) in enumerate(WAG_TILES):
                last = act.activation(RAW[0:m, f, 1:L + 1], BANK[f // 2][0:m, (f % 2) * L:(f % 2 + 1) * L], ACT.Copy)
                if f % 2:
                    last.then_inc(act_took, 1)
            read_chunk(n_kpe, 1, [KPE[:, t, :] for t in range(TT)], width=ROPE)
            for j in range(2):
                read_chunk(n_c + 2 * j, j, [CQ[:, 2 * j + t, :] for t in range(TT)])
            for j in range(4):
                act.wait_ge(act_took, ACT_RKV + 2 * 9 + 2)
                act.activation(XN2[:, j // 2, (j % 2) * CH:(j % 2 + 1) * CH], CQ[:, j, :], ACT.Square,
                               accum_out=cstat[:, j:j + 1]).then_inc(c_sq, 1)
            act.wait_ge(c_var, 1)
            sqrt_of(crstd, crstd).then_inc(c_rstd, 1)
            act.wait_ge(wag_ready, 3)
            act.activation(HW[0:64, :], HW[0:64, :], ACT.Tanh).then_inc(rw_mid, 1)
            take_feature([KPT[:, k, :] for k in range(2)], 24)
            for q, name in enumerate(("mla_q_norm_g_2", "mla_kv_norm_g_2")):
                take_feature([CT[:, 4 * q + k, :] for k in range(4)], 25 + 2 * q, [col(name, k) for k in range(4)])
            scale = float(DH + ROPE) ** -0.5
            for part in range(4):
                dst, o = (QN, KN)[part // 2], 4 * (part % 2)
                act.wait_ge(lora_ready, part + 1)
                for t in range(TT):
                    act.activation(dst[:, o + 2 * t:o + 2 * t + 2, :].rearrange("p a n -> p (a n)"), BANK[t][:, :],
                                   ACT.Copy, scale=scale if part < 2 else 1.0).then_inc(act_took, 1)
                act.wait_ge(piece_done, n_uq + part + 1)
                for t in range(TT):
                    if part < 2:
                        act.activation(QPE[:, t, part * 256:(part + 1) * 256], BANK[2 + t][:, 0:256], ACT.Copy,
                                       scale=scale).then_inc(act_took, 1)
                    else:
                        act.activation(VM[:, t, (part - 2) * CH:(part - 1) * CH], BANK[2 + t][:, :],
                                       ACT.Copy).then_inc(act_took, 1)
            take_feature([QPT[:, k, :] for k in range(4)], 29)
            attention_act(act, HEADS, 2 * HEADS, S2, Pr2, PT2)
            take_feature([HT[:, 8 + k, :] for k in range(8)], 31)
            act.activation(HG0, HG0, ACT.Sigmoid).then_inc(wag_ready, 1)
            act.activation(HG1[0:32, :], HG1[0:32, :], ACT.Sigmoid).then_inc(rw_mid, 1)
            for r in range(8):
                act.wait_ge(rw_small, r + 1)
                dst, bias = ((Lw, "rwkv_w0_2"), (Bv, "rwkv_a0_2"))[r // 4]
                for f in range(2):
                    k = 2 * (r % 4) + f
                    act.activation(dst[:, k, :], BANK[r % 4][:, f * L:(f + 1) * L], ACT.Sigmoid,
                                   bias=col(bias, k)).then_inc(rw_small_took, 1)
            act.wait_ge(kk_var, 1)
            act.activation(sqk.rearrange("p f n -> p (f n)"), sqk.rearrange("p f n -> p (f n)"),
                           ACT.Sqrt).then_inc(kk_rstd, 1)
            act.wait_ge(fac_raw, 1)
            act.activation(small[:, 328:360], small[:, 328:360], ACT.Exp).then_inc(fac_ready, 1)
            act.wait_ge(prep_ready, 1)
            P_ = Steps(pe_step, pe_names)
            A_, D_ = Steps(act_step, act_names), Steps(dve_step, dve_names)
            with act.Fori(0, 2) as g, act.Fori(0, NCH) as c:
                it = g * NCH + c
                e = El[:, ds(4 * g, 4), ds(c * C, C)]
                A_.mark(act.activation(EX, e, ACT.Exp), "EX")
                A_.mark(act.activation(EN, e, ACT.Exp, scale=-1.0), "EN")
                D_.wait(act, "DEL", it)
                A_.mark(act.activation(EXC, DEL, ACT.Exp), "EXC")
                for name, dst, bank, w in (("btok", b_tok, 2, P), ("ktok", k_tok, 3, P), ("Vp", Vp, 4, N),
                                           ("P1", P1, 4, N), ("U", Us, 2, N)):
                    P_.wait(act, name, it)
                    A_.mark(act.activation(dst.rearrange("p q n -> p (q n)"), BANK[bank][:, 0:4 * w], ACT.Copy), name)
                D_.wait(act, "gi", it)
                A_.mark(act.activation(gvar, gvar, ACT.Sqrt), "sq")
                P_.wait(act, "YT", it)
                A_.mark(act.activation(HT[:, ds(4 * g, 4), ds(c * C, C)],
                                       BANK[6][:, 0:4 * N].rearrange("p (q n) -> p q n", q=4), ACT.Copy), "YT")
            norm_act(2, XN3, 16)
            act.dma_start(fg_row, a["final_norm_g_2"].rearrange("(o n) -> o n", o=1).to_broadcast([P, D])).then_inc(fg_in, 16)
            take_feature([HT[:, k, :] for k in range(KT)], 35, [col("ffn_norm_g_2", k) for k in range(KT)])
            with act.Fori(0, FF // CH) as i:
                act.wait_ge(piece_done, i * 4 + (n_gu + 2))
                act.wait_ge(conv_ready, i + 1)
                for t in range(TT):
                    act.activation(RAWF[:, 2 * t:2 * t + 2, 2:L + 2],
                                   BANK[t][:, :].rearrange("p (f n) -> p f n", f=2), ACT.Copy).then_inc(act_took, 1)
                act.wait_ge(conv_ready, i + 2)
                act.activation(CV.rearrange("p f n -> p (f n)"), CV.rearrange("p f n -> p (f n)"),
                               ACT.Silu).then_inc(gate_act, 1)
            norm_act(3, XN3, 24)

        @block.vector
        def _(dve):
            own = Chain(dve, dve_chain_s)

            def inverse_mean(dst, src, width, eps=EPS):
                own.link(dve.tensor_scalar(dst, src, 1.0 / width, eps, ALU.mult, ALU.add))
                return dve.reciprocal(dst, dst)

            def norm_dve(q):
                dve.wait_ge(ssq_ready, 2 * (q + 1))
                inverse_mean(rstd, ss, D).then_inc(var_ready, 1)

            def scale_x(q, dst):
                dve.wait_ge(rstd_ready, q + 1)
                for t in range(TT):
                    dve.tensor_scalar(dst[:, t, :], X[:, t, :], rstd[:, t:t + 1], None, ALU.mult).then_inc(xn_ready, 1)

            norm_dve(0)
            dve.wait_ge(colsT_ready, 1)
            for g, r in enumerate(GROUP_ROWS):
                last = dve.tensor_copy(cols[:, g * P:g * P + r], BANK[6][:, g * P:g * P + r])
            last.then_inc(cols_ready, 1)
            dve.wait_ge(cols_ready, 1)
            for b in range(2):
                own.mark(dve.tensor_scalar(qgain[:, b:b + 1], col(("q_norm_a", "q_norm_b")[b]), float(DH) ** -0.5, None, ALU.mult))
                own.mark(dve.tensor_copy(qgain[:, 2 + b:3 + b], col(("k_norm_a", "k_norm_b")[b])))
            scale_x(0, XN)
            dve.wait_ge(modT_ready, 1)
            own.link(dve.tensor_tensor(mod[:, 0:32], BANK[7][:, 0:32], col("b_ada", 0, 32), ALU.add))
            own.link(dve.tensor_scalar(gs, mod[:, 16:32], 1.0, None, ALU.add))
            dve.tensor_tensor(gs, gs, col("g_norm", 0, 16), ALU.mult).then_inc(mod_ready, 1)
            dve.wait_ge(act_took, 2)
            for t in range(TT):
                own.link(dve.tensor_tensor(square[:, t, 0:IDX_DIM], KI[:, t, 0:IDX_DIM], KI[:, t, 0:IDX_DIM], ALU.mult))
                own.link(dve.tensor_reduce(kss[:, t:t + 1], square[:, t, 0:IDX_DIM], AX_X, ALU.add))
            inverse_mean(krstd, kss, IDX_DIM).then_inc(ki_var, 1)
            dve.wait_ge(ki_rstd, 1)
            dve.wait_ge(misc_in, 16)
            dve.wait_ge(consts_set, CONSTS)
            for t in range(TT):
                for lo in range(2):
                    dve.scalar_tensor_tensor(out=KIX[:, t, lo, lo * IDX_DIM:(lo + 1) * IDX_DIM], in0=KI[:, t, 0:IDX_DIM],
                                             scalar=krstd[:, t:t + 1], in1=kin_g, op0=ALU.mult,
                                             op1=ALU.mult).then_inc(kix_ready, 1)
            for s in range(16):
                j, t = s // 2, s % 2
                w = (t + 1) * P
                sc = score[:, 0:P] if t == 0 else score[:, P:SPAN]
                dve.wait_ge(relu_ready, s + 1)
                for f in range(2):
                    wt = KI[:, t, IDX_DIM + 2 * j + f:IDX_DIM + 2 * j + f + 1]
                    r = relu[:, t, f * w:(f + 1) * w]
                    if j == 0 and f == 0:
                        own.link(dve.tensor_scalar(sc, r, wt, None, ALU.mult))
                    else:
                        ins = dve.scalar_tensor_tensor(out=sc, in0=r, scalar=wt, in1=sc, op0=ALU.mult, op1=ALU.add)
                        if f == 1:
                            ins.then_inc(relu_used, 1)
                            dve.wait_ge(relu_used, s + 1)
                        else:
                            own.link(ins)
            own.link(dve.tensor_tensor(score, score, causal_mask, ALU.add))
            own.link(dve.tensor_copy(work, score))
            halves = [(0, P), (P, L)]
            for r in range(TOPK // 8):
                for t, (c0, w) in enumerate(halves):
                    own.mark(dve.max(top8[:, t, :], work[:, c0:c0 + w]))
                own.wait()
                if r < TOPK // 8 - 1:
                    for t, (c0, w) in enumerate(halves):
                        own.mark(dve.match_replace(work[:, c0:c0 + w], top8[:, t, :], work[:, c0:c0 + w], -3e38))
                    own.wait()
            for t, (c0, w) in enumerate(halves):
                thr = top8[:, t, 7:8]
                sc, wk, gt = score[:, c0:c0 + w], work[:, c0:c0 + w], bias_a[:, c0:c0 + w]
                eq, run = square[:, t, 0:w], relu[:, t, 0:w]
                own.link(dve.tensor_scalar(gt, sc, thr, None, ALU.is_gt, ALU.add, accum_out=cnt[:, t:t + 1]))
                own.link(dve.tensor_scalar(need[:, t:t + 1], cnt[:, t:t + 1], -1.0, float(TOPK), ALU.mult, ALU.add))
                own.link(dve.tensor_scalar(eq, sc, thr, None, ALU.is_equal))
                own.link(dve.memset(wk, 1.0))
                own.link(dve.tensor_tensor_scan(run, wk, eq, 0.0, ALU.mult, ALU.add))
                own.link(dve.scalar_tensor_tensor(out=eq, in0=run, scalar=need[:, t:t + 1], in1=eq,
                                                  op0=ALU.is_le, op1=ALU.mult))
                own.link(dve.tensor_tensor(gt, gt, eq, ALU.add))
                own.link(dve.tensor_scalar(gt, gt, -1.0, -NEG, ALU.add, ALU.mult))
                own.link(dve.tensor_tensor(gt, gt, causal_dist[:, c0:c0 + w], ALU.add))
            with dve.Fori(0, 2) as b:
                own.enter(b, 12)
                for j in range(4):
                    s = stage[:, j % 2]
                    flat = s.rearrange("p t n -> p (t n)")
                    sq = square.rearrange("p t n -> p (t n)")
                    dve.wait_ge(act_took, b * 16 + 6 + 2 * (j + 1))
                    own.link(dve.tensor_tensor(sq, flat, flat, ALU.mult))
                    hs, hr = hss[:, 8 * (j % 2):8 * (j % 2) + 8], hrstd[:, 8 * (j % 2):8 * (j % 2) + 8]
                    own.link(dve.tensor_reduce(hs, sq.rearrange("p (g n) -> p g n", n=DH), AX_X, ALU.add))
                    inverse_mean(hr, hs, DH).then_inc(head_var, 1)
                    dve.wait_ge(head_rstd, b * 4 + j + 1)
                    for g in range(8):
                        v = s[:, g // 4, (g % 4) * DH:(g % 4 + 1) * DH]
                        last = dve.tensor_scalar(v, v, hr[:, g:g + 1], None, ALU.mult)
                    last.then_inc(head_normed, 1)
                own.leave(2)

            dve.wait_ge(piece_done, n_gate)
            dve.tensor_copy(cs_wide, cs.unsqueeze(2).to_broadcast([P, KT, P])).then_inc(cs_wide_ready, 1)
            dve.wait_ge(bgate_in, 16)
            dve.wait_ge(act_took, ACT_RKV)
            own.link(dve.tensor_tensor(gate_row, gate_row, bgate_row, ALU.add))

            def emit(h, t, o, inv):
                b, hh = h // HEADS, h % HEADS
                z = Z1[:, b, t, hh * DH:(hh + 1) * DH]
                return dve.scalar_tensor_tensor(out=z, in0=o, scalar=inv, in1=z, op0=ALU.mult, op1=ALU.mult)

            attention_dve(dve, own, 2 * HEADS, 0,
                          lambda h: bias_a if h < HEADS else causal_dist,
                          lambda h: slope[:, h:h + 1], emit, S_sb)
            for c in range(4):
                dve.wait_ge(piece_done, n_wo + 2 * c + 2)
                for t in range(TT):
                    xc = X[:, t, c * CH:(c + 1) * CH]
                    own.link(dve.tensor_tensor(wo_tmp[:, t, :], BANK[2 * (c % 2) + t][:, :],
                                               gate_row[:, c * CH:(c + 1) * CH], ALU.mult))
                    dve.tensor_tensor(xc, xc, wo_tmp[:, t, :], ALU.add).then_inc(x_updated, 1)
            norm_dve(1)
            scale_x(1, XN2)
            for j in range(32):
                own.mark(dve.memset(inv_freq[:, j:j + 1], float(np.float32(10000.0) ** np.float32(-j / 32.0))))
            dve.wait_ge(pos_in, 32)
            own.mark(dve.tensor_copy(pos, pos_i))
            own.wait()
            flat = lambda v: v.rearrange("p t n -> p (t n)")
            two_pi = 2 * np.pi
            c1 = 6.28125
            c2 = float(np.float32(int((two_pi - c1) * 2 ** 21) / 2 ** 21))
            c3 = float(two_pi - c1 - c2)
            magic = 1.5 * 2 ** 23
            for part in range(2):
                th, nt = ang[:, part], turns[:, part]
                for t in range(TT):
                    own.mark(dve.tensor_scalar(th[:, t, :], inv_freq, pos[:, t:t + 1], None, ALU.mult))
                own.wait()
                own.link(dve.tensor_scalar(flat(nt), flat(th), float(1 / two_pi), 0.25 * part, ALU.mult, ALU.add))
                own.link(dve.tensor_scalar(flat(nt), flat(nt), magic, -magic, ALU.add, ALU.add))
                for cc in (c1, c2, c3):
                    own.link(dve.scalar_tensor_tensor(out=flat(th), in0=flat(nt), scalar=-cc, in1=flat(th),
                                                      op0=ALU.mult, op1=ALU.add))
                own.link(dve.tensor_scalar(flat(th), flat(th), float(np.pi / 2) * part, None, ALU.add))
                lim = float(np.nextafter(np.float32(np.pi), np.float32(0)))
                own.link(dve.tensor_scalar(flat(nt), flat(th), lim, -lim, ALU.min, ALU.max))
            dve.tensor_copy(small[:, 510:511], pos[:, 0:1]).then_inc(ang_ready, 1)
            own.link(dve.memset(RAW[:, :, 0:1], 0.0))
            dve.memset(small[:, 509:510], 0.0).then_inc(raw_clear, 1)
            dve.memset(small[:, 508:509], 0.0).then_inc(shifted, 1)
            gm, rm, _ = VEC["rwkv_mu_2"]
            mu0 = gm * P + rm
            with dve.Fori(0, 3) as i:
                own.enter(i, 2)
                for j in range(2):
                    dve.wait_ge(act_took, i * 4 + (ACT_RKV + 2 * j + 2))
                    own.link(dve.tensor_tensor(SH, RAW[:, :, 0:L], RAW[:, :, 1:L + 1], ALU.subtract))
                    for f in range(4):
                        last = dve.scalar_tensor_tensor(out=RKV[:, ds(8 * i + (4 * j + f), 1), :].rearrange("p o n -> p (o n)"),
                                                        in0=SH[:, f, :], scalar=cols[:, ds(8 * i + (mu0 + 4 * j + f), 1)],
                                                        in1=RAW[:, f, 1:L + 1], op0=ALU.mult, op1=ALU.add)
                    last.then_inc(shifted, 1)
                own.leave(3)
            dve.wait_ge(act_took, ACT_RKV + 14)
            for f, (dst, (_, m)) in enumerate(zip((HW, HA, HG0, HG1), WAG_TILES)):
                own.link(dve.tensor_tensor(SH[0:m, f, :], RAW[0:m, f, 0:L], RAW[0:m, f, 1:L + 1], ALU.subtract))
                ins = dve.scalar_tensor_tensor(out=dst[0:m, :], in0=SH[0:m, f, :], scalar=cols[0:m, mu0 + 24 + f:mu0 + 25 + f],
                                               in1=RAW[0:m, f, 1:L + 1], op0=ALU.mult, op1=ALU.add)
                if f < 3:
                    ins.then_inc(wag_ready, 1)
                else:
                    own.mark(ins)
            dve.wait_ge(act_took, ACT_RKV + 16)
            own.link(dve.memset(KPX, 0.0))
            dve.wait_ge(trig_ready, 1)

            def rotate(dst, src, t, heads, emit=None):
                sn = ang[:, 0, t, :].unsqueeze(1).to_broadcast([P, heads, 32])
                cn = ang[:, 1, t, :].unsqueeze(1).to_broadcast([P, heads, 32])
                tmp = [rope_tmp[:, i, 0:heads * 32].rearrange("p (h n) -> p h n", n=32) for i in range(4)]
                lo, hi = src[:, :, 0:32], src[:, :, 32:64]
                for d, x, y in ((0, lo, cn), (1, hi, sn), (2, hi, cn), (3, lo, sn)):
                    own.mark(dve.tensor_tensor(tmp[d], x, y, ALU.mult))
                own.wait()
                return (dve.tensor_tensor(dst[:, :, 0:32], tmp[0], tmp[1], ALU.subtract),
                        dve.tensor_tensor(dst[:, :, 32:64], tmp[2], tmp[3], ALU.add))

            for t in range(TT):
                x, y = rotate(KPX[:, t, 0:1, 0:ROPE], KPE[:, t:t + 1, :], t, 1)
                own.mark(x)
                own.mark(y)
                own.wait()
                dve.tensor_copy(KPX[:, t, 1, ROPE:2 * ROPE], KPX[:, t, 0, 0:ROPE]).then_inc(kpx_ready, 2)
            dve.wait_ge(c_sq, 4)
            inverse_mean(crstd, cstat, LORA).then_inc(c_var, 1)
            dve.wait_ge(c_rstd, 1)
            for j in range(4):
                dve.tensor_scalar(CQ[:, j, :], CQ[:, j, :], crstd[:, j:j + 1], None, ALU.mult).then_inc(c_normed, 1)
            dve.wait_ge(act_took, ACT_RKV + 28)
            for t in range(TT):
                x, y = rotate(QPR[:, t, :].rearrange("p (h n) -> p h n", n=ROPE),
                              QPE[:, t, :].rearrange("p (h n) -> p h n", n=ROPE), t, HEADS)
                own.mark(x)
                if t == 0:
                    own.mark(y)
                    own.wait()
                else:
                    y.then_inc(qpr_ready, 1)

            def emit2(h, t, o, inv):
                return dve.tensor_scalar(YM[:, t, h * DH:(h + 1) * DH], o, inv, None, ALU.mult)

            attention_dve(dve, own, HEADS, 2 * HEADS, lambda h: causal_mask, lambda h: 1.0, emit2, S2)
            own.link(dve.memset(small[:, 507:508], 0.0))
            dve.memset(small[:, 506:507], 0.0).then_inc(masks_free, 1)
            R_, K_, V_ = RKV[:, 0:8], RKV[:, 8:16], RKV[:, 16:24]
            fl = lambda v: v.rearrange("p f n -> p (f n)")
            own.link(dve.tensor_scalar(one_ka, col("rwkv_k_a_2", 0, 8), -1.0, 1.0, ALU.mult, ALU.add))
            dve.wait_ge(xT_taken, 2 * 35)
            for f in range(8):
                own.mark(dve.tensor_scalar(KKn[:, f, :], K_[:, f, :], col("rwkv_k_k_2", f), None, ALU.mult))
            own.wait()
            dve.tensor_tensor(fl(sqk), fl(KKn), fl(KKn), ALU.mult).then_inc(kk_sq, 1)
            dve.wait_ge(rw_small_took, 8)
            dve.wait_ge(rw_masks, 1)
            own.link(dve.tensor_scalar(fl(Lw), fl(Lw), -float(np.exp(-0.5)), None, ALU.mult))
            for f in range(8):
                own.mark(dve.tensor_tensor_scan(El[:, f, :], chunk_start, Lw[:, f, :], 0.0, ALU.mult, ALU.add))
            own.wait()
            e4 = fl(El).rearrange("p (g t) -> p g t", t=C)
            own.mark(dve.tensor_copy(small[:, 264:296], e4[:, :, C - 1]))
            own.mark(dve.tensor_copy(small[:, 296:328], e4[:, :, C // 2 - 1]))
            own.wait()
            own.mark(dve.tensor_tensor(e4, e4, small[:, 296:328].unsqueeze(2).to_broadcast([P, 32, C]), ALU.subtract))
            own.link(dve.tensor_tensor(fac, end_s, mid_s, ALU.subtract))
            own.link(dve.tensor_tensor(fac[:, :, 0:NCH - 1], fac[:, :, 0:NCH - 1], mid_s[:, :, 1:NCH], ALU.add))
            dve.tensor_copy(small[:, 505:506], small[:, 328:329]).then_inc(fac_raw, 1)
            dve.wait_ge(rw_small_took, 16)
            for f in range(8):
                own.mark(dve.tensor_scalar(kfac[:, f, :], Bv[:, f, :], col("rwkv_k_a_2", f), one_ka[:, f:f + 1],
                                           ALU.mult, ALU.add))
            own.wait()
            own.mark(dve.tensor_tensor(fl(K_), fl(K_), fl(kfac), ALU.mult))
            for g in range(4):
                dve.wait_ge(kk_sum, g + 1)
                own.mark(dve.tensor_scalar(fl(sqk[:, 2 * g:2 * g + 2]), BANK[g][:, :], 1e-24, None, ALU.max))
            own.wait()
            dve.reciprocal(fl(sqk), fl(sqk)).then_inc(kk_var, 1)
            dve.wait_ge(kk_rstd, 1)
            own.link(dve.tensor_tensor(fl(KKn), fl(KKn), fl(sqk), ALU.mult))
            own.link(dve.tensor_tensor(fl(Bv), fl(Bv), fl(KKn), ALU.mult))
            own.link(dve.tensor_scalar(fl(KKn), fl(KKn), -1.0, None, ALU.mult))
            for v in (a_bd, b_bd, k_bd, r_bd, v_bd, y_bd):
                own.mark(dve.memset(v, 0.0))
            own.wait()
            dve.wait_ge(fac_ready, 1)
            dve.memset(small[:, 504:505], 0.0).then_inc(prep_ready, 1)
            P_ = Steps(pe_step, pe_names)
            A_, D_ = Steps(act_step, act_names), Steps(dve_step, dve_names)
            four = lambda m: m.unsqueeze(1).to_broadcast([P, 4, P])
            bank4 = lambda b, w: BANK[b][:, 0:4 * w].rearrange("p (q n) -> p q n", q=4)
            with dve.Fori(0, 2) as g:
                own.enter(g, 1)
                own.mark(dve.memset(ST, 0.0))
                own.leave(2)
                with dve.Fori(0, NCH) as c:
                    it = g * NCH + c

                    def part(v, h=None):
                        v = v[:, ds(4 * g, 4), ds(c * C, C)]
                        return v if h is None else v[h * N:(h + 1) * N]

                    D_.mark(dve.tensor_tensor(DEL, part(El), part(Lw), ALU.subtract), "DEL")
                    for nm, dst, src, fct, ready in (("v", v_bd, V_, None, None), ("b", b_bd, Bv, EN, "EN"),
                                                     ("k", k_bd, K_, EN, "EN"), ("r", r_bd, R_, EX, "EX"),
                                                     ("a", a_bd, KKn, EXC, "EXC")):
                        if ready:
                            A_.wait(dve, ready, it)
                        for h in range(2):
                            o = dst[h * N:(h + 1) * N, :, h * N:(h + 1) * N]
                            x = part(src, h)
                            D_.mark(dve.tensor_copy(o, x) if fct is None else
                                    dve.tensor_tensor(o, x, fct[h * N:(h + 1) * N], ALU.mult), f"{nm}{h}")
                    for nm, dst, bank, m in (("LT", LT, 0, below), ("AkT", AkT, 1, below), ("BrT", BrT, 5, upto_diag),
                                             ("KrT", KrT, 6, upto_diag)):
                        P_.wait(dve, nm, it)
                        D_.mark(dve.tensor_tensor(dst, bank4(bank, P), four(m), ALU.mult), nm)
                    for m in range(LEVELS):
                        P_.wait(dve, f"T{m}", it)
                        D_.mark(dve.tensor_tensor(T2, bank4(7, P), four(level[m]), ALU.mult), f"T{m}")
                        if m == 0:
                            D_.wait(dve, "T0", it)
                            D_.mark(dve.tensor_tensor(Xi, T2, four(ident[:]), ALU.add), "X0")
                            P_.wait(dve, "Z0", it)
                            D_.mark(dve.tensor_tensor(Zi, bank4(1, P), four(ident[:]), ALU.add), "Z0")
                            continue
                        if m < LEVELS - 1:
                            P_.wait(dve, f"X{m}", it)
                            D_.mark(dve.tensor_tensor(Xi, Xi, bank4(0, P), ALU.add), f"X{m}")
                        P_.wait(dve, f"Z{m}", it)
                        D_.mark(dve.tensor_tensor(Zi, Zi, bank4(1, P), ALU.add), f"Z{m}")
                    b4 = lambda v: v.unsqueeze(2).to_broadcast([P, 4, N])
                    P_.wait(dve, "S", it)
                    D_.mark(dve.tensor_tensor(ST, ST, bank4(5, N), ALU.add), "Ssum")
                    D_.mark(dve.tensor_reduce(gsum, bank4(3, N), AX_X, ALU.add), "gs")
                    D_.wait(dve, "gs", it)
                    D_.mark(dve.scalar_tensor_tensor(out=YC, in0=b4(gsum), scalar=-1.0 / N, in1=bank4(3, N),
                                                     op0=ALU.mult, op1=ALU.add), "yc")
                    D_.wait(dve, "yc", it)
                    D_.mark(dve.tensor_tensor(YQ, YC, YC, ALU.mult), "yq")
                    D_.wait(dve, "yq", it)
                    D_.mark(dve.tensor_reduce(gvar, YQ, AX_X, ALU.add), "gv")
                    D_.wait(dve, "gv", it)
                    D_.mark(dve.tensor_scalar(gvar, gvar, 1.0 / N, GN_EPS, ALU.mult, ALU.add), "ge")
                    D_.wait(dve, "ge", it)
                    D_.mark(dve.reciprocal(gvar, gvar), "gi")
                    A_.wait(dve, "sq", it)
                    for h in range(2):
                        D_.mark(dve.tensor_tensor(y_bd[h * N:(h + 1) * N, :, h * N:(h + 1) * N], YC[h * N:(h + 1) * N],
                                                  b4(gvar)[h * N:(h + 1) * N], ALU.mult), f"y{h}")
                    D_.mark(dve.tensor_tensor(ST, ST, fac[:, ds(4 * g, 4), ds(c, 1)].to_broadcast([P, 4, N]), ALU.mult), "S")
                    D_.wait(dve, "S", it)
            A_.wait(dve, "YT", 7)
            D_.wait(dve, "S", 7)
            P_.wait(dve, "YT", 7)
            own.link(dve.tensor_tensor(fl(RK2), fl(R_), fl(K_), ALU.mult))
            for f in range(8):
                ins = dve.tensor_scalar(RK2[:, f, :], RK2[:, f, :], col("rwkv_r_k_2", f), None, ALU.mult)
            ins.then_inc(rk_ready, 1)
            for f in range(8):
                own.mark(dve.tensor_scalar(HT[:, f, :], HT[:, f, :], col("rwkv_gn_w_2", f), col("rwkv_gn_b_2", f),
                                           ALU.mult, ALU.add))
            for g in range(4):
                dve.wait_ge(bonus_ready, g + 1)
                dve.tensor_tensor(fl(BV[:, 2 * g:2 * g + 2]), BANK[g][:, :], fl(V_[:, 2 * g:2 * g + 2]),
                                  ALU.mult).then_inc(bonus_took, 1)
            dve.wait_ge(bonus_took, 4)
            own.wait()
            own.link(dve.tensor_tensor(fl(HT[:, 0:8, :]), fl(HT[:, 0:8, :]), fl(BV), ALU.add))
            for g in range(4):
                if g < 3:
                    dve.wait_ge(g_ready, g + 1)
                else:
                    dve.wait_ge(piece_done, n_wo2)
                dve.tensor_tensor(fl(HT[:, 2 * g:2 * g + 2, :]), fl(HT[:, 2 * g:2 * g + 2, :]), BANK[g][:, :],
                                  ALU.mult).then_inc(g_took, 2)
            for c in range(4):
                dve.wait_ge(piece_done, n_wo2 + 2 * c + 2)
                for t in range(TT):
                    xc = X[:, t, c * CH:(c + 1) * CH]
                    dve.tensor_tensor(xc, xc, BANK[2 * (c % 2) + t][:, :], ALU.add).then_inc(x_updated, 1)
            norm_dve(2)
            scale_x(2, XN3)
            own.link(dve.memset(RAWF[:, :, 0:2], 0.0))
            dve.memset(small[:, 503:504], 0.0).then_inc(conv_ready, 1)
            dve.memset(small[:, 502:503], 0.0).then_inc(up_taken, 1)
            tap = [VEC[f"conv{t}"][0] * P + VEC[f"conv{t}"][1] for t in range(3)]
            cb = VEC["ffn_conv_b_2"][0] * P + VEC["ffn_conv_b_2"][1]
            with dve.Fori(0, FF // CH) as i:
                own.enter(i, 8)
                dve.wait_ge(act_took, i * 2 + (ACT_RKV + 38))
                dve.wait_ge(up_taken, i * 2 + 1)
                for f in range(4):
                    w = lambda t: cols[:, ds(4 * i + (tap[t] + f), 1)]
                    own.mark(dve.tensor_scalar(CV[:, f, :], RAWF[:, f, 2:L + 2], w(2), cols[:, ds(4 * i + (cb + f), 1)],
                                               ALU.mult, ALU.add))
                own.wait()
                for f in range(4):
                    w = lambda t: cols[:, ds(4 * i + (tap[t] + f), 1)]
                    own.mark(dve.scalar_tensor_tensor(out=CV[:, f, :], in0=RAWF[:, f, 1:L + 1], scalar=w(1), in1=CV[:, f, :],
                                                      op0=ALU.mult, op1=ALU.add))
                own.wait()
                for f in range(4):
                    w = lambda t: cols[:, ds(4 * i + (tap[t] + f), 1)]
                    last = dve.scalar_tensor_tensor(out=CV[:, f, :], in0=RAWF[:, f, 0:L], scalar=w(0), in1=CV[:, f, :],
                                                    op0=ALU.mult, op1=ALU.add)
                last.then_inc(conv_ready, 1)
                dve.wait_ge(gate_act, i + 1)
                dve.wait_ge(piece_done, i * 4 + (n_gu + 4))
                for t in range(TT):
                    dve.tensor_tensor(AC[:, ds(4 * i + 2 * t, 2), :], CV[:, 2 * t:2 * t + 2, :],
                                      BANK[2 + t][:, :].rearrange("p (f n) -> p f n", f=2), ALU.mult).then_inc(up_taken, 1)
                own.leave(FF // CH)
            with dve.Fori(0, 2) as i:
                for j in range(2):
                    dve.wait_ge(piece_done, i * 12 + (n_dn + 6 * j + 6))
                    for t in range(TT):
                        xc = X[:, t, ds(i * 2 * CH + j * CH, CH)]
                        dve.tensor_tensor(xc, xc, BANK[2 * j + t][:, :], ALU.add).then_inc(x_updated, 1)
            norm_dve(3)
            dve.wait_ge(rstd_ready, 4)
            dve.wait_ge(fg_in, 16)
            for t in range(TT):
                dve.scalar_tensor_tensor(out=XN3[:, t, :], in0=X[:, t, :], scalar=rstd[:, t:t + 1], in1=fg_row,
                                         op0=ALU.mult, op1=ALU.mult).then_inc(fin_ready, 1)



_INS = ["x", "c", "w_ada", "b_ada", "g_norm", "w_in", "q_norm_a", "k_norm_a", "k_norm_idx", "q_norm_b",
        "k_norm_b", "w_out", "positions_2", "attn_norm_g_2", "w_in_2", "rwkv_mu_2", "rwkv_w0_2", "rwkv_w2_2",
        "rwkv_a0_2", "rwkv_a2_2", "rwkv_g2_2", "rwkv_k_k_2", "rwkv_k_a_2", "rwkv_r_k_2", "rwkv_gn_w_2",
        "rwkv_gn_b_2", "mla_q_norm_g_2", "mla_w_uq_2", "mla_kv_norm_g_2", "mla_w_ukv_2", "w_out_2",
        "ffn_norm_g_2", "ffn_w_gate_2", "ffn_w_up_2", "ffn_conv_w_2", "ffn_conv_b_2", "ffn_w_down_2",
        "final_norm_g_2"]
_OUT = (1, L, D)


def kernel(**inputs):
    import concourse.bacc as bacc
    from concourse.bass_utils import run_bass_kernel_spmd

    nc = bacc.Bacc("TRN2", target_bir_lowering=False, num_devices=1)
    arrays, args = {}, {}
    for name in _INS:
        v = np.ascontiguousarray(inputs[name])
        arrays[f"in_{name}"] = v
        args[name] = nc.dram_tensor(f"in_{name}", v.shape, mybir.dt.from_np(v.dtype), kind="ExternalInput").ap()
    out = nc.dram_tensor("out", _OUT, F32, kind="ExternalOutput").ap()
    build(nc, args, out)
    return run_bass_kernel_spmd(nc, [arrays], core_ids=[0]).results[0]["out"]
```

```python
from contextlib import ExitStack

import numpy as np
import concourse.bass as bass
from concourse import mybir

F32 = mybir.dt.float32
F32R = mybir.dt.float32r
I32 = mybir.dt.int32
ALU = mybir.AluOpType
ACT = mybir.ActivationFunctionType
AX_X = mybir.AxisListType.X
ds = bass.ds

P = 128
L = 256
TT = L // P
D = 2048
KT = D // P
DH = 128
HEADS = 8
D_A = HEADS * DH
IDX_HEADS, IDX_DIM, TOPK = 16, 64, 64
IDX_COL = 4 * D_A
KW_COL = IDX_COL + IDX_HEADS * IDX_DIM
KW = IDX_DIM + IDX_HEADS
B_COL = KW_COL + KW
EPS = 1e-6
NEG = -1e30
SPAN = P + L

NSLOT = 4
PK = 4
PIECES = KT // PK
CH = 512

RW = 1024
NP_ = 8
N = 64
C = 64
NCH = L // C
WAG_COL = 3 * RW
WAG = 64 + 64 + 160
CQ_COL = WAG_COL + WAG
KPE_COL = CQ_COL + 1024
LORA = 512
ROPE = 64
MLA_W = HEADS * (DH + ROPE)
FF = 5632
FT = FF // P
GN_EPS = 64e-5

VEC = {}


def _place():
    groups = [
        [("c", 16), ("b_ada", 48), ("g_norm", 16), ("attn_norm_g_2", 16), ("ffn_norm_g_2", 16),
         ("q_norm_a", 1), ("k_norm_a", 1), ("q_norm_b", 1), ("k_norm_b", 1),
         ("mla_q_norm_g_2", 4), ("mla_kv_norm_g_2", 4)],
        [("rwkv_mu_2", 27), ("rwkv_w0_2", 8), ("rwkv_a0_2", 8), ("rwkv_k_k_2", 8), ("rwkv_k_a_2", 8),
         ("rwkv_r_k_2", 8), ("rwkv_gn_w_2", 8), ("rwkv_gn_b_2", 8), ("ffn_conv_b_2", 44)],
        [("conv0", 44), ("conv1", 44)],
        [("conv2", 44)],
    ]
    for g, names in enumerate(groups):
        row = 0
        for name, rows in names:
            VEC[name] = (g, row, rows)
            row += rows
    return [sum(r for _, r in names) for names in groups]


GROUP_ROWS = _place()


class Chain:

    def __init__(self, eng, sem):
        self.eng, self.sem, self.n, self.i, self.per = eng, sem, 0, None, 0

    def value(self):
        return self.n if self.i is None else self.i * self.per + self.n

    def mark(self, ins):
        ins.then_inc(self.sem, 1)
        self.n += 1
        return ins

    def wait(self):
        self.eng.wait_ge(self.sem, self.value())

    def link(self, ins):
        self.mark(ins)
        self.wait()

    def enter(self, i, per):
        self.i, self.per, self.start = i, per, self.n

    def leave(self, times):
        assert self.n - self.start == self.per, (self.n - self.start, self.per)
        self.n, self.i = self.start + self.per * times, None


class Steps:

    def __init__(self, sem, names):
        self.sem, self.names, self.at = sem, names, 0

    def mark(self, ins, name):
        assert self.names[self.at % len(self.names)] == name, (self.names[self.at % len(self.names)], name)
        self.at += 1
        ins.then_inc(self.sem, 1)

    def wait(self, eng, name, step):
        eng.wait_ge(self.sem, step * len(self.names) + (self.names.index(name) + 1))


def build(nc, a, out):
    ctx = ExitStack()
    with ctx:
        def sb(name, *shape, dt=F32):
            return ctx.enter_context(nc.sbuf_tensor(name, [P, *shape], dt))

        def sem(name):
            return ctx.enter_context(nc.semaphore(name))

        BANK = [ctx.enter_context(nc.psum_tensor(f"bank{i}", [P, 512], F32)) for i in range(8)]

        base = (nc.sbuf_base + 31) // 32 * 32
        ctx.enter_context(nc.sbuf_tensor("slab", [P, 52688], F32))

        def sb(name, off, *shape, dt=F32):
            return nc.alloc_sbuf_tensor_at(name, [P, *shape], dt, offset=base + 4 * off)

        X = sb("X", 0, TT, D)
        WR = sb("WR", 4096, NSLOT, PK * CH)
        WL = sb("WL", 4096, NSLOT, PK * CH, dt=F32R)
        WH = sb("WH", 12288, 2, PK * CH, dt=F32R)
        HH = sb("HH", 16384, KT, L, dt=F32R)
        HL = sb("HL", 20480, KT, L, dt=F32R)
        CSH = sb("CSH", 16384, KT, P, dt=F32R)
        CSL = sb("CSL", 18432, KT, P, dt=F32R)
        bgate_row = sb("bgate_row", 20480, D)[:, :]
        YR = sb("YR", 20480, 8, L)
        cols = sb("cols", 24576, 4 * P)
        ident = sb("ident", 25088, P)
        ones = sb("ones", 25216, P)
        small = sb("small", 25344, 512)
        masks = sb("masks", 25856, 1216)
        causal_dist = masks[:, 0:SPAN]
        causal_mask = masks[:, SPAN:2 * SPAN]
        bias_a = masks[:, 2 * SPAN:3 * SPAN]
        slope = sb("slope", 27072, 2 * HEADS)
        ARENA = 25600
        arena = sb("arena", 27088, ARENA)

        used = [0]

        def at(off, *shape):
            n = int(np.prod(shape))
            assert off + n <= ARENA, (off, n)
            v = arena[:, off:off + n]
            used[0] = off + n
            if len(shape) == 1:
                return v
            names = "abcd"[:len(shape)]
            return v.rearrange(f"p ({' '.join(names)}) -> p {' '.join(names)}",
                               **{m: s for m, s in zip(names[1:], shape[1:])})

        def col(name, j=0, n=1):
            g, row, _ = VEC[name]
            return cols[:, g * P + row + j:g * P + row + j + n]

        mod = small[:, 0:48]
        cs = small[:, 48:64]
        gs = small[:, 64:80]
        qgain = small[:, 80:84]
        ss = small[:, 84:86]
        rstd = small[:, 86:88]
        sgc = small[:, 88:104]
        nmax = small[:, 104:104 + 32]
        rowsum = small[:, 136:136 + 32]
        rsum_inv = small[:, 168:168 + 32]
        hss = small[:, 200:216]
        hrstd = small[:, 216:232]
        top8 = small[:, 232:248].rearrange("p (t e) -> p t e", t=TT)
        cnt = small[:, 248:250]
        need = small[:, 250:252]
        kss = small[:, 252:254]
        krstd = small[:, 254:256]

        V1 = at(0, 2, TT, D_A)
        Z1 = at(4096, 2, TT, D_A)
        QT = at(8192, 2, HEADS, L)
        KTT = at(12288, 2, HEADS, L)
        XN = at(8192, TT, D)
        rows = at(16384, 4, P)
        stage = at(16896, 2, TT, CH)
        square = at(18944, TT, CH)
        QI = at(19968, 8, L)
        S_sb = at(16896, 2, SPAN)
        Pr = at(17664, 2, SPAN)
        PTs = at(18432, 2, SPAN)
        KI = at(22016, TT, KW)
        KIX = at(22176, TT, 2, P)
        KB = at(22688, 2, L)
        relu = at(23200, 2, CH)
        score = at(24224, SPAN)
        work = at(24608, SPAN)
        kin_g = at(24992, IDX_DIM)
        MROW = at(0, 2 * D)[0:1, :]
        gate_row = at(19968, D)
        wo_tmp = at(10752, 2, CH)
        hf1 = at(16896, 2, 2, L)

        RKV = at(0, 24, L)
        HWA, HG0, HG1 = (at(6144 + 256 * i, L) for i in range(3))
        RAW = at(7168, 4, L + 1)
        SH = at(8196, 4, L)
        S2, Pr2, PT2 = at(7168, 2, SPAN), at(7936, 2, SPAN), at(8704, 2, SPAN)
        CQ = at(9472, 4, LORA)
        YM = at(9472, TT, 1024)
        KPE = at(11520, TT, ROPE)
        CT = at(11648, 8, L)
        QN = at(13696, HEADS, L)
        KN = at(15744, HEADS, L)
        VM = at(17792, TT, 1024)
        QPE = at(19840, TT, 512)
        QPR = at(20864, TT, 512)
        QPT = at(21888, 4, L)
        KPX = at(22912, TT, 2, P)
        KPT = at(23424, 2, L)
        ang = at(23936, 2, TT, 32)
        turns = at(24064, 2, TT, 32)
        inv_freq = at(24192, 32)
        rope_tmp = at(24224, 4, 256)
        pos_i = arena[:, 25248:25250].bitcast(I32)
        pos = at(25250, 2)
        XN2 = at(13696, TT, D)
        hf2 = at(17792, 2, 2, L)
        hf3 = at(20864, 2, 2, L)
        cstat = small[:, 256:260]
        crstd = small[:, 260:264]

        Lw = at(7168, 8, L)
        El = at(9216, 8, L)
        Bv = at(11264, 8, L)
        KKn = at(13312, 8, L)
        sqk = at(15360, 8, L)
        chunk_start = at(17408, L)
        kfac = at(17664, 8, L)
        w4 = [at(15360 + 512 * i, 4, P) for i in range(15)]
        a_bd, b_bd, k_bd, r_bd, v_bd, LT, AkT, BrT, KrT, b_tok, k_tok, Xi, Zi, T2, y_bd = w4
        n4 = [at(23040 + 256 * i, 4, N) for i in range(10)]
        P1, Us, Vp, ST, YC, YQ, EX, EN, EXC, DEL = n4
        level = [masks[:, P * i:P * (i + 1)] for i in range(6)]
        below, upto_diag = masks[:, 768:896], masks[:, 896:1024]
        I2 = masks[:, 1024:1088]
        head_ones = masks[:, 1088:1216]
        end_s = small[:, 264:296].rearrange("p (f c) -> p f c", c=NCH)
        mid_s = small[:, 296:328].rearrange("p (f c) -> p f c", c=NCH)
        fac = small[:, 328:360].rearrange("p (f c) -> p f c", c=NCH)
        one_ka = small[:, 360:368]
        gsum, gvar = small[:, 368:372], small[:, 372:376]
        RK2 = at(15360, 8, L)
        BV = at(17408, 8, L)

        AC = at(0, FT, L)
        RAWF = at(11264, 4, L + 2)
        CV = at(12296, 4, L)
        XN3 = at(16384, TT, D)
        fg_row = at(20480, D)
        hf4 = at(0, 2, 2, L)
        AH = sb("AH", 27088 + 11264, 2, PK, L, dt=F32R)
        AL = sb("AL", 27088 + 13312, 2, PK, L, dt=F32R)

        piece_in = [sem(f"piece_in{s}") for s in range(NSLOT)]
        piece_done = sem("piece_done")
        half_done = sem("half_done")
        act_took, dve_took = sem("act_took"), sem("dve_took")
        x_in, params_in, misc_in = sem("x_in"), sem("params_in"), sem("misc_in")
        rows_clear, consts_set = sem("rows_clear"), sem("consts_set")
        pool_chain, dve_chain_s, act_chain_s = sem("pool_chain"), sem("dve_chain"), sem("act_chain")
        colsT_ready, cols_ready = sem("colsT_ready"), sem("cols_ready")
        cs_ready = sem("cs_ready")
        mod_ready = sem("mod_ready")
        ssq_ready, var_ready, rstd_ready, xn_ready = sem("ssq_ready"), sem("var_ready"), sem("rstd_ready"), sem("xn_ready")
        xT_ready, xT_taken = sem("xT_ready"), sem("xT_taken")
        ki_var, ki_rstd, kix_ready, kixT_ready, kb_ready = map(sem, ["ki_var", "ki_rstd", "kix_ready", "kixT_ready", "kb_ready"])
        idx_ready, relu_ready, relu_used = sem("idx_ready"), sem("relu_ready"), sem("relu_used")
        chunk_out, head_var, head_rstd, head_normed, headT_ready, headT_taken = map(
            sem, ["chunk_out", "head_var", "head_rstd", "head_normed", "headT_ready", "headT_taken"])
        scores_ready, scores_biased, max_ready, probs_ready = map(
            sem, ["scores_ready", "scores_biased", "max_ready", "probs_ready"])
        probsT_ready, probsT_taken, out_ready, out_taken = map(
            sem, ["probsT_ready", "probsT_taken", "out_ready", "out_taken"])
        row_took, modT_ready, cs_wide_ready, bgate_in = map(sem, ["row_took", "modT_ready", "cs_wide_ready", "bgate_in"])
        x_updated = sem("x_updated")
        stored = sem("stored")
        hi_ready, lo_ready, ht_ready, a_ready, cs_split, ada_row = map(
            sem, ["hi_ready", "lo_ready", "ht_ready", "a_ready", "cs_split", "ada_row"])
        shifted, raw_clear, wag_ready = sem("shifted"), sem("raw_clear"), sem("wag_ready")
        pos_in, fg_in = sem("pos_in"), sem("fg_in")
        ang_ready, trig_ready = sem("ang_ready"), sem("trig_ready")
        c_sq, c_var, c_rstd, c_normed, kpx_ready, qpr_ready = map(
            sem, ["c_sq", "c_var", "c_rstd", "c_normed", "kpx_ready", "qpr_ready"])
        lora_ready = sem("lora_ready")
        masks_free, rw_masks, rw_mid = sem("masks_free"), sem("rw_masks"), sem("rw_mid")
        rw_small, rw_small_took, kk_sq, kk_sum, kk_var, kk_rstd = map(
            sem, ["rw_small", "rw_small_took", "kk_sq", "kk_sum", "kk_var", "kk_rstd"])
        prep_ready, fac_raw, fac_ready = sem("prep_ready"), sem("fac_raw"), sem("fac_ready")
        pe_step, act_step, dve_step = sem("pe_step"), sem("act_step"), sem("dve_step")
        rk_ready, bonus_ready, bonus_took, g_ready, g_took = map(
            sem, ["rk_ready", "bonus_ready", "bonus_took", "g_ready", "g_took"])
        conv_ready, gate_act, up_taken = sem("conv_ready"), sem("gate_act"), sem("up_taken")
        fin_ready = sem("fin_ready")

        def attention_pe(pe, heads, base, qk, v, Pr, PTs):
            def scores(h):
                if h >= 2:
                    pe.wait_ge(scores_biased, base + h - 1)
                for t in range(TT):
                    o = BANK[4 + h % 2][:, t * P:t * P + (t + 1) * P]
                    parts = qk(h, t)
                    for n, (q, k) in enumerate(parts):
                        last = pe.matmul(o, q, k, start=(n == 0), stop=(n == len(parts) - 1))
                last.then_inc(scores_ready, 1)

            scores(0)
            scores(1)
            for h in range(heads):
                pe.wait_ge(probs_ready, 2 * (base + h + 1))
                if h >= 2:
                    pe.wait_ge(probsT_taken, base + h - 1)
                for n, c0 in enumerate((0, P, 2 * P)):
                    last = pe.transpose(BANK[2 + h % 2][:, n * P:(n + 1) * P], Pr[:, h % 2, c0:c0 + P], ident[:])
                last.then_inc(probsT_ready, 1)
                if h + 2 < heads:
                    scores(h + 2)
                pe.wait_ge(probsT_taken, base + h + 1)
                if h >= 2:
                    pe.wait_ge(out_taken, 2 * (base + h - 1))
                o = BANK[6 + h % 2]
                pt = PTs[:, h % 2]
                pe.matmul(o[:, 0:DH], pt[:, 0:P], v(h, 0), start=True, stop=True)
                pe.matmul(o[:, DH:2 * DH], pt[:, P:2 * P], v(h, 0), start=True, stop=False)
                pe.matmul(o[:, DH:2 * DH], pt[:, 2 * P:3 * P], v(h, 1), start=False, stop=True) \
                    .then_inc(out_ready, 1)

        def attention_act(act, heads, base, S_sb, Pr, PTs):
            def exps(h):
                act.wait_ge(max_ready, 2 * (base + h + 1))
                if base + h >= 2:
                    act.wait_ge(probsT_ready, base + h - 1)
                for t, (c0, w) in enumerate(((0, P), (P, L))):
                    act.activation(Pr[:, h % 2, c0:c0 + w], S_sb[:, h % 2, c0:c0 + w], ACT.Exp,
                                   bias=nmax[:, 2 * h + t:2 * h + t + 1],
                                   accum_out=rowsum[:, 2 * h + t:2 * h + t + 1]).then_inc(probs_ready, 1)

            def turn(h):
                act.wait_ge(probsT_ready, base + h + 1)
                if base + h >= 2:
                    act.wait_ge(out_ready, base + h - 1)
                act.activation(PTs[:, h % 2, :], BANK[2 + h % 2][:, 0:SPAN], ACT.Copy).then_inc(probsT_taken, 1)

            for h in range(heads):
                exps(h)
                if h >= 1:
                    turn(h - 1)
            turn(heads - 1)

        def attention_dve(dve, own, heads, base, bias, coef, emit, S_sb):
            def maxima(h):
                dve.wait_ge(scores_ready, base + h + 1)
                if base + h >= 2:
                    dve.wait_ge(probs_ready, 2 * (base + h - 1))
                dve.scalar_tensor_tensor(out=S_sb[:, h % 2, :], in0=bias(h), scalar=coef(h),
                                         in1=BANK[4 + h % 2][:, 0:SPAN], op0=ALU.mult,
                                         op1=ALU.add).then_inc(scores_biased, 1)
                dve.wait_ge(scores_biased, base + h + 1)
                for t, (c0, w) in enumerate(((0, P), (P, L))):
                    dve.tensor_reduce(nmax[:, 2 * h + t:2 * h + t + 1], S_sb[:, h % 2, c0:c0 + w], AX_X, ALU.max,
                                      negate=True).then_inc(max_ready, 1)

            def finish(h):
                dve.wait_ge(probs_ready, 2 * (base + h + 1))
                own.link(dve.reciprocal(rsum_inv[:, 2 * h:2 * h + 2], rowsum[:, 2 * h:2 * h + 2]))
                dve.wait_ge(out_ready, base + h + 1)
                for t in range(TT):
                    emit(h, t, BANK[6 + h % 2][:, t * DH:(t + 1) * DH],
                         rsum_inv[:, 2 * h + t:2 * h + t + 1]).then_inc(out_taken, 1)

            for h in range(heads):
                maxima(h)
                if h >= 1:
                    finish(h - 1)
            finish(heads - 1)

        PARAMS = [(n, n) for n in VEC if not n.startswith("conv")]
        PARAM_DMAS = len(PARAMS) + 1 + 3

        block = ctx.enter_context(nc.Block())

        ACT_GATE, ACT_RKV = 38, 42
        NADA = 2 * D // CH
        n_ada = 0
        n_kw = n_ada + PIECES * NADA
        n_qi = n_kw + PIECES
        n_br = n_qi + 2 * PIECES
        n_gate = n_br + 16 * PIECES
        n_wo = n_gate + 4 * PIECES
        n_rkv = n_wo + 4 * PIECES
        n_wag = n_rkv + 6 * PIECES
        n_kpe = n_wag + PIECES
        n_c = n_kpe + PIECES
        n_uq = n_c + 2 * PIECES
        n_ukv = n_uq + 4
        n_w2 = n_ukv + 4
        n_wo2 = n_w2 + 4
        n_gu = n_wo2 + 4 * PIECES
        n_dn = n_gu + 2 * (FF // CH) * PIECES
        UNSPLIT = n_wo2 - n_uq

        def width_of(n):
            if n_kw <= n < n_kw + PIECES:
                return KW
            if n_wag <= n < n_wag + PIECES:
                return 3 * P
            return ROPE if n_kpe <= n < n_kpe + PIECES else CH

        def nth(n):
            return n if n < n_wo2 else n - UNSPLIT

        LEVELS = 6
        inv = []
        for m in range(LEVELS):
            inv += [f"T{m}"] + ([f"X{m}"] if 0 < m < LEVELS - 1 else []) + [f"Z{m}"]
        pe_names = ["LT", "AkT", "btok", "ktok", "Vp", "BrT", "KrT"] + inv + ["P1", "U", "Y", "S", "YT"]
        act_names = ["EX", "EN", "EXC", "btok", "ktok", "Vp", "P1", "U", "sq", "YT"]
        dve_names = (["DEL"] + [f"{x}{h}" for x in "vbkra" for h in range(2)] + ["LT", "AkT", "BrT", "KrT"]
                     + [f"T{m}" if k == "T" else f"{k}{m}" for m in range(LEVELS)
                        for k in (["T"] + (["X"] if m < LEVELS - 1 else []) + ["Z"])]
                     + ["Ssum", "gs", "yc", "yq", "gv", "ge", "gi", "y0", "y1", "S"])

        def view(tensor, at_slot, width, k=PK):
            return tensor[:, at_slot, :].rearrange("p (k n) -> p k n", k=k)[:, :, 0:width]

        def half(tensor, at_slot, s, width):
            return view(tensor, at_slot, width)[:, s * PK // 2:(s + 1) * PK // 2, :]

        @block.sync
        def _(sp):
            def load(n, src, width, k=PK, shift=0):
                if n >= NSLOT or not isinstance(shift, int):
                    sp.wait_ge(piece_done, shift + (n - NSLOT + 1))
                sp.dma_start(view(WR, n % NSLOT, width, k), src).then_inc(piece_in[n % NSLOT], 16)

            def chunk(n, w, c0, width, shift=0):
                for q in range(PIECES):
                    src = w[q * PK * P:(q + 1) * PK * P, ds(c0, width)]
                    load(n + q, src.rearrange("(k p) n -> p k n", p=P), width, shift=shift)

            w_ada, w_in, w_out = a["w_ada"][0], a["w_in"][0], a["w_out"][0]
            chunk(n_ada, w_ada, 0, CH)
            with sp.Fori(1, NADA) as i:
                chunk(n_ada, w_ada, i * CH, CH, shift=i * PIECES)
            chunk(n_kw, w_in, KW_COL, KW)
            for j in range(2):
                chunk(n_qi + PIECES * j, w_in, IDX_COL + j * CH, CH)
            with sp.Fori(0, 2) as b, sp.Fori(0, 8) as j:
                chunk(n_br, w_in, b * B_COL + j * CH, CH, shift=b * (8 * PIECES) + j * PIECES)
            with sp.Fori(0, 4) as i:
                chunk(n_gate, w_ada, i * CH + 2 * D, CH, shift=i * PIECES)
            with sp.Fori(0, 4) as i:
                chunk(n_wo, w_out, i * CH, CH, shift=i * PIECES)
            w_in2, w_uq, w_ukv = a["w_in_2"][0], a["mla_w_uq_2"][0], a["mla_w_ukv_2"][0]
            with sp.Fori(0, 6) as i:
                chunk(n_rkv, w_in2, i * CH, CH, shift=i * PIECES)
            chunk(n_wag, w_in2, WAG_COL, 3 * P)
            chunk(n_kpe, w_in2, KPE_COL, ROPE)
            for j in range(2):
                chunk(n_c + PIECES * j, w_in2, CQ_COL + j * CH, CH)
            for n, w, width in ((n_uq, w_uq, 2 * (DH + ROPE)), (n_ukv, w_ukv, 4 * DH)):
                for j in range(4):
                    load(n + j, w[:, j * width:(j + 1) * width].rearrange("(k p) n -> p k n", p=P), width)
            for j, (w, p0, r0, r) in enumerate([("rwkv_w2_2", 0, 0, 64), ("rwkv_a2_2", 64, 0, 64),
                                                ("rwkv_g2_2", 0, 0, P), ("rwkv_g2_2", 0, P, 32)]):
                n = n_w2 + j
                sp.wait_ge(piece_done, n - NSLOT + 1)
                sp.dma_start(WR[p0:p0 + r, n % NSLOT, 0:RW], a[w][0, r0:r0 + r, :]).then_inc(piece_in[n % NSLOT], 16)
            with sp.Fori(0, 4) as i:
                chunk(n_wo2, a["w_out_2"][0], i * CH, CH, shift=i * PIECES)
            with sp.Fori(0, FF // CH) as i:
                for j, w in enumerate(("ffn_w_gate_2", "ffn_w_up_2")):
                    chunk(n_gu + PIECES * j, a[w][0], i * CH, CH, shift=i * (2 * PIECES))
            wd = a["ffn_w_down_2"][0]
            with sp.Fori(0, FT // PK) as i:
                for c in range(4):
                    src = wd[ds(i * (PK * P), PK * P), c * CH:(c + 1) * CH]
                    load(n_dn + c, src.rearrange("(k p) n -> p k n", p=P), CH, shift=i * PIECES)
            sp.wait_ge(fin_ready, 2)
            for t in range(TT):
                sp.dma_start(out[0, t * P:(t + 1) * P, :], XN3[:, t, :]).then_inc(stored, 16)
            sp.wait_ge(stored, 32)

        @block.gpsimd
        def _(pool):
            own = Chain(pool, pool_chain)
            pool.memset(rows[:, :, :], 0.0).then_inc(rows_clear, 1)
            pool.memset(ones[:], 1.0).then_inc(consts_set, 1)
            own.link(pool.memset(ident[:], 0.0))
            pool.affine_select(out=ident[:], in_=ident[:], compare_op=ALU.not_equal, fill=1.0, base=0,
                               pattern=[[-1, P]], channel_multiplier=1).then_inc(consts_set, 1)
            for t, (c0, w) in enumerate(((0, P), (P, L))):
                own.mark(pool.iota(causal_dist[:, c0:c0 + w], pattern=[[1, w]], base=-t * P,
                                   channel_multiplier=-1, allow_small_or_imprecise_dtypes=True))
            own.link(pool.memset(causal_mask, 0.0))
            for t, (c0, w) in enumerate(((0, P), (P, L))):
                for m in (causal_dist, causal_mask):
                    pool.affine_select(out=m[:, c0:c0 + w], in_=m[:, c0:c0 + w], compare_op=ALU.is_ge,
                                       fill=NEG, base=t * P, pattern=[[-1, w]],
                                       channel_multiplier=1).then_inc(consts_set, 1)
            for h in range(2 * HEADS):
                pool.memset(slope[:, h:h + 1], float(np.float32(2.0 ** (-8.0 * (h % HEADS + 1) / HEADS)))) \
                    .then_inc(consts_set, 1)
            pool.memset(KIX[:, :, :, :], 0.0).then_inc(consts_set, 1)

            def low(n, more=0):
                w = width_of(n)
                for s in range(2):
                    pool.wait_ge(hi_ready, more * 2 + (2 * nth(n) + s + 1))
                    pool.tensor_tensor(half(WL, n % NSLOT, s, w), half(WR, n % NSLOT, s, w), half(WH, nth(n) % 2, s, w),
                                       ALU.subtract).then_inc(lo_ready, 1)

            def lows(first, end):
                with pool.Fori(0, (end - first) // PIECES) as i:
                    for q in range(PIECES):
                        low(first + q, i * PIECES)

            lows(n_ada, n_kw)
            for q in range(PIECES):
                low(n_kw + q)
            lows(n_qi, n_wag)
            for q in range(2 * PIECES):
                low(n_wag + q)
            lows(n_c, n_uq)
            pool.wait_ge(masks_free, 1)
            own.link(pool.memset(masks[:, 0:768], 0.0))
            own.link(pool.memset(masks[:, 768:1024], 1.0))
            own.link(pool.memset(I2, 0.0))
            own.link(pool.memset(head_ones, 0.0))
            own.link(pool.memset(chunk_start, 1.0))
            for m in range(LEVELS):
                b = 1 << m
                v = level[m].rearrange("p (j two m) -> p j two m", two=2, m=b)[:, :, 0, :]
                nb = P // (2 * b)
                own.link(pool.memset(v, 1.0))
                own.link(pool.affine_select(out=v, in_=v, compare_op=ALU.is_ge, fill=0.0, base=-b,
                                            pattern=[[-2 * b, nb], [0, b]], channel_multiplier=1))
                own.link(pool.affine_select(out=v, in_=v, compare_op=ALU.is_ge, fill=0.0, base=2 * b - 1,
                                            pattern=[[2 * b, nb], [0, b]], channel_multiplier=-1))
            own.link(pool.affine_select(out=below, in_=below, compare_op=ALU.is_gt, fill=0.0, base=0,
                                        pattern=[[1, P]], channel_multiplier=-1))
            own.link(pool.affine_select(out=upto_diag, in_=upto_diag, compare_op=ALU.is_ge, fill=0.0, base=0,
                                        pattern=[[1, P]], channel_multiplier=-1))
            own.link(pool.affine_select(out=I2, in_=I2, compare_op=ALU.not_equal, fill=1.0, base=0,
                                        pattern=[[-1, N]], channel_multiplier=1))
            own.link(pool.affine_select(out=I2, in_=I2, compare_op=ALU.not_equal, fill=1.0, base=-N,
                                        pattern=[[-1, N]], channel_multiplier=1))
            for h in range(2):
                own.link(pool.memset(head_ones[h * N:(h + 1) * N, h * N:(h + 1) * N], 1.0))
            own.link(pool.memset(chunk_start.rearrange("p (c t) -> p c t", t=C)[:, :, 0], 0.0))
            pool.memset(small[:, 511:512], 0.0).then_inc(rw_masks, 1)
            lows(n_wo2, n_dn + 4 * (FT // PK))
        CONSTS = 2 + 4 + 2 * HEADS + 1

        @block.tensor
        def _(pe):
            def split(n, k, more=0):
                if k % (PK // 2) == 0:
                    pe.wait_ge(lo_ready, more * 2 + (2 * nth(n) + k // (PK // 2) + 1))

            def done(k, last):
                if k == PK // 2 - 1:
                    last.then_inc(half_done, 1)
                elif k == PK - 1:
                    last.then_inc(piece_done, 1)

            def arrived(n):
                pe.wait_ge(piece_in[n % NSLOT], 16 * (n // NSLOT + 1))

            def product(out, stat, mov, start, stop):
                pe.matmul(out, stat[0], mov[0], start=start, stop=False, skip_group_check=True)
                pe.matmul(out, stat[0], mov[1], start=False, stop=False, skip_group_check=True)
                return pe.matmul(out, stat[1], mov[0], start=False, stop=stop, skip_group_check=True)

            def tok_chunk(n, pair, width, more=0):
                for q in range(PIECES):
                    wh, wl = view(WH, nth(n + q) % 2, width), view(WL, (n + q) % NSLOT, width)
                    for k in range(PK):
                        kk = q * PK + k
                        split(n + q, k, more)
                        for t in range(TT):
                            o = slice(t * P, (t + 1) * P)
                            last = product(BANK[2 * pair + t][:, 0:width], (HH[:, kk, o], HL[:, kk, o]),
                                           (wh[:, k, :], wl[:, k, :]), kk == 0, kk == KT - 1)
                        done(k, last)

            def feat_chunk(n, pair, width, more=0):
                for q in range(PIECES):
                    wh, wl = view(WH, nth(n + q) % 2, width), view(WL, (n + q) % NSLOT, width)
                    for k in range(PK):
                        kk = q * PK + k
                        split(n + q, k, more)
                        for f in range(width // P):
                            o = slice(f * P, (f + 1) * P)
                            last = product(BANK[2 * pair + f // 2][:, (f % 2) * L:(f % 2 + 1) * L],
                                           (wh[:, k, o], wl[:, k, o]), (HH[:, kk, :], HL[:, kk, :]),
                                           kk == 0 and f % 2 == 0, kk == KT - 1)
                        done(k, last)

            def ada_chunk(n, bank, more=0):
                for q in range(PIECES):
                    wh, wl = view(WH, nth(n + q) % 2, CH), view(WL, (n + q) % NSLOT, CH)
                    for k in range(PK):
                        kk = q * PK + k
                        split(n + q, k, more)
                        last = product(bank, (CSH[:, kk, :], CSL[:, kk, :]), (wh[:, k, :], wl[:, k, :]),
                                       kk == 0, kk == KT - 1)
                        done(k, last)

            def to_feature(src, kt, first, base):
                for g in range(kt // 2):
                    bank = BANK[first + (base + g) % 2]
                    if base + g >= 2:
                        pe.wait_ge(xT_taken, 2 * (base + g - 1))
                    for f in range(2):
                        for t in range(TT):
                            last = pe.transpose(bank[:, f * L + t * P:f * L + (t + 1) * P],
                                                src[:, t, (2 * g + f) * P:(2 * g + f + 1) * P], ident[:])
                    last.then_inc(xT_ready, 1)

            pe.wait_ge(consts_set, 2)
            pe.wait_ge(params_in, PARAM_DMAS * 16)
            for g, r in enumerate(GROUP_ROWS):
                last = pe.transpose(BANK[6][:, g * P:g * P + r], rows[0:r, g, :], ident[0:r, 0:r])
            last.then_inc(colsT_ready, 1)
            pe.wait_ge(cs_split, 1)
            for j in range(2):
                ada_chunk(n_ada + PIECES * j, BANK[j][:, :])
            with pe.Fori(1, NADA // 2) as i:
                for j in range(2):
                    pe.wait_ge(row_took, i * 2 + j - 1)
                    ada_chunk(n_ada + PIECES * j, BANK[j][:, :], more=i * (2 * PIECES))
            for j in range(2 * KT):
                pe.wait_ge(row_took, j // 4 + 1)
                last = pe.matmul(BANK[7][:, j:j + 1], MROW[:, j * P:(j + 1) * P], ones[0:1, 0:1],
                                 start=True, stop=True)
            last.then_inc(modT_ready, 1)
            pe.wait_ge(xn_ready, 2)
            to_feature(XN, KT, 4, 0)
            pe.wait_ge(ht_ready, 8)
            tok_chunk(n_kw, 0, KW)
            feat_chunk(n_qi, 1, CH)
            pe.wait_ge(act_took, 2)
            feat_chunk(n_qi + PIECES, 0, CH)
            pe.wait_ge(kix_ready, 4)
            for lo in range(2):
                for t in range(TT):
                    last = pe.transpose(BANK[6][:, lo * L + t * P:lo * L + (t + 1) * P], KIX[:, t, lo, :], ident[:])
            last.then_inc(kixT_ready, 1)
            pe.wait_ge(kb_ready, 1)
            pe.wait_ge(act_took, 6)
            for j in range(8):
                for t in range(TT):
                    s = 2 * j + t
                    w = (t + 1) * P
                    if s >= 2:
                        pe.wait_ge(relu_ready, s - 1)
                    pe.matmul(BANK[4 + t][:, 0:2 * w].rearrange("p (a n) -> p a n", a=2), QI[:, j, t * P:(t + 1) * P], KB[:, :, 0:w],
                              start=True, stop=True).then_inc(idx_ready, 1)
            with pe.Fori(0, 2) as b:
                for j in range(8):
                    pe.wait_ge(act_took, b * 16 + 6 + 2 * j - 2)
                    tok_chunk(n_br + PIECES * j, (j + 1) % 2, CH, more=b * (8 * PIECES))
                    if 1 <= j <= 4:
                        c = j - 1
                        pe.wait_ge(head_normed, b * 4 + c + 1)
                        for g in range(2):
                            for f in range(2):
                                for t in range(TT):
                                    h = 2 * g + f
                                    last = pe.transpose(BANK[4 + 2 * (c % 2) + g][:, f * L + t * P:f * L + (t + 1) * P],
                                                        stage[:, c % 2, t, h * P:(h + 1) * P], ident[:])
                        last.then_inc(headT_ready, 1)
            pe.wait_ge(cs_split, 2)
            with pe.Fori(0, 2) as i:
                for j in range(2):
                    pe.wait_ge(act_took, i * 2 + (ACT_GATE - 1 + j))
                    ada_chunk(n_gate + PIECES * j, BANK[2 * j][:, :], more=i * (2 * PIECES))
            attention_pe(pe, 2 * HEADS, 0,
                         lambda h, t: [(QT[:, h // HEADS, h % HEADS, t * P:(t + 1) * P],
                                        KTT[:, h // HEADS, h % HEADS, 0:(t + 1) * P])],
                         lambda h, k: V1[:, h // HEADS, k, (h % HEADS) * DH:(h % HEADS + 1) * DH], Pr, PTs)
            pe.wait_ge(out_taken, 4 * HEADS)
            for bb in range(2):
                to_feature(Z1[:, bb], 8, 4, 8 + 4 * bb)
            pe.wait_ge(ht_ready, 16)
            pe.wait_ge(act_took, ACT_RKV)
            for c in range(4):
                if c >= 2:
                    pe.wait_ge(x_updated, 2 * (c - 1))
                tok_chunk(n_wo + PIECES * c, c % 2, CH)
            pe.wait_ge(xn_ready, 4)
            to_feature(XN2, KT, 4, 16)
            pe.wait_ge(ht_ready, 24)
            with pe.Fori(0, 3) as i:
                for j in range(2):
                    pe.wait_ge(act_took, i * 4 + (ACT_RKV + 2 * j - 2))
                    feat_chunk(n_rkv + PIECES * j, j, CH, more=i * (2 * PIECES))
            pe.wait_ge(act_took, ACT_RKV + 2 * 5)
            feat_chunk(n_wag, 0, 3 * P)
            pe.wait_ge(act_took, ACT_RKV + 2 * 6)
            tok_chunk(n_kpe, 1, ROPE)
            for j in range(2):
                pe.wait_ge(act_took, ACT_RKV + 2 * (7 + j))
                tok_chunk(n_c + PIECES * j, j, CH)
            pe.wait_ge(kpx_ready, 4)
            to_feature(KPX.rearrange("p t a n -> p t (a n)"), 2, 4, 24)
            pe.wait_ge(c_normed, 2 * TT)
            for q in range(2):
                to_feature(CQ[:, 2 * q:2 * q + 2, :], 4, 4, 25 + 2 * q)
            pe.wait_ge(xT_taken, 2 * 29)
            for part, (n, stride) in enumerate(((n_uq, 192), (n_uq + 2, 192), (n_ukv, 256), (n_ukv + 2, 256))):
                c0 = 0 if part < 2 else 4
                w = [view(WR, (n + m) % NSLOT, 2 * stride) for m in range(2)]
                pe.wait_ge(act_took, ACT_RKV + 2 * (9 + 2 * part))
                for h in range(4):
                    if h % 2 == 0:
                        arrived(n + h // 2)
                    for k in range(4):
                        last = pe.matmul(BANK[h // 2][:, (h % 2) * L:(h % 2 + 1) * L],
                                         w[h // 2][:, k, (h % 2) * stride:(h % 2) * stride + P], CT[:, c0 + k, :],
                                         start=(k == 0), stop=(k == 3))
                last.then_inc(lora_ready, 1)
                pe.wait_ge(act_took, ACT_RKV + 2 * (10 + 2 * part))
                width = stride - P
                for m in range(2):
                    for t in range(TT):
                        for k in range(4):
                            last = pe.matmul(BANK[2 + t][:, 2 * m * width:2 * (m + 1) * width].rearrange("p (h n) -> p h n", h=2),
                                             CT[:, c0 + k, t * P:(t + 1) * P],
                                             w[m][:, k, :].rearrange("p (h n) -> p h n", h=2)[:, :, P:stride],
                                             start=(k == 0), stop=(k == 3))
                    last.then_inc(piece_done, 1)
            pe.wait_ge(qpr_ready, 1)
            to_feature(QPR, 4, 4, 29)
            pe.wait_ge(xT_taken, 2 * 31)
            pe.wait_ge(act_took, ACT_RKV + 36)
            attention_pe(pe, HEADS, 2 * HEADS,
                         lambda h, t: [(QN[:, h, t * P:(t + 1) * P], KN[:, h, 0:(t + 1) * P]),
                                       (QPT[:, h // 2, t * P:(t + 1) * P], KPT[:, h % 2, 0:(t + 1) * P])],
                         lambda h, k: VM[:, k, h * DH:(h + 1) * DH], Pr2, PT2)
            pe.wait_ge(out_taken, 6 * HEADS)
            to_feature(YM, 8, 4, 31)
            pe.wait_ge(rw_mid, 1)
            for q in range(2):
                arrived(n_w2 + q)
                for g in range(4):
                    r = 4 * q + g
                    if r >= 4:
                        pe.wait_ge(rw_small_took, 2 * (r - 3))
                    p0 = 64 * q
                    for f in range(2):
                        last = pe.matmul(BANK[r % 4][:, f * L:(f + 1) * L],
                                         WR[p0:p0 + 64, (n_w2 + q) % NSLOT, (2 * g + f) * P:(2 * g + f + 1) * P],
                                         HWA[p0:p0 + 64, :], start=True, stop=True)
                    if g < 3:
                        last.then_inc(rw_small, 1)
                    else:
                        last.then_inc(piece_done, 1)
            pe.wait_ge(rw_masks, 1)
            pe.wait_ge(rw_small_took, 16)
            pe.wait_ge(kk_sq, 1)
            for g in range(4):
                pe.matmul(BANK[g][:, :], head_ones, sqk[:, 2 * g:2 * g + 2, :], start=True, stop=True).then_inc(kk_sum, 1)
            pe.wait_ge(prep_ready, 1)
            P_ = Steps(pe_step, pe_names)
            A_, D_ = Steps(act_step, act_names), Steps(dve_step, dve_names)
            with pe.Fori(0, 2) as g, pe.Fori(0, NCH) as c:
                it = g * NCH + c

                def four(name, bank, lhsT, rhs, width, extra=()):
                    o = BANK[bank][:, 0:4 * width].rearrange("p (q n) -> p q n", q=4)
                    terms = [(lhsT, rhs), *extra]
                    for q in range(4):
                        for n, (x, y) in enumerate(terms):
                            last = pe.matmul(o[:, q, :], x[:, q, :], y[:, q, :] if len(y.shape) == 3 else y,
                                             start=(n == 0), stop=(n == len(terms) - 1))
                    P_.mark(last, name)

                D_.wait(pe, "a1", it)
                four("LT", 0, b_bd, a_bd, P)
                four("AkT", 1, k_bd, a_bd, P)
                for name, bank, src in (("btok", 2, b_bd), ("ktok", 3, k_bd)):
                    for q in range(4):
                        last = pe.transpose(BANK[bank][:, q * P:(q + 1) * P], src[:, q, :], ident[:])
                    P_.mark(last, name)
                four("Vp", 4, v_bd, I2, N)
                four("BrT", 5, b_bd, r_bd, P)
                four("KrT", 6, k_bd, r_bd, P)
                for m in range(LEVELS):
                    if m == 0:
                        D_.wait(pe, "LT", it)
                        four("T0", 7, LT, ident[:], P)
                        D_.wait(pe, "T0", it)
                        four("Z0", 1, T2, ident[:], P)
                        continue
                    D_.wait(pe, f"X{m - 1}", it)
                    four(f"T{m}", 7, LT, Xi, P)
                    D_.wait(pe, f"T{m}", it)
                    if m < LEVELS - 1:
                        four(f"X{m}", 0, Zi, T2, P)
                    four(f"Z{m}", 1, T2, Zi, P)
                A_.wait(pe, "Vp", it)
                D_.wait(pe, "AkT", it)
                four("P1", 4, a_bd, ST, N, [(AkT, Vp)])
                D_.wait(pe, f"Z{LEVELS - 1}", it)
                A_.wait(pe, "P1", it)
                four("U", 2, Zi, P1, N)
                A_.wait(pe, "U", it)
                D_.wait(pe, "KrT", it)
                four("Y", 3, r_bd, ST, N, [(BrT, Us), (KrT, Vp)])
                four("S", 5, b_tok, Us, N, [(k_tok, Vp)])
                D_.wait(pe, "y1", it)
                four("YT", 6, y_bd, I2, N)
            pe.wait_ge(rk_ready, 1)
            for g in range(4):
                pe.matmul(BANK[g][:, :], head_ones, RK2[:, 2 * g:2 * g + 2, :], start=True, stop=True) \
                    .then_inc(bonus_ready, 1)
            arrived(n_w2 + 2)
            arrived(n_w2 + 3)
            for g in range(4):
                pe.wait_ge(bonus_took, g + 1)
                for f in range(2):
                    for n, h in enumerate((HG0, HG1)):
                        r = (P, 32)[n]
                        last = pe.matmul(BANK[g][:, f * L:(f + 1) * L],
                                         WR[0:r, (n_w2 + 2 + n) % NSLOT, (2 * g + f) * P:(2 * g + f + 1) * P],
                                         h[0:r, :], start=(n == 0), stop=(n == 1))
                if g < 3:
                    last.then_inc(g_ready, 1)
                else:
                    last.then_inc(piece_done, 2)
            pe.wait_ge(g_took, 8)
            pe.wait_ge(ht_ready, 28)
            for c in range(4):
                if c >= 2:
                    pe.wait_ge(x_updated, 8 + 2 * (c - 1))
                tok_chunk(n_wo2 + PIECES * c, c % 2, CH)
            pe.wait_ge(xn_ready, 6)
            to_feature(XN3, KT, 4, 35)
            pe.wait_ge(ht_ready, 36)
            with pe.Fori(0, FF // CH) as i:
                pe.wait_ge(act_took, i * 2 + (ACT_RKV + 36))
                feat_chunk(n_gu, 0, CH, more=i * (2 * PIECES))
                pe.wait_ge(up_taken, i * 2 + 1)
                feat_chunk(n_gu + PIECES, 1, CH, more=i * (2 * PIECES))
            pe.wait_ge(up_taken, FF // CH * 2 + 1)

            def down(g, first, final, more=0):
                pe.wait_ge(a_ready, more + (g + 1))
                for c in range(4):
                    n = n_dn + 4 * g + c
                    wh, wl = view(WH, nth(n) % 2, CH), view(WL, n % NSLOT, CH)
                    for k in range(PK):
                        split(n, k, more * PIECES)
                        for t in range(TT):
                            o = slice(t * P, (t + 1) * P)
                            last = product(BANK[2 * c + t][:, :], (AH[:, g % 2, k, o], AL[:, g % 2, k, o]),
                                           (wh[:, k, :], wl[:, k, :]), first and k == 0, final and k == PK - 1)
                        done(k, last)

            down(0, True, False)
            with pe.Fori(0, 4) as i:
                down(1, False, False, more=i * 2)
                down(2, False, False, more=i * 2)
            down(9, False, False)
            down(10, False, True)

        @block.scalar
        def _(act):
            own = Chain(act, act_chain_s)
            for t in range(TT):
                act.dma_start(X[:, t, :], a["x"][0, t * P:(t + 1) * P, :]).then_inc(x_in, 16)
            act.wait_ge(rows_clear, 1)
            for name, _ in PARAMS:
                g, row, r = VEC[name]
                v = a[name]
                if len(v.shape) == 3:
                    v = v.rearrange("o a b -> o (a b)")
                v = v[0]
                if name == "rwkv_mu_2":
                    for r0, rn, c0, w in ((0, 26, 0, P), (26, 1, 26 * P, 32)):
                        act.dma_start(rows[row + r0:row + r0 + rn, g, 0:w],
                                      v[c0:c0 + rn * w].rearrange("(a n) -> a n", a=rn)).then_inc(params_in, 16)
                else:
                    act.dma_start(rows[row:row + r, g, :], v.rearrange("(a n) -> a n", n=P)).then_inc(params_in, 16)
            for tap in range(3):
                g, row, r = VEC[f"conv{tap}"]
                act.dma_start(rows[row:row + r, g, :],
                              a["ffn_conv_w_2"][0, tap, :].rearrange("(a n) -> a n", n=P)).then_inc(params_in, 16)
            act.dma_start(kin_g, a["k_norm_idx"][0:1, :].to_broadcast([P, IDX_DIM])).then_inc(misc_in, 16)

            act.wait_ge(x_in, 32)
            for t in range(TT):
                act.activation(XN[:, t, :], X[:, t, :], ACT.Square, accum_out=ss[:, t:t + 1]).then_inc(ssq_ready, 1)
            act.wait_ge(cols_ready, 1)
            act.activation(cs, col("c", 0, 16), ACT.Silu).then_inc(cs_ready, 1)

            def high(n, more=0):
                act.wait_ge(piece_in[n % NSLOT], more * (16 // NSLOT) + 16 * (n // NSLOT + 1))
                w = width_of(n)
                for s in range(2):
                    if nth(n) >= 2 or not isinstance(more, int):
                        if s == 0:
                            act.wait_ge(half_done, more + (nth(n) - 1))
                        else:
                            act.wait_ge(piece_done, more + (n - 1 if not n_wo2 <= n < n_wo2 + 2 else n_uq + n - n_wo2 - 1))
                    act.activation(half(WH, nth(n) % 2, s, w), half(WR, n % NSLOT, s, w), ACT.Copy).then_inc(hi_ready, 1)

            def rest_then_next(n, more=0, following=True):
                for q in (2, 3, 4, 5)[:4 if following else 2]:
                    high(n + q, more)

            def sqrt_of(dst, src):
                return act.activation(dst, src, ACT.Sqrt)

            act.wait_ge(var_ready, 1)
            sqrt_of(rstd, rstd).then_inc(rstd_ready, 1)

            def read_chunk(n, pair, dsts, func=ACT.Copy, more=0, width=CH, parts=P, signal=None):
                act.wait_ge(piece_done, more + (n + PIECES))
                for t, dst in enumerate(dsts):
                    act.activation(dst, BANK[2 * pair + t][0:parts, 0:width], func).then_inc(act_took, 1)

            def take_row(j, dst, more=0):
                act.wait_ge(piece_done, more + (PIECES * (j + 1)))
                act.activation(dst, BANK[j % 2][0:1, :], ACT.Copy).then_inc(row_took, 1)

            high(0)
            high(1)
            for j in range(2):
                rest_then_next(PIECES * j)
                take_row(j, MROW[:, j * CH:(j + 1) * CH])
            with act.Fori(1, NADA // 2 - 1) as i:
                for j in range(2):
                    rest_then_next(PIECES * j, more=i * (2 * PIECES))
                    take_row(j, MROW[:, ds(i * 2 * CH + j * CH, CH)], more=i * (2 * PIECES))
            for j in range(2):
                c = NADA - 2 + j
                rest_then_next(PIECES * c)
                take_row(j, MROW[:, c * CH:(c + 1) * CH], more=PIECES * (NADA - 2))

            def take_feature(dsts, base, gains=None):
                for g in range(len(dsts) // 2):
                    act.wait_ge(xT_ready, base + g + 1)
                    for f in range(2):
                        k = 2 * g + f
                        act.activation(dsts[k], BANK[4 + (base + g) % 2][:, f * L:(f + 1) * L], ACT.Copy,
                                       scale=gains[k] if gains else 1.0).then_inc(xT_taken, 1)

            def take_split(hf, groups, base, ht, gains=None, biases=None):
                for g in range(groups):
                    act.wait_ge(xT_ready, base + g + 1)
                    if g >= 2:
                        act.wait_ge(ht_ready, ht + g - 1)
                    for f in range(2):
                        k = 2 * g + f
                        src = BANK[4 + (base + g) % 2][:, f * L:(f + 1) * L]
                        if biases:
                            ins = act.activation(hf[:, g % 2, f, :], src, ACT.Identity, bias=biases[k], scale=gains[k])
                        else:
                            ins = act.activation(hf[:, g % 2, f, :], src, ACT.Copy, scale=gains[k] if gains else 1.0)
                        ins.then_inc(xT_taken, 1)

            act.wait_ge(mod_ready, 1)
            take_split(hf1, 8, 0, 0, [gs[:, k:k + 1] for k in range(KT)], [mod[:, k:k + 1] for k in range(KT)])
            rest_then_next(n_kw)
            read_chunk(n_kw, 0, [KI[:, t, :] for t in range(TT)], width=KW)
            high(n_qi + 2)
            high(n_qi + 3)
            act.wait_ge(ki_var, 1)
            sqrt_of(krstd, krstd).then_inc(ki_rstd, 1)
            high(n_qi + 4)
            high(n_qi + 5)
            for j in range(2):
                if j == 1:
                    rest_then_next(n_qi + PIECES)
                read_chunk(n_qi + PIECES * j, (1 + j) % 2, [QI[:, 4 * j + 2 * t:4 * j + 2 * t + 2, :].rearrange(
                    "p a n -> p (a n)") for t in range(TT)])
            act.wait_ge(kixT_ready, 1)
            act.activation(KB.rearrange("p a n -> p (a n)"), BANK[6][:, :], ACT.Copy).then_inc(kb_ready, 1)
            for s in range(16):
                t = s % 2
                w = (t + 1) * 2 * P
                act.wait_ge(idx_ready, s + 1)
                if s >= 2:
                    act.wait_ge(relu_used, s - 1)
                act.activation(relu[:, t, 0:w], BANK[4 + t][:, 0:w], ACT.Relu).then_inc(relu_ready, 1)
            with act.Fori(0, 2) as b:
                more = b * (8 * PIECES)
                for j in range(8):
                    n, pair = n_br + PIECES * j, (j + 1) % 2
                    high(n + 2, more)
                    high(n + 3, more)
                    if 1 <= j <= 4:
                        act.wait_ge(head_var, b * 4 + j)
                        hr = hrstd[:, 8 * ((j - 1) % 2):8 * ((j - 1) % 2) + 8]
                        sqrt_of(hr, hr).then_inc(head_rstd, 1)
                    high(n + 4, more)
                    high(n + 5, more)
                    if j < 4:
                        if j >= 2:
                            act.wait_ge(headT_ready, b * 4 + (j - 1))
                        read_chunk(n, pair, [stage[:, j % 2, t, :] for t in range(TT)], more=more)
                    elif j < 6:
                        read_chunk(n, pair, [V1[:, ds(b, 1), t, (j - 4) * CH:(j - 3) * CH].rearrange("p o n -> p (o n)")
                                             for t in range(TT)], more=more)
                    else:
                        read_chunk(n, pair, [Z1[:, ds(b, 1), t, (j - 6) * CH:(j - 5) * CH].rearrange("p o n -> p (o n)")
                                             for t in range(TT)], func=ACT.Silu, more=more)
                    if 1 <= j <= 4:
                        c = j - 1
                        act.wait_ge(headT_ready, b * 4 + c + 1)
                        dst = QT if c < 2 else KTT
                        for g in range(2):
                            h = 4 * (c % 2) + 2 * g
                            act.activation(dst[:, ds(b, 1), h:h + 2, :].rearrange("p o a n -> p (o a n)"),
                                           BANK[4 + 2 * (c % 2) + g][:, :], ACT.Copy,
                                           scale=qgain[:, ds(b + (0 if c < 2 else 2), 1)]).then_inc(headT_taken, 1)
            act.wait_ge(piece_done, n_gate)
            act.dma_start(bgate_row, a["b_ada"][0:1, 2 * D:3 * D].to_broadcast([P, D])).then_inc(bgate_in, 16)
            for c in range(4):
                rest_then_next(n_gate + PIECES * c)
                act.wait_ge(piece_done, n_gate + PIECES * (c + 1))
                act.activation(gate_row[:, c * CH:(c + 1) * CH], BANK[2 * (c % 2)][:, :], ACT.Copy).then_inc(act_took, 1)
            attention_act(act, 2 * HEADS, 0, S_sb, Pr, PTs)
            take_split(hf1, 8, 8, 8)
            for c in range(4):
                rest_then_next(n_wo + PIECES * c)
            for t in range(TT):
                act.dma_start(pos_i[:, t:t + 1], a["positions_2"][0, t * P:(t + 1) * P].rearrange("(p o) -> p o", o=1)) \
                   .then_inc(pos_in, 16)

            def norm_act(q, junk, updates, c=None):
                act.wait_ge(x_updated, updates)
                for t in range(TT):
                    act.activation(junk[:, t, :], X[:, t, :], ACT.Square, accum_out=ss[:, t:t + 1]).then_inc(ssq_ready, 1)
                act.wait_ge(var_ready, q + 1)
                sqrt_of(rstd, rstd).then_inc(rstd_ready, 1)

            norm_act(1, XN2, 8)
            take_split(hf2, 8, 16, 16, [col("attn_norm_g_2", k) for k in range(KT)])
            act.wait_ge(ang_ready, 1)
            act.activation(ang.rearrange("p s t n -> p (s t n)"), turns.rearrange("p s t n -> p (s t n)"),
                           ACT.Sin).then_inc(trig_ready, 1)
            act.wait_ge(raw_clear, 1)
            def read_raw(i, j):
                rest_then_next(n_rkv + PIECES * (j if not isinstance(i, int) else 2 * i + j),
                               0 if isinstance(i, int) else i * (2 * PIECES))
                act.wait_ge(piece_done, i * (2 * PIECES) + (n_rkv + PIECES * (j + 1)))
                act.wait_ge(shifted, i * 2 + (j + 1))
                for t in range(TT):
                    act.activation(RAW[:, 2 * t:2 * t + 2, 1:L + 1],
                                   BANK[2 * j + t][:, :].rearrange("p (f n) -> p f n", f=2),
                                   ACT.Copy).then_inc(act_took, 1)

            with act.Fori(0, 2) as i:
                for j in range(2):
                    read_raw(i, j)
            for j in range(2):
                read_raw(2, j)
            rest_then_next(n_wag)
            act.wait_ge(piece_done, n_wag + PIECES)
            act.wait_ge(shifted, 7)
            for t in range(TT):
                act.activation(RAW[:, 2 * t:2 * t + 2 - t, 1:L + 1],
                               BANK[t][:, 0:(2 - t) * L].rearrange("p (f n) -> p f n", n=L), ACT.Copy).then_inc(act_took, 1)
            rest_then_next(n_kpe)
            read_chunk(n_kpe, 1, [KPE[:, t, :] for t in range(TT)], width=ROPE)
            for j in range(2):
                rest_then_next(n_c + PIECES * j, following=j == 0)
                read_chunk(n_c + PIECES * j, j, [CQ[:, 2 * j + t, :] for t in range(TT)])
            for j in range(4):
                act.wait_ge(act_took, ACT_RKV + 2 * 9 + 2)
                act.activation(XN2[:, j // 2, (j % 2) * CH:(j % 2 + 1) * CH], CQ[:, j, :], ACT.Square,
                               accum_out=cstat[:, j:j + 1]).then_inc(c_sq, 1)
            act.wait_ge(c_var, 1)
            sqrt_of(crstd, crstd).then_inc(c_rstd, 1)
            act.wait_ge(wag_ready, 3)
            act.activation(HWA[0:64, :], HWA[0:64, :], ACT.Tanh).then_inc(rw_mid, 1)
            take_feature([KPT[:, k, :] for k in range(2)], 24)
            for q, name in enumerate(("mla_q_norm_g_2", "mla_kv_norm_g_2")):
                take_feature([CT[:, 4 * q + k, :] for k in range(4)], 25 + 2 * q, [col(name, k) for k in range(4)])
            scale = float(DH + ROPE) ** -0.5
            for part in range(4):
                dst, o = (QN, KN)[part // 2], 4 * (part % 2)
                act.wait_ge(lora_ready, part + 1)
                for t in range(TT):
                    act.activation(dst[:, o + 2 * t:o + 2 * t + 2, :].rearrange("p a n -> p (a n)"), BANK[t][:, :],
                                   ACT.Copy, scale=scale if part < 2 else 1.0).then_inc(act_took, 1)
                act.wait_ge(piece_done, n_uq + 2 * (part + 1))
                for t in range(TT):
                    if part < 2:
                        act.activation(QPE[:, t, part * 256:(part + 1) * 256], BANK[2 + t][:, 0:256], ACT.Copy,
                                       scale=scale).then_inc(act_took, 1)
                    else:
                        act.activation(VM[:, t, (part - 2) * CH:(part - 1) * CH], BANK[2 + t][:, :],
                                       ACT.Copy).then_inc(act_took, 1)
            take_feature([QPT[:, k, :] for k in range(4)], 29)
            attention_act(act, HEADS, 2 * HEADS, S2, Pr2, PT2)
            take_split(hf3, 4, 31, 24)
            act.activation(HG0, HG0, ACT.Sigmoid).then_inc(rw_mid, 1)
            act.activation(HG1[0:32, :], HG1[0:32, :], ACT.Sigmoid).then_inc(rw_mid, 1)
            for r in range(8):
                if r % 4 < 3:
                    act.wait_ge(rw_small, r + 1 - r // 4)
                else:
                    act.wait_ge(piece_done, n_w2 + r // 4 + 1)
                dst, bias = ((Lw, "rwkv_w0_2"), (Bv, "rwkv_a0_2"))[r // 4]
                for f in range(2):
                    k = 2 * (r % 4) + f
                    act.activation(dst[:, k, :], BANK[r % 4][:, f * L:(f + 1) * L], ACT.Sigmoid,
                                   bias=col(bias, k)).then_inc(rw_small_took, 1)
            act.wait_ge(kk_var, 1)
            act.activation(sqk.rearrange("p f n -> p (f n)"), sqk.rearrange("p f n -> p (f n)"),
                           ACT.Sqrt).then_inc(kk_rstd, 1)
            act.wait_ge(fac_raw, 1)
            act.activation(small[:, 328:360], small[:, 328:360], ACT.Exp).then_inc(fac_ready, 1)
            act.wait_ge(prep_ready, 1)
            high(n_wo2)
            high(n_wo2 + 1)
            P_ = Steps(pe_step, pe_names)
            A_, D_ = Steps(act_step, act_names), Steps(dve_step, dve_names)
            with act.Fori(0, 2) as g, act.Fori(0, NCH) as c:
                it = g * NCH + c
                e = El[:, ds(4 * g, 4), ds(c * C, C)]
                A_.mark(act.activation(EX, e, ACT.Exp), "EX")
                A_.mark(act.activation(EN, e, ACT.Exp, scale=-1.0), "EN")
                D_.wait(act, "DEL", it)
                A_.mark(act.activation(EXC, DEL, ACT.Exp), "EXC")
                for name, dst, bank, w in (("btok", b_tok, 2, P), ("ktok", k_tok, 3, P), ("Vp", Vp, 4, N),
                                           ("P1", P1, 4, N), ("U", Us, 2, N)):
                    P_.wait(act, name, it)
                    A_.mark(act.activation(dst.rearrange("p q n -> p (q n)"), BANK[bank][:, 0:4 * w], ACT.Copy), name)
                D_.wait(act, "gi", it)
                A_.mark(act.activation(gvar, gvar, ACT.Sqrt), "sq")
                P_.wait(act, "YT", it)
                A_.mark(act.activation(YR[:, ds(4 * g, 4), ds(c * C, C)],
                                       BANK[6][:, 0:4 * N].rearrange("p (q n) -> p q n", q=4), ACT.Copy), "YT")
            for c in range(4):
                rest_then_next(n_wo2 + PIECES * c)
            norm_act(2, XN3, 16)
            act.dma_start(fg_row, a["final_norm_g_2"].rearrange("(o n) -> o n", o=1).to_broadcast([P, D])).then_inc(fg_in, 16)
            take_split(hf4, 8, 35, 28, [col("ffn_norm_g_2", k) for k in range(KT)])
            with act.Fori(0, FF // CH) as i:
                more = i * (2 * PIECES)
                rest_then_next(n_gu, more)
                act.wait_ge(piece_done, more + (n_gu + PIECES))
                act.wait_ge(conv_ready, i + 1)
                for t in range(TT):
                    act.activation(RAWF[:, 2 * t:2 * t + 2, 2:L + 2],
                                   BANK[t][:, :].rearrange("p (f n) -> p f n", f=2), ACT.Copy).then_inc(act_took, 1)
                rest_then_next(n_gu + PIECES, more)
                act.wait_ge(conv_ready, i + 2)
                act.activation(CV.rearrange("p f n -> p (f n)"), CV.rearrange("p f n -> p (f n)"),
                               ACT.Silu).then_inc(gate_act, 1)
            with act.Fori(0, FT // PK - 1) as i:
                rest_then_next(n_dn, i * PIECES)
            rest_then_next(n_dn + PIECES * (FT // PK - 1), following=False)
            norm_act(3, XN3, 24)

        @block.vector
        def _(dve):
            own = Chain(dve, dve_chain_s)

            def inverse_mean(dst, src, width, eps=EPS):
                own.link(dve.tensor_scalar(dst, src, 1.0 / width, eps, ALU.mult, ALU.add))
                return dve.reciprocal(dst, dst)

            def norm_dve(q):
                dve.wait_ge(ssq_ready, 2 * (q + 1))
                inverse_mean(rstd, ss, D).then_inc(var_ready, 1)

            def scale_x(q, dst):
                dve.wait_ge(rstd_ready, q + 1)
                for t in range(TT):
                    dve.tensor_scalar(dst[:, t, :], X[:, t, :], rstd[:, t:t + 1], None, ALU.mult).then_inc(xn_ready, 1)

            def ht_split(hf, groups, base, first):
                for g in range(groups):
                    k = slice(first + 2 * g, first + 2 * g + 2)
                    dve.wait_ge(xT_taken, 2 * (base + g + 1))
                    own.link(dve.tensor_copy(HH[:, k, :], hf[:, g % 2]))
                    dve.tensor_tensor(HL[:, k, :], hf[:, g % 2], HH[:, k, :], ALU.subtract).then_inc(ht_ready, 1)

            def split_c():
                wide = cs.unsqueeze(2).to_broadcast([P, KT, P])
                own.link(dve.tensor_copy(CSH[:, :, :], wide))
                dve.tensor_tensor(CSL[:, :, :], wide, CSH[:, :, :], ALU.subtract).then_inc(cs_split, 1)

            norm_dve(0)
            dve.wait_ge(colsT_ready, 1)
            for g, r in enumerate(GROUP_ROWS):
                last = dve.tensor_copy(cols[:, g * P:g * P + r], BANK[6][:, g * P:g * P + r])
            last.then_inc(cols_ready, 1)
            dve.wait_ge(cols_ready, 1)
            for b in range(2):
                own.mark(dve.tensor_scalar(qgain[:, b:b + 1], col(("q_norm_a", "q_norm_b")[b]), float(DH) ** -0.5, None, ALU.mult))
                own.mark(dve.tensor_copy(qgain[:, 2 + b:3 + b], col(("k_norm_a", "k_norm_b")[b])))
            dve.wait_ge(cs_ready, 1)
            split_c()
            scale_x(0, XN)
            dve.wait_ge(modT_ready, 1)
            own.link(dve.tensor_tensor(mod[:, 0:32], BANK[7][:, 0:32], col("b_ada", 0, 32), ALU.add))
            own.link(dve.tensor_scalar(gs, mod[:, 16:32], 1.0, None, ALU.add))
            dve.tensor_tensor(gs, gs, col("g_norm", 0, 16), ALU.mult).then_inc(mod_ready, 1)
            ht_split(hf1, 8, 0, 0)
            dve.wait_ge(act_took, 2)
            for t in range(TT):
                own.link(dve.tensor_tensor(square[:, t, 0:IDX_DIM], KI[:, t, 0:IDX_DIM], KI[:, t, 0:IDX_DIM], ALU.mult))
                own.link(dve.tensor_reduce(kss[:, t:t + 1], square[:, t, 0:IDX_DIM], AX_X, ALU.add))
            inverse_mean(krstd, kss, IDX_DIM).then_inc(ki_var, 1)
            dve.wait_ge(ki_rstd, 1)
            dve.wait_ge(misc_in, 16)
            dve.wait_ge(consts_set, CONSTS)
            for t in range(TT):
                for lo in range(2):
                    dve.scalar_tensor_tensor(out=KIX[:, t, lo, lo * IDX_DIM:(lo + 1) * IDX_DIM], in0=KI[:, t, 0:IDX_DIM],
                                             scalar=krstd[:, t:t + 1], in1=kin_g, op0=ALU.mult,
                                             op1=ALU.mult).then_inc(kix_ready, 1)
            for s in range(16):
                j, t = s // 2, s % 2
                w = (t + 1) * P
                sc = score[:, 0:P] if t == 0 else score[:, P:SPAN]
                dve.wait_ge(relu_ready, s + 1)
                for f in range(2):
                    wt = KI[:, t, IDX_DIM + 2 * j + f:IDX_DIM + 2 * j + f + 1]
                    r = relu[:, t, f * w:(f + 1) * w]
                    if j == 0 and f == 0:
                        own.link(dve.tensor_scalar(sc, r, wt, None, ALU.mult))
                    else:
                        ins = dve.scalar_tensor_tensor(out=sc, in0=r, scalar=wt, in1=sc, op0=ALU.mult, op1=ALU.add)
                        if f == 1:
                            ins.then_inc(relu_used, 1)
                            dve.wait_ge(relu_used, s + 1)
                        else:
                            own.link(ins)
            own.link(dve.tensor_tensor(score, score, causal_mask, ALU.add))
            own.link(dve.tensor_copy(work, score))
            halves = [(0, P), (P, L)]
            for r in range(TOPK // 8):
                for t, (c0, w) in enumerate(halves):
                    own.mark(dve.max(top8[:, t, :], work[:, c0:c0 + w]))
                own.wait()
                if r < TOPK // 8 - 1:
                    for t, (c0, w) in enumerate(halves):
                        own.mark(dve.match_replace(work[:, c0:c0 + w], top8[:, t, :], work[:, c0:c0 + w], -3e38))
                    own.wait()
            for t, (c0, w) in enumerate(halves):
                thr = top8[:, t, 7:8]
                sc, wk, gt = score[:, c0:c0 + w], work[:, c0:c0 + w], bias_a[:, c0:c0 + w]
                eq, run = square[:, t, 0:w], relu[:, t, 0:w]
                own.link(dve.tensor_scalar(gt, sc, thr, None, ALU.is_gt, ALU.add, accum_out=cnt[:, t:t + 1]))
                own.link(dve.tensor_scalar(need[:, t:t + 1], cnt[:, t:t + 1], -1.0, float(TOPK), ALU.mult, ALU.add))
                own.link(dve.tensor_scalar(eq, sc, thr, None, ALU.is_equal))
                own.link(dve.memset(wk, 1.0))
                own.link(dve.tensor_tensor_scan(run, wk, eq, 0.0, ALU.mult, ALU.add))
                own.link(dve.scalar_tensor_tensor(out=eq, in0=run, scalar=need[:, t:t + 1], in1=eq,
                                                  op0=ALU.is_le, op1=ALU.mult))
                own.link(dve.tensor_tensor(gt, gt, eq, ALU.add))
                own.link(dve.tensor_scalar(gt, gt, -1.0, -NEG, ALU.add, ALU.mult))
                own.link(dve.tensor_tensor(gt, gt, causal_dist[:, c0:c0 + w], ALU.add))
            with dve.Fori(0, 2) as b:
                own.enter(b, 12)
                for j in range(4):
                    s = stage[:, j % 2]
                    flat = s.rearrange("p t n -> p (t n)")
                    sq = square.rearrange("p t n -> p (t n)")
                    dve.wait_ge(act_took, b * 16 + 6 + 2 * (j + 1))
                    own.link(dve.tensor_tensor(sq, flat, flat, ALU.mult))
                    hs, hr = hss[:, 8 * (j % 2):8 * (j % 2) + 8], hrstd[:, 8 * (j % 2):8 * (j % 2) + 8]
                    own.link(dve.tensor_reduce(hs, sq.rearrange("p (g n) -> p g n", n=DH), AX_X, ALU.add))
                    inverse_mean(hr, hs, DH).then_inc(head_var, 1)
                    dve.wait_ge(head_rstd, b * 4 + j + 1)
                    for g in range(8):
                        v = s[:, g // 4, (g % 4) * DH:(g % 4 + 1) * DH]
                        last = dve.tensor_scalar(v, v, hr[:, g:g + 1], None, ALU.mult)
                    last.then_inc(head_normed, 1)
                own.leave(2)

            dve.wait_ge(piece_done, n_gate)
            split_c()
            dve.wait_ge(bgate_in, 16)
            dve.wait_ge(act_took, ACT_RKV)
            own.link(dve.tensor_tensor(gate_row, gate_row, bgate_row, ALU.add))

            def emit(h, t, o, inv):
                b, hh = h // HEADS, h % HEADS
                z = Z1[:, b, t, hh * DH:(hh + 1) * DH]
                return dve.scalar_tensor_tensor(out=z, in0=o, scalar=inv, in1=z, op0=ALU.mult, op1=ALU.mult)

            attention_dve(dve, own, 2 * HEADS, 0,
                          lambda h: bias_a if h < HEADS else causal_dist,
                          lambda h: slope[:, h:h + 1], emit, S_sb)
            ht_split(hf1, 8, 8, 0)
            for c in range(4):
                dve.wait_ge(piece_done, n_wo + PIECES * (c + 1))
                for t in range(TT):
                    xc = X[:, t, c * CH:(c + 1) * CH]
                    own.link(dve.tensor_tensor(wo_tmp[:, t, :], BANK[2 * (c % 2) + t][:, :],
                                               gate_row[:, c * CH:(c + 1) * CH], ALU.mult))
                    dve.tensor_tensor(xc, xc, wo_tmp[:, t, :], ALU.add).then_inc(x_updated, 1)
            norm_dve(1)
            scale_x(1, XN2)
            for j in range(32):
                own.mark(dve.memset(inv_freq[:, j:j + 1], float(np.float32(10000.0) ** np.float32(-j / 32.0))))
            dve.wait_ge(pos_in, 32)
            own.mark(dve.tensor_copy(pos, pos_i))
            own.wait()
            flat = lambda v: v.rearrange("p t n -> p (t n)")
            two_pi = 2 * np.pi
            c1 = 6.28125
            c2 = float(np.float32(int((two_pi - c1) * 2 ** 21) / 2 ** 21))
            c3 = float(two_pi - c1 - c2)
            magic = 1.5 * 2 ** 23
            for part in range(2):
                th, nt = ang[:, part], turns[:, part]
                for t in range(TT):
                    own.mark(dve.tensor_scalar(th[:, t, :], inv_freq, pos[:, t:t + 1], None, ALU.mult))
                own.wait()
                own.link(dve.tensor_scalar(flat(nt), flat(th), float(1 / two_pi), 0.25 * part, ALU.mult, ALU.add))
                own.link(dve.tensor_scalar(flat(nt), flat(nt), magic, -magic, ALU.add, ALU.add))
                for cc in (c1, c2, c3):
                    own.link(dve.scalar_tensor_tensor(out=flat(th), in0=flat(nt), scalar=-cc, in1=flat(th),
                                                      op0=ALU.mult, op1=ALU.add))
                own.link(dve.tensor_scalar(flat(th), flat(th), float(np.pi / 2) * part, None, ALU.add))
                lim = float(np.nextafter(np.float32(np.pi), np.float32(0)))
                own.link(dve.tensor_scalar(flat(nt), flat(th), lim, -lim, ALU.min, ALU.max))
            dve.tensor_copy(small[:, 510:511], pos[:, 0:1]).then_inc(ang_ready, 1)
            ht_split(hf2, 8, 16, 0)
            own.link(dve.memset(RAW[:, :, 0:1], 0.0))
            dve.memset(small[:, 509:510], 0.0).then_inc(raw_clear, 1)
            dve.memset(small[:, 508:509], 0.0).then_inc(shifted, 1)
            gm, rm, _ = VEC["rwkv_mu_2"]
            mu0 = gm * P + rm
            with dve.Fori(0, 3) as i:
                own.enter(i, 2)
                for j in range(2):
                    dve.wait_ge(act_took, i * 4 + (ACT_RKV + 2 * j + 2))
                    own.link(dve.tensor_tensor(SH, RAW[:, :, 0:L], RAW[:, :, 1:L + 1], ALU.subtract))
                    for f in range(4):
                        last = dve.scalar_tensor_tensor(out=RKV[:, ds(8 * i + (4 * j + f), 1), :].rearrange("p o n -> p (o n)"),
                                                        in0=SH[:, f, :], scalar=cols[:, ds(8 * i + (mu0 + 4 * j + f), 1)],
                                                        in1=RAW[:, f, 1:L + 1], op0=ALU.mult, op1=ALU.add)
                    last.then_inc(shifted, 1)
                own.leave(3)
            dve.wait_ge(act_took, ACT_RKV + 14)
            own.link(dve.tensor_tensor(SH[:, 0:3, :], RAW[:, 0:3, 0:L], RAW[:, 0:3, 1:L + 1], ALU.subtract))
            for f, (dst, m) in enumerate(((HWA, P), (HG0, P), (HG1, 32))):
                dve.scalar_tensor_tensor(out=dst[0:m, :], in0=SH[0:m, f, :], scalar=cols[0:m, mu0 + 24 + f:mu0 + 25 + f],
                                         in1=RAW[0:m, f, 1:L + 1], op0=ALU.mult, op1=ALU.add).then_inc(wag_ready, 1)
            dve.wait_ge(act_took, ACT_RKV + 16)
            own.link(dve.memset(KPX, 0.0))
            dve.wait_ge(trig_ready, 1)

            def rotate(dst, src, t, heads, emit=None):
                sn = ang[:, 0, t, :].unsqueeze(1).to_broadcast([P, heads, 32])
                cn = ang[:, 1, t, :].unsqueeze(1).to_broadcast([P, heads, 32])
                tmp = [rope_tmp[:, i, 0:heads * 32].rearrange("p (h n) -> p h n", n=32) for i in range(4)]
                lo, hi = src[:, :, 0:32], src[:, :, 32:64]
                for d, x, y in ((0, lo, cn), (1, hi, sn), (2, hi, cn), (3, lo, sn)):
                    own.mark(dve.tensor_tensor(tmp[d], x, y, ALU.mult))
                own.wait()
                return (dve.tensor_tensor(dst[:, :, 0:32], tmp[0], tmp[1], ALU.subtract),
                        dve.tensor_tensor(dst[:, :, 32:64], tmp[2], tmp[3], ALU.add))

            for t in range(TT):
                x, y = rotate(KPX[:, t, 0:1, 0:ROPE], KPE[:, t:t + 1, :], t, 1)
                own.mark(x)
                own.mark(y)
                own.wait()
                dve.tensor_copy(KPX[:, t, 1, ROPE:2 * ROPE], KPX[:, t, 0, 0:ROPE]).then_inc(kpx_ready, 2)
            dve.wait_ge(c_sq, 4)
            inverse_mean(crstd, cstat, LORA).then_inc(c_var, 1)
            dve.wait_ge(c_rstd, 1)
            for j in range(4):
                dve.tensor_scalar(CQ[:, j, :], CQ[:, j, :], crstd[:, j:j + 1], None, ALU.mult).then_inc(c_normed, 1)
            dve.wait_ge(act_took, ACT_RKV + 28)
            for t in range(TT):
                x, y = rotate(QPR[:, t, :].rearrange("p (h n) -> p h n", n=ROPE),
                              QPE[:, t, :].rearrange("p (h n) -> p h n", n=ROPE), t, HEADS)
                own.mark(x)
                if t == 0:
                    own.mark(y)
                    own.wait()
                else:
                    y.then_inc(qpr_ready, 1)

            def emit2(h, t, o, inv):
                return dve.tensor_scalar(YM[:, t, h * DH:(h + 1) * DH], o, inv, None, ALU.mult)

            attention_dve(dve, own, HEADS, 2 * HEADS, lambda h: causal_mask, lambda h: 1.0, emit2, S2)
            dve.memset(small[:, 506:507], 0.0).then_inc(masks_free, 1)
            ht_split(hf3, 4, 31, 8)
            R_, K_, V_ = RKV[:, 0:8], RKV[:, 8:16], RKV[:, 16:24]
            fl = lambda v: v.rearrange("p f n -> p (f n)")
            own.link(dve.tensor_scalar(one_ka, col("rwkv_k_a_2", 0, 8), -1.0, 1.0, ALU.mult, ALU.add))
            for f in range(8):
                own.mark(dve.tensor_scalar(KKn[:, f, :], K_[:, f, :], col("rwkv_k_k_2", f), None, ALU.mult))
            own.wait()
            dve.tensor_tensor(fl(sqk), fl(KKn), fl(KKn), ALU.mult).then_inc(kk_sq, 1)
            dve.wait_ge(rw_small_took, 8)
            dve.wait_ge(rw_masks, 1)
            own.link(dve.tensor_scalar(fl(Lw), fl(Lw), -float(np.exp(-0.5)), None, ALU.mult))
            for f in range(8):
                own.mark(dve.tensor_tensor_scan(El[:, f, :], chunk_start, Lw[:, f, :], 0.0, ALU.mult, ALU.add))
            own.wait()
            e4 = fl(El).rearrange("p (g t) -> p g t", t=C)
            own.mark(dve.tensor_copy(small[:, 264:296], e4[:, :, C - 1]))
            own.mark(dve.tensor_copy(small[:, 296:328], e4[:, :, C // 2 - 1]))
            own.wait()
            own.mark(dve.tensor_tensor(e4, e4, small[:, 296:328].unsqueeze(2).to_broadcast([P, 32, C]), ALU.subtract))
            own.link(dve.tensor_tensor(fac, end_s, mid_s, ALU.subtract))
            own.link(dve.tensor_tensor(fac[:, :, 0:NCH - 1], fac[:, :, 0:NCH - 1], mid_s[:, :, 1:NCH], ALU.add))
            dve.tensor_copy(small[:, 505:506], small[:, 328:329]).then_inc(fac_raw, 1)
            dve.wait_ge(rw_small_took, 16)
            for f in range(8):
                own.mark(dve.tensor_scalar(kfac[:, f, :], Bv[:, f, :], col("rwkv_k_a_2", f), one_ka[:, f:f + 1],
                                           ALU.mult, ALU.add))
            own.wait()
            own.mark(dve.tensor_tensor(fl(K_), fl(K_), fl(kfac), ALU.mult))
            for g in range(4):
                dve.wait_ge(kk_sum, g + 1)
                own.mark(dve.tensor_scalar(fl(sqk[:, 2 * g:2 * g + 2]), BANK[g][:, :], 1e-24, None, ALU.max))
            own.wait()
            dve.reciprocal(fl(sqk), fl(sqk)).then_inc(kk_var, 1)
            dve.wait_ge(kk_rstd, 1)
            own.link(dve.tensor_tensor(fl(KKn), fl(KKn), fl(sqk), ALU.mult))
            own.link(dve.tensor_tensor(fl(Bv), fl(Bv), fl(KKn), ALU.mult))
            own.link(dve.tensor_scalar(fl(KKn), fl(KKn), -1.0, None, ALU.mult))
            for v in (a_bd, b_bd, k_bd, r_bd, v_bd, y_bd):
                own.mark(dve.memset(v, 0.0))
            own.wait()
            dve.wait_ge(fac_ready, 1)
            dve.memset(small[:, 504:505], 0.0).then_inc(prep_ready, 1)
            P_ = Steps(pe_step, pe_names)
            A_, D_ = Steps(act_step, act_names), Steps(dve_step, dve_names)
            four = lambda m: m.unsqueeze(1).to_broadcast([P, 4, P])
            bank4 = lambda b, w: BANK[b][:, 0:4 * w].rearrange("p (q n) -> p q n", q=4)
            with dve.Fori(0, 2) as g:
                own.enter(g, 1)
                own.mark(dve.memset(ST, 0.0))
                own.leave(2)
                with dve.Fori(0, NCH) as c:
                    it = g * NCH + c

                    def part(v, h=None):
                        v = v[:, ds(4 * g, 4), ds(c * C, C)]
                        return v if h is None else v[h * N:(h + 1) * N]

                    D_.mark(dve.tensor_tensor(DEL, part(El), part(Lw), ALU.subtract), "DEL")
                    for nm, dst, src, fct, ready in (("v", v_bd, V_, None, None), ("b", b_bd, Bv, EN, "EN"),
                                                     ("k", k_bd, K_, EN, "EN"), ("r", r_bd, R_, EX, "EX"),
                                                     ("a", a_bd, KKn, EXC, "EXC")):
                        if ready:
                            A_.wait(dve, ready, it)
                        for h in range(2):
                            o = dst[h * N:(h + 1) * N, :, h * N:(h + 1) * N]
                            x = part(src, h)
                            D_.mark(dve.tensor_copy(o, x) if fct is None else
                                    dve.tensor_tensor(o, x, fct[h * N:(h + 1) * N], ALU.mult), f"{nm}{h}")
                    for nm, dst, bank, m in (("LT", LT, 0, below), ("AkT", AkT, 1, below), ("BrT", BrT, 5, upto_diag),
                                             ("KrT", KrT, 6, upto_diag)):
                        P_.wait(dve, nm, it)
                        D_.mark(dve.tensor_tensor(dst, bank4(bank, P), four(m), ALU.mult), nm)
                    for m in range(LEVELS):
                        P_.wait(dve, f"T{m}", it)
                        D_.mark(dve.tensor_tensor(T2, bank4(7, P), four(level[m]), ALU.mult), f"T{m}")
                        if m == 0:
                            D_.wait(dve, "T0", it)
                            D_.mark(dve.tensor_tensor(Xi, T2, four(ident[:]), ALU.add), "X0")
                            P_.wait(dve, "Z0", it)
                            D_.mark(dve.tensor_tensor(Zi, bank4(1, P), four(ident[:]), ALU.add), "Z0")
                            continue
                        if m < LEVELS - 1:
                            P_.wait(dve, f"X{m}", it)
                            D_.mark(dve.tensor_tensor(Xi, Xi, bank4(0, P), ALU.add), f"X{m}")
                        P_.wait(dve, f"Z{m}", it)
                        D_.mark(dve.tensor_tensor(Zi, Zi, bank4(1, P), ALU.add), f"Z{m}")
                    b4 = lambda v: v.unsqueeze(2).to_broadcast([P, 4, N])
                    P_.wait(dve, "S", it)
                    D_.mark(dve.tensor_tensor(ST, ST, bank4(5, N), ALU.add), "Ssum")
                    D_.mark(dve.tensor_reduce(gsum, bank4(3, N), AX_X, ALU.add), "gs")
                    D_.wait(dve, "gs", it)
                    D_.mark(dve.scalar_tensor_tensor(out=YC, in0=b4(gsum), scalar=-1.0 / N, in1=bank4(3, N),
                                                     op0=ALU.mult, op1=ALU.add), "yc")
                    D_.wait(dve, "yc", it)
                    D_.mark(dve.tensor_tensor(YQ, YC, YC, ALU.mult), "yq")
                    D_.wait(dve, "yq", it)
                    D_.mark(dve.tensor_reduce(gvar, YQ, AX_X, ALU.add), "gv")
                    D_.wait(dve, "gv", it)
                    D_.mark(dve.tensor_scalar(gvar, gvar, 1.0 / N, GN_EPS, ALU.mult, ALU.add), "ge")
                    D_.wait(dve, "ge", it)
                    D_.mark(dve.reciprocal(gvar, gvar), "gi")
                    A_.wait(dve, "sq", it)
                    for h in range(2):
                        D_.mark(dve.tensor_tensor(y_bd[h * N:(h + 1) * N, :, h * N:(h + 1) * N], YC[h * N:(h + 1) * N],
                                                  b4(gvar)[h * N:(h + 1) * N], ALU.mult), f"y{h}")
                    D_.mark(dve.tensor_tensor(ST, ST, fac[:, ds(4 * g, 4), ds(c, 1)].to_broadcast([P, 4, N]), ALU.mult), "S")
                    D_.wait(dve, "S", it)
            A_.wait(dve, "YT", 7)
            D_.wait(dve, "S", 7)
            P_.wait(dve, "YT", 7)
            own.link(dve.tensor_tensor(fl(RK2), fl(R_), fl(K_), ALU.mult))
            for f in range(8):
                ins = dve.tensor_scalar(RK2[:, f, :], RK2[:, f, :], col("rwkv_r_k_2", f), None, ALU.mult)
            ins.then_inc(rk_ready, 1)
            for f in range(8):
                own.mark(dve.tensor_scalar(YR[:, f, :], YR[:, f, :], col("rwkv_gn_w_2", f), col("rwkv_gn_b_2", f),
                                           ALU.mult, ALU.add))
            for g in range(4):
                dve.wait_ge(bonus_ready, g + 1)
                dve.tensor_tensor(fl(BV[:, 2 * g:2 * g + 2]), BANK[g][:, :], fl(V_[:, 2 * g:2 * g + 2]),
                                  ALU.mult).then_inc(bonus_took, 1)
            dve.wait_ge(bonus_took, 4)
            own.wait()
            own.link(dve.tensor_tensor(fl(YR[:, :, :]), fl(YR[:, :, :]), fl(BV), ALU.add))
            for g in range(4):
                if g < 3:
                    dve.wait_ge(g_ready, g + 1)
                else:
                    dve.wait_ge(piece_done, n_wo2)
                y, k = YR[:, 2 * g:2 * g + 2, :], slice(2 * g, 2 * g + 2)
                own.link(dve.tensor_tensor(fl(y), fl(y), BANK[g][:, :], ALU.mult))
                own.link(dve.tensor_copy(HH[:, k, :], y))
                dve.tensor_tensor(HL[:, k, :], y, HH[:, k, :], ALU.subtract).then_inc(g_took, 2)
            for c in range(4):
                dve.wait_ge(piece_done, n_wo2 + PIECES * (c + 1))
                for t in range(TT):
                    xc = X[:, t, c * CH:(c + 1) * CH]
                    dve.tensor_tensor(xc, xc, BANK[2 * (c % 2) + t][:, :], ALU.add).then_inc(x_updated, 1)
            norm_dve(2)
            scale_x(2, XN3)
            ht_split(hf4, 8, 35, 0)
            own.link(dve.memset(RAWF[:, :, 0:2], 0.0))
            dve.memset(small[:, 503:504], 0.0).then_inc(conv_ready, 1)
            dve.memset(small[:, 502:503], 0.0).then_inc(up_taken, 1)
            tap = [VEC[f"conv{t}"][0] * P + VEC[f"conv{t}"][1] for t in range(3)]
            cb = VEC["ffn_conv_b_2"][0] * P + VEC["ffn_conv_b_2"][1]
            with dve.Fori(0, FF // CH) as i:
                own.enter(i, 8)
                dve.wait_ge(act_took, i * 2 + (ACT_RKV + 38))
                dve.wait_ge(up_taken, i * 2 + 1)
                for f in range(4):
                    w = lambda t: cols[:, ds(4 * i + (tap[t] + f), 1)]
                    own.mark(dve.tensor_scalar(CV[:, f, :], RAWF[:, f, 2:L + 2], w(2), cols[:, ds(4 * i + (cb + f), 1)],
                                               ALU.mult, ALU.add))
                own.wait()
                for f in range(4):
                    w = lambda t: cols[:, ds(4 * i + (tap[t] + f), 1)]
                    own.mark(dve.scalar_tensor_tensor(out=CV[:, f, :], in0=RAWF[:, f, 1:L + 1], scalar=w(1), in1=CV[:, f, :],
                                                      op0=ALU.mult, op1=ALU.add))
                own.wait()
                for f in range(4):
                    w = lambda t: cols[:, ds(4 * i + (tap[t] + f), 1)]
                    last = dve.scalar_tensor_tensor(out=CV[:, f, :], in0=RAWF[:, f, 0:L], scalar=w(0), in1=CV[:, f, :],
                                                    op0=ALU.mult, op1=ALU.add)
                last.then_inc(conv_ready, 1)
                dve.wait_ge(gate_act, i + 1)
                dve.wait_ge(piece_done, i * (2 * PIECES) + (n_gu + 2 * PIECES))
                for t in range(TT):
                    dve.tensor_tensor(AC[:, ds(4 * i + 2 * t, 2), :], CV[:, 2 * t:2 * t + 2, :],
                                      BANK[2 + t][:, :].rearrange("p (f n) -> p f n", f=2), ALU.mult).then_inc(up_taken, 1)
                own.leave(FF // CH)
            def split_hidden(g, dyn=None):
                tile = AC[:, PK * g:PK * (g + 1), :] if dyn is None else AC[:, ds(dyn * (2 * PK) + PK * g, PK), :]
                own.link(dve.tensor_copy(AH[:, g % 2], tile))
                dve.tensor_tensor(AL[:, g % 2], tile, AH[:, g % 2], ALU.subtract).then_inc(a_ready, 1)

            dve.wait_ge(up_taken, FF // CH * 2 + 1)
            split_hidden(0)
            split_hidden(1)
            with dve.Fori(0, 4) as i:
                own.enter(i, 2)
                for g in (2, 3):
                    dve.wait_ge(piece_done, i * (2 * PIECES) + (n_dn + PIECES * (g - 1)))
                    split_hidden(g, i)
                own.leave(4)
            dve.wait_ge(piece_done, n_dn + PIECES * 9)
            split_hidden(10)
            dve.wait_ge(piece_done, n_dn + PIECES * (FT // PK))
            for c in range(4):
                for t in range(TT):
                    xc = X[:, t, c * CH:(c + 1) * CH]
                    dve.tensor_tensor(xc, xc, BANK[2 * c + t][:, :], ALU.add).then_inc(x_updated, 1)
            norm_dve(3)
            dve.wait_ge(rstd_ready, 4)
            dve.wait_ge(fg_in, 16)
            for t in range(TT):
                dve.scalar_tensor_tensor(out=XN3[:, t, :], in0=X[:, t, :], scalar=rstd[:, t:t + 1], in1=fg_row,
                                         op0=ALU.mult, op1=ALU.mult).then_inc(fin_ready, 1)



_INS = ["x", "c", "w_ada", "b_ada", "g_norm", "w_in", "q_norm_a", "k_norm_a", "k_norm_idx", "q_norm_b",
        "k_norm_b", "w_out", "positions_2", "attn_norm_g_2", "w_in_2", "rwkv_mu_2", "rwkv_w0_2", "rwkv_w2_2",
        "rwkv_a0_2", "rwkv_a2_2", "rwkv_g2_2", "rwkv_k_k_2", "rwkv_k_a_2", "rwkv_r_k_2", "rwkv_gn_w_2",
        "rwkv_gn_b_2", "mla_q_norm_g_2", "mla_w_uq_2", "mla_kv_norm_g_2", "mla_w_ukv_2", "w_out_2",
        "ffn_norm_g_2", "ffn_w_gate_2", "ffn_w_up_2", "ffn_conv_w_2", "ffn_conv_b_2", "ffn_w_down_2",
        "final_norm_g_2"]
_OUT = (1, L, D)


def kernel(**inputs):
    import concourse.bacc as bacc
    from concourse.bass_utils import run_bass_kernel_spmd

    nc = bacc.Bacc("TRN2", target_bir_lowering=False, num_devices=1)
    arrays, args = {}, {}
    for name in _INS:
        v = np.ascontiguousarray(inputs[name])
        arrays[f"in_{name}"] = v
        args[name] = nc.dram_tensor(f"in_{name}", v.shape, mybir.dt.from_np(v.dtype), kind="ExternalInput").ap()
    out = nc.dram_tensor("out", _OUT, F32, kind="ExternalOutput").ap()
    build(nc, args, out)
    return run_bass_kernel_spmd(nc, [arrays], core_ids=[0]).results[0]["out"]
```

```python
from contextlib import ExitStack

import numpy as np
import concourse.bass as bass
from concourse import mybir

F32 = mybir.dt.float32
F32R = mybir.dt.float32r
I32 = mybir.dt.int32
ALU = mybir.AluOpType
ACT = mybir.ActivationFunctionType
AX_X = mybir.AxisListType.X
ds = bass.ds

P = 128
L = 256
TT = L // P
D = 2048
KT = D // P
DH = 128
HEADS = 8
D_A = HEADS * DH
IDX_HEADS, IDX_DIM, TOPK = 16, 64, 64
IDX_COL = 4 * D_A
KW_COL = IDX_COL + IDX_HEADS * IDX_DIM
KW = IDX_DIM + IDX_HEADS
B_COL = KW_COL + KW
EPS = 1e-6
NEG = -1e30
SPAN = P + L

NSLOT = 4
PK = 4
PIECES = KT // PK
CH = 512

RW = 1024
NP_ = 8
N = 64
C = 64
NCH = L // C
WAG_COL = 3 * RW
WAG = 64 + 64 + 160
CQ_COL = WAG_COL + WAG
LORA = 512
ROPE = 64
FF = 5632
FT = FF // P
GN_EPS = 64e-5

VEC = {}


def _place():
    groups = [
        [("c", 16), ("b_ada", 48), ("g_norm", 16), ("attn_norm_g_2", 16), ("ffn_norm_g_2", 16),
         ("q_norm_a", 1), ("k_norm_a", 1), ("q_norm_b", 1), ("k_norm_b", 1),
         ("mla_q_norm_g_2", 4), ("mla_kv_norm_g_2", 4)],
        [("rwkv_mu_2", 27), ("rwkv_w0_2", 8), ("rwkv_a0_2", 8), ("rwkv_k_k_2", 8), ("rwkv_k_a_2", 8),
         ("rwkv_r_k_2", 8), ("rwkv_gn_w_2", 8), ("rwkv_gn_b_2", 8), ("ffn_conv_b_2", 44)],
        [("conv0", 44), ("conv1", 44)],
        [("conv2", 44)],
    ]
    for g, names in enumerate(groups):
        row = 0
        for name, rows in names:
            VEC[name] = (g, row, rows)
            row += rows
    return [sum(r for _, r in names) for names in groups]


GROUP_ROWS = _place()


class Chain:

    def __init__(self, eng, sem):
        self.eng, self.sem, self.n, self.i, self.per = eng, sem, 0, None, 0

    def value(self):
        return self.n if self.i is None else self.i * self.per + self.n

    def mark(self, ins):
        ins.then_inc(self.sem, 1)
        self.n += 1
        return ins

    def wait(self):
        self.eng.wait_ge(self.sem, self.value())

    def link(self, ins):
        self.mark(ins)
        self.wait()

    def enter(self, i, per):
        self.i, self.per, self.start = i, per, self.n

    def leave(self, times):
        assert self.n - self.start == self.per, (self.n - self.start, self.per)
        self.n, self.i = self.start + self.per * times, None


class Steps:

    def __init__(self, sem, names):
        self.sem, self.names, self.at = sem, names, 0

    def mark(self, ins, name):
        assert self.names[self.at % len(self.names)] == name, (self.names[self.at % len(self.names)], name)
        self.at += 1
        ins.then_inc(self.sem, 1)

    def wait(self, eng, name, step):
        eng.wait_ge(self.sem, step * len(self.names) + (self.names.index(name) + 1))


def build(nc, a, out):
    ctx = ExitStack()
    with ctx:
        def sb(name, *shape, dt=F32):
            return ctx.enter_context(nc.sbuf_tensor(name, [P, *shape], dt))

        def sem(name):
            return ctx.enter_context(nc.semaphore(name))

        BANK = [ctx.enter_context(nc.psum_tensor(f"bank{i}", [P, 512], F32)) for i in range(8)]

        base = (nc.sbuf_base + 31) // 32 * 32
        ctx.enter_context(nc.sbuf_tensor("slab", [P, 52944], F32))

        def sb(name, off, *shape, dt=F32):
            return nc.alloc_sbuf_tensor_at(name, [P, *shape], dt, offset=base + 4 * off)

        X = sb("X", 0, TT, D)
        WR = sb("WR", 4096, NSLOT, PK * CH)
        WL = sb("WL", 4096, NSLOT, PK * CH, dt=F32R)
        WH = sb("WH", 12288, 2, PK * CH, dt=F32R)
        HX = sb("HX", 16384, 2, KT, L, dt=F32R)
        HH, HL = HX[:, 0], HX[:, 1]
        CSH = sb("CSH", 16384, KT, P, dt=F32R)
        CSL = sb("CSL", 18432, KT, P, dt=F32R)
        bgate_row = sb("bgate_row", 20480, D)[:, :]
        YR = sb("YR", 20480, 8, L)
        cols = sb("cols", 24576, 4 * P)
        ident = sb("ident", 25088, P)
        level0T = sb("level0T", 25216, P)[:]
        small = sb("small", 25344, 512)
        masks = sb("masks", 25856, 1216)
        causal_dist = masks[:, 0:SPAN]
        causal_mask = masks[:, SPAN:2 * SPAN]
        bias_a = masks[:, 2 * SPAN:3 * SPAN]
        slope = sb("slope", 27072, 2 * HEADS)
        ARENA = 25600
        arena = sb("arena", 27088, ARENA)
        diag = sb("diag", 52688, TT, P)

        used = [0]

        def at(off, *shape):
            n = int(np.prod(shape))
            assert off + n <= ARENA, (off, n)
            v = arena[:, off:off + n]
            used[0] = off + n
            if len(shape) == 1:
                return v
            names = "abcd"[:len(shape)]
            return v.rearrange(f"p ({' '.join(names)}) -> p {' '.join(names)}",
                               **{m: s for m, s in zip(names[1:], shape[1:])})

        def col(name, j=0, n=1):
            g, row, _ = VEC[name]
            return cols[:, g * P + row + j:g * P + row + j + n]

        mod = small[:, 0:48]
        cs = small[:, 48:64]
        gs = small[:, 64:80]
        qgain = small[:, 80:84]
        ss = small[:, 84:86]
        rstd = small[:, 86:88]
        sq4 = small[:, 88:96]
        nmax = small[:, 104:104 + 32]
        rowsum = small[:, 136:136 + 32]
        rsum_inv = small[:, 168:168 + 32]
        hss = small[:, 200:216]
        hrstd = small[:, 216:232]
        top8 = small[:, 232:248].rearrange("p (t e) -> p t e", t=TT)
        cnt = small[:, 248:250]
        need = small[:, 250:252]
        kss = small[:, 252:254]
        krstd = small[:, 254:256]

        V1 = at(0, 2, TT, D_A)
        Z1 = at(4096, 2, TT, D_A)
        QT = at(8192, 2, HEADS, L)
        KTT = at(12288, 2, HEADS, L)
        XN = at(8192, TT, D)
        rows = at(16384, 4, P)
        stage = at(16896, 2, TT, CH)
        square = at(18944, TT, CH)
        QI = at(19968, 8, L)
        S_sb = at(16896, 2, SPAN)
        Pr = at(17664, 2, SPAN)
        PTs = at(18432, 2, SPAN)
        KI = at(22016, TT, KW)
        KIT = at(23200, L)
        KIX = at(22176, TT, 2, P)
        KB = at(22688, 2, L)
        relu = at(23200, 2, CH)
        score = at(24224, SPAN)
        work = at(24608, SPAN)
        kin_g = at(24992, IDX_DIM)
        xT = at(0, KT, L)
        c_rows = at(16896, P)
        gate_row = at(19968, D)
        wo_tmp = at(10752, 2, CH)
        hf1 = at(16896, 2, 2, L)

        RKV = at(0, 24, L)
        HWA, HG0, HG1 = (at(6144 + 256 * i, L) for i in range(3))
        RAW = at(7168, 4, L + 1)
        SH = at(8196, 4, L)
        S2, Pr2, PT2 = at(7168, 2, SPAN), at(7936, 2, SPAN), at(8704, 2, SPAN)
        CQ = at(9472, 4, LORA)
        YM = at(9472, TT, 1024)
        KPE = at(11520, TT, ROPE)
        CT = at(11648, 8, L)
        QN = at(13696, HEADS, L)
        KN = at(15744, HEADS, L)
        VM = at(17792, TT, 1024)
        QPE = at(19840, TT, 512)
        QPR = at(20864, TT, 512)
        QPT = at(21888, 4, L)
        KPX = at(22912, TT, 2, P)
        KPT = at(23424, 2, L)
        ang = at(23936, 2, TT, 32)
        turns = at(24064, 2, TT, 32)
        inv_freq = at(24192, 32)
        rope_tmp = at(24224, 4, 256)
        pos_i = arena[:, 25248:25250].bitcast(I32)
        pos = at(25250, 2)
        XN2 = at(13696, TT, D)
        hf2 = at(17792, 2, 2, L)
        cstat = small[:, 256:260]
        crstd = small[:, 260:264]

        half1 = sb("half1", 11264, 7168)
        Lw = YR
        El = half1[:, 5120:7168].rearrange("p (f n) -> p f n", f=8)
        KKn = sb("KKn", 18432, 8, L)
        Bv = sb("Bv", 22528, 8, L)
        sqk = half1[:, 1024:3072].rearrange("p (f n) -> p f n", f=8)
        EXr = half1[:, 3072:5120].rearrange("p (f n) -> p f n", f=8)
        kfac = half1[:, 3072:4096].rearrange("p (f n) -> p f n", f=4)
        chunk_start = at(25252, L)
        YMT = at(7168, 8, L)
        half1_flat = [half1[:, 512 * i:512 * (i + 1)] for i in range(14)] + [at(24064, 512)]
        spare = WR[:, 1, :]
        w4 = [[spare[:, 512 * i:512 * (i + 1)].rearrange("p (q n) -> p q n", q=4) for i in range(3)]
              + [at(15360 + 512 * i, 4, P) for i in range(3, 15)],
              [v.rearrange("p (q n) -> p q n", q=4) for v in half1_flat]]
        a_bd, b_bd, k_bd, r_bd, v_bd, y_bd, LT, AkT, BrT, KrT, b_tok, k_tok, Xi, Zi, T2 = zip(*w4)
        n4 = [[at(23040 + 256 * i, 4, N) for i in range(4)], [at(24576 + 256 * i, 4, N) for i in range(4)]]
        P1, Us, Vp, ST = zip(*n4)
        pairs_zero = [at(15360 + 3 * 512, 3 * 512), half1[:, 0:6 * 512]]
        RK = WR[:, 2, :].rearrange("p (f n) -> p f n", f=8)
        level = [masks[:, P * i:P * (i + 1)] for i in range(3)] + [spare[:, 1536 + P * i:1536 + P * (i + 1)] for i in range(3)]
        below, upto_diag = masks[:, 768:896], masks[:, 896:1024]
        I2 = masks[:, 1024:1088]
        head_ones = masks[:, 1088:1216]
        head_cols = head_ones.rearrange("p (h m) -> p h m", h=2)[:, :, 0]
        end_s = small[:, 264:296].rearrange("p (f c) -> p f c", c=NCH)
        mid_s = small[:, 296:328].rearrange("p (f c) -> p f c", c=NCH)
        fac = small[:, 328:360].rearrange("p (f c) -> p f c", c=NCH)
        one_ka = small[:, 360:368]
        y_scale = small[:, 368:368 + 2 * 2 * NP_]
        YQ = at(9216, 8, L)
        y_wide = at(9216, TT, NP_, P)
        BV = at(11264, 8, L)
        DECAY = float(np.exp(-0.5))

        AC = at(0, FT, L)
        RAWF = at(11264, 4, L + 2)
        CV = at(12296, 4, L)
        UPS = at(16384, 4, L)
        XN3 = at(16384, TT, D)
        fg_row = at(20480, D)
        hf4 = at(0, 2, 2, L)
        AH = sb("AH", 27088 + 22528, 2, PK, L, dt=F32R)
        AL = sb("AL", 27088 + 13824, 2, PK, L, dt=F32R)

        piece_in = [sem(f"piece_in{s}") for s in range(NSLOT)]
        piece_done = sem("piece_done")
        lo_ready_dve = sem("lo_ready_dve")
        half_done = sem("half_done")
        act_took = sem("act_took")
        x_in, params_in = sem("x_in"), sem("params_in")
        rows_clear, consts_set = sem("rows_clear"), sem("consts_set")
        pool_chain, dve_chain_s, act_chain_s = sem("pool_chain"), sem("dve_chain"), sem("act_chain")
        colsT_ready, cols_ready = sem("colsT_ready"), sem("cols_ready")
        cs_ready = sem("cs_ready")
        mod_ready = sem("mod_ready")
        ssq_ready, var_ready, rstd_ready, xn_ready = sem("ssq_ready"), sem("var_ready"), sem("rstd_ready"), sem("xn_ready")
        xT_ready, xT_taken = sem("xT_ready"), sem("xT_taken")
        kiT_taken, ki_ready = sem("kiT_taken"), sem("ki_ready")
        ki_var, ki_rstd, kix_ready, kixT_ready, kb_ready = map(sem, ["ki_var", "ki_rstd", "kix_ready", "kixT_ready", "kb_ready"])
        idx_ready, relu_ready, relu_used = sem("idx_ready"), sem("relu_ready"), sem("relu_used")
        head_var, head_rstd, head_normed, headT_ready, headT_taken = map(
            sem, ["head_var", "head_rstd", "head_normed", "headT_ready", "headT_taken"])
        scores_ready, scores_biased, max_ready, probs_ready = map(
            sem, ["scores_ready", "scores_biased", "max_ready", "probs_ready"])
        probsT_ready, probsT_taken, out_ready, out_taken = map(
            sem, ["probsT_ready", "probsT_taken", "out_ready", "out_taken"])
        row_took, bgate_in, c_in, cT_ready, x_scaled = map(sem, ["row_took", "bgate_in", "c_in", "cT_ready", "x_scaled"])
        x_updated = sem("x_updated")
        stored = sem("stored")
        hi_ready, lo_ready, ht_ready, a_ready, cs_split = map(
            sem, ["hi_ready", "lo_ready", "ht_ready", "a_ready", "cs_split"])
        raw_taken, wag_ready = sem("raw_taken"), sem("wag_ready")
        pos_in, fg_in = sem("pos_in"), sem("fg_in")
        ang_ready, trig_ready = sem("ang_ready"), sem("trig_ready")
        c_sq, c_var, c_rstd, c_normed, kpx_ready, qpr_ready = map(
            sem, ["c_sq", "c_var", "c_rstd", "c_normed", "kpx_ready", "qpr_ready"])
        lora_ready = sem("lora_ready")
        masks_free, rw_masks, rw_mid = sem("masks_free"), sem("rw_masks"), sem("rw_mid")
        pairs_cleared = sem("pairs_cleared")
        decay_summed, exc_ready, ex_ready, en_ready = map(
            sem, ["decay_summed", "exc_ready", "ex_ready", "en_ready"])
        kk_raw = sem("kk_raw")
        k_mod, rk_raw, kk_ready, ops_ready = map(sem, ["k_mod", "rk_raw", "kk_ready", "ops_ready"])
        pool_step = sem("pool_step")
        y_centred, y_sq, y_var, y_rstd_sq, y_normed, y_scaled, y_sum, y_hi = map(
            sem, ["y_centred", "y_sq", "y_var", "y_rstd_sq", "y_normed", "y_scaled", "y_sum", "y_hi"])
        rw_small, rw_small_took, kk_sq, kk_sum, kk_var, kk_rstd = map(
            sem, ["rw_small", "rw_small_took", "kk_sq", "kk_sum", "kk_var", "kk_rstd"])
        fac_raw, fac_ready = sem("fac_raw"), sem("fac_ready")
        pe_step, act_step, dve_step = sem("pe_step"), sem("act_step"), sem("dve_step")
        rk_ready, bonus_ready, bonus_took, g_ready, g_took = map(
            sem, ["rk_ready", "bonus_ready", "bonus_took", "g_ready", "g_took"])
        conv_ready, gate_act, up_taken = sem("conv_ready"), sem("gate_act"), sem("up_taken")
        fin_ready = sem("fin_ready")

        def attention_pe(pe, heads, base, qk, v, Pr, PTs, beside=lambda h: None):
            def scores(h):
                if h >= 2:
                    pe.wait_ge(scores_biased, base + h - 1)
                for t in range(TT):
                    o = BANK[4 + h % 2][:, t * P:t * P + (t + 1) * P]
                    parts = qk(h, t)
                    for n, (q, k) in enumerate(parts):
                        last = pe.matmul(o, q, k, start=(n == 0), stop=(n == len(parts) - 1))
                last.then_inc(scores_ready, 1)

            scores(0)
            scores(1)
            for h in range(heads):
                pe.wait_ge(probs_ready, 2 * (base + h + 1))
                if h >= 2:
                    pe.wait_ge(probsT_taken, base + h - 1)
                for n, c0 in enumerate((0, P, 2 * P)):
                    last = pe.transpose(BANK[2 + h % 2][:, n * P:(n + 1) * P], Pr[:, h % 2, c0:c0 + P], ident[:])
                last.then_inc(probsT_ready, 1)
                if h + 2 < heads:
                    scores(h + 2)
                beside(h)
                pe.wait_ge(probsT_taken, base + h + 1)
                if h >= 2:
                    pe.wait_ge(out_taken, 2 * (base + h - 1))
                o = BANK[6 + h % 2]
                pt = PTs[:, h % 2]
                pe.matmul(o[:, 0:DH], pt[:, 0:P], v(h, 0), start=True, stop=True)
                pe.matmul(o[:, DH:2 * DH], pt[:, P:2 * P], v(h, 0), start=True, stop=False)
                pe.matmul(o[:, DH:2 * DH], pt[:, 2 * P:3 * P], v(h, 1), start=False, stop=True) \
                    .then_inc(out_ready, 1)

        def attention_act(act, heads, base, S_sb, Pr, PTs, beside=lambda h: None):
            def exps(h):
                act.wait_ge(max_ready, 2 * (base + h + 1))
                if base + h >= 2:
                    act.wait_ge(probsT_ready, base + h - 1)
                for t, (c0, w) in enumerate(((0, P), (P, L))):
                    act.activation(Pr[:, h % 2, c0:c0 + w], S_sb[:, h % 2, c0:c0 + w], ACT.Exp,
                                   bias=nmax[:, 2 * h + t:2 * h + t + 1],
                                   accum_out=rowsum[:, 2 * h + t:2 * h + t + 1]).then_inc(probs_ready, 1)

            def turn(h):
                act.wait_ge(probsT_ready, base + h + 1)
                if base + h >= 2:
                    act.wait_ge(out_ready, base + h - 1)
                act.activation(PTs[:, h % 2, :], BANK[2 + h % 2][:, 0:SPAN], ACT.Copy).then_inc(probsT_taken, 1)

            for h in range(heads):
                exps(h)
                if h >= 1:
                    turn(h - 1)
                    beside(h - 1)
            turn(heads - 1)
            beside(heads - 1)

        def attention_dve(dve, own, heads, base, bias, coef, emit, S_sb, beside=lambda h: None):
            def maxima(h):
                dve.wait_ge(scores_ready, base + h + 1)
                if base + h >= 2:
                    dve.wait_ge(probs_ready, 2 * (base + h - 1))
                dve.scalar_tensor_tensor(out=S_sb[:, h % 2, :], in0=bias(h), scalar=coef(h),
                                         in1=BANK[4 + h % 2][:, 0:SPAN], op0=ALU.mult,
                                         op1=ALU.add).then_inc(scores_biased, 1)
                dve.wait_ge(scores_biased, base + h + 1)
                for t, (c0, w) in enumerate(((0, P), (P, L))):
                    dve.tensor_reduce(nmax[:, 2 * h + t:2 * h + t + 1], S_sb[:, h % 2, c0:c0 + w], AX_X, ALU.max,
                                      negate=True).then_inc(max_ready, 1)

            def finish(h):
                dve.wait_ge(probs_ready, 2 * (base + h + 1))
                own.link(dve.reciprocal(rsum_inv[:, 2 * h:2 * h + 2], rowsum[:, 2 * h:2 * h + 2]))
                dve.wait_ge(out_ready, base + h + 1)
                for t in range(TT):
                    emit(h, t, BANK[6 + h % 2][:, t * DH:(t + 1) * DH],
                         rsum_inv[:, 2 * h + t:2 * h + t + 1]).then_inc(out_taken, 1)

            for h in range(heads):
                maxima(h)
                if h >= 2:
                    finish(h - 2)
                    beside(h - 2)
            finish(heads - 2)
            finish(heads - 1)

        PARAMS = [(n, n) for n in VEC if not n.startswith("conv")]
        PARAM_DMAS = len(PARAMS) + 1 + 3 + 1

        block = ctx.enter_context(nc.Block())

        RAW_C = 4 * 6 + 3
        ACT_GATE, ACT_RKV = 38, 42
        NADA = 2 * D // CH
        n_ada = 0
        n_kw = n_ada + PIECES * NADA
        n_qi = n_kw + 1
        n_br = n_qi + 2 * PIECES
        n_gate = n_br + 16 * PIECES
        n_wo = n_gate + 4 * PIECES
        n_rkv = n_wo + 4 * PIECES
        n_wag = n_rkv + 6 * PIECES
        n_c = n_wag + PIECES
        n_low = n_c + 3 * PIECES
        n_uq = n_low + 2
        n_ukv = n_uq + 4
        n_g2 = n_ukv + 4
        n_wo2 = n_g2 + 2
        n_gu = n_wo2 + 4 * PIECES
        n_dn = n_gu + 2 * (FF // CH) * PIECES
        UNSPLIT = n_wo2 - n_low

        C_WIDTH = (384, 384, 320)
        C_PARTS = [[((0, 384), 0, (0, 384))],
                   [((0, 128), 0, (384, 512)), ((128, 384), 1, (0, 256))],
                   [((0, 256), 1, (256, 512)), ((256, 320), 2, (0, 64))]]

        def width_of(n):
            if n == n_kw:
                return P
            if n_c <= n < n_low:
                return C_WIDTH[(n - n_c) // PIECES]
            if n_wag <= n < n_wag + PIECES:
                return 3 * P
            return CH

        def tiles_of(n):
            return KT if n == n_kw else PK

        def nth(n):
            return n if n < n_wo2 else n - UNSPLIT

        n_end = n_dn + 4 * (FT // PK)

        def shared(n):
            return n < n_kw or n >= n_dn

        LOW_BANK = (0, 1, 2, 3)

        def lows_before(n):
            split = [m for m in range(n) if not n_low <= m < n_wo2]
            both = sum(shared(m) for m in split)
            return 2 * len(split) - both, both

        def low_part(eng, n, s, more, ready):
            w = (s, width_of(n), tiles_of(n))
            eng.wait_ge(hi_ready, more * 2 + (2 * nth(n) + s + 1))
            eng.tensor_tensor(half(WL, n % NSLOT, *w), half(WR, n % NSLOT, *w), half(WH, nth(n) % 2, *w),
                              ALU.subtract).then_inc(ready, 1)

        LEVELS = 6

        def both(*names):
            return [f"{n}_{s}" for s in range(2) for n in names]

        levels_pe, levels_dve = [], []
        for m in range(1, LEVELS):
            xz = ([f"X{m}"] if m < LEVELS - 1 else []) + [f"Z{m}"]
            levels_pe += both(f"T{m}") + (both("P1") if m == 3 else []) + both(*xz)
            levels_dve += both(f"T{m}") + both(*xz)
        pe_names = (both("LT") + both("btok", "ktok") + both("AkT") + both("T0") + both("Vp") + both("BrT") + both("KrT")
                    + levels_pe + both("U") + both("Y", "S") + both("YT"))
        act_names = both("btok", "ktok") + both("Vp") + both("P1") + both("U") + both("y0", "y1") + both("YT")
        dve_names = (both("LT") + both("AkT") + both("T0", "X0", "Zm", "Z0") + both("BrT") + both("KrT") + levels_dve
                     + both("Ssum", "S"))
        pool_names = [f"{x}{h}_{s}" for x in "bakvr" for s in range(2) for h in range(2)]

        def view(tensor, at_slot, width, k=PK):
            return tensor[:, at_slot, :].rearrange("p (k n) -> p k n", k=k)[:, :, 0:width]

        def half(tensor, at_slot, s, width, k):
            return view(tensor, at_slot, width, k)[:, s * k // 2:(s + 1) * k // 2, :]

        @block.sync
        def _(sp):
            def load(n, src, width, k=PK, shift=0):
                if n >= NSLOT or not isinstance(shift, int):
                    sp.wait_ge(piece_done, shift + (n - NSLOT + 1))
                sp.dma_start(view(WR, n % NSLOT, width, k), src).then_inc(piece_in[n % NSLOT], 16)

            def chunk(n, w, c0, width, shift=0):
                for q in range(PIECES):
                    src = w[q * PK * P:(q + 1) * PK * P, ds(c0, width)]
                    load(n + q, src.rearrange("(k p) n -> p k n", p=P), width, shift=shift)

            w_ada, w_in, w_out = a["w_ada"][0], a["w_in"][0], a["w_out"][0]
            chunk(n_ada, w_ada, 0, CH)
            sp.wait_ge(rows_clear, 1)
            for name, _ in PARAMS:
                g, row, r = VEC[name]
                v = a[name]
                if len(v.shape) == 3:
                    v = v.rearrange("o a b -> o (a b)")
                v = v[0]
                if name == "rwkv_mu_2":
                    for r0, rn, c0, w in ((0, 26, 0, P), (26, 1, 26 * P, 32)):
                        sp.dma_start(rows[row + r0:row + r0 + rn, g, 0:w],
                                      v[c0:c0 + rn * w].rearrange("(a n) -> a n", a=rn)).then_inc(params_in, 16)
                else:
                    sp.dma_start(rows[row:row + r, g, :], v.rearrange("(a n) -> a n", n=P)).then_inc(params_in, 16)
            for tap in range(3):
                g, row, r = VEC[f"conv{tap}"]
                sp.dma_start(rows[row:row + r, g, :],
                              a["ffn_conv_w_2"][0, tap, :].rearrange("(a n) -> a n", n=P)).then_inc(params_in, 16)
            sp.dma_start(kin_g, a["k_norm_idx"][0:1, :].to_broadcast([P, IDX_DIM])).then_inc(params_in, 16)
            with sp.Fori(1, NADA) as i:
                chunk(n_ada, w_ada, i * CH, CH, shift=i * PIECES)
            load(n_kw, w_in[:, KW_COL:KW_COL + P].rearrange("(k p) n -> p k n", p=P), P, KT)
            for j in range(2):
                chunk(n_qi + PIECES * j, w_in, IDX_COL + j * CH, CH)
            with sp.Fori(0, 2) as b, sp.Fori(0, 8) as j:
                chunk(n_br, w_in, b * B_COL + j * CH, CH, shift=b * (8 * PIECES) + j * PIECES)
            with sp.Fori(0, 4) as i:
                chunk(n_gate, w_ada, i * CH + 2 * D, CH, shift=i * PIECES)
            with sp.Fori(0, 4) as i:
                chunk(n_wo, w_out, i * CH, CH, shift=i * PIECES)
            w_in2, w_uq, w_ukv = a["w_in_2"][0], a["mla_w_uq_2"][0], a["mla_w_ukv_2"][0]
            with sp.Fori(0, 6) as i:
                chunk(n_rkv, w_in2, i * CH, CH, shift=i * PIECES)
            chunk(n_wag, w_in2, WAG_COL, 3 * P)
            for j in range(3):
                chunk(n_c + PIECES * j, w_in2, CQ_COL + sum(C_WIDTH[:j]), C_WIDTH[j])

            def low_rank(n, name, p0, r0, r):
                sp.wait_ge(piece_done, n - NSLOT + 1)
                sp.dma_start(WR[p0:p0 + r, n % NSLOT, 0:RW], a[name][0, r0:r0 + r, :]).then_inc(piece_in[n % NSLOT], 16)

            low_rank(n_low, "rwkv_w2_2", 0, 0, 64)
            low_rank(n_low + 1, "rwkv_a2_2", 64, 0, 64)
            for n, w, width in ((n_uq, w_uq, 2 * (DH + ROPE)), (n_ukv, w_ukv, 4 * DH)):
                for j in range(4):
                    load(n + j, w[:, j * width:(j + 1) * width].rearrange("(k p) n -> p k n", p=P), width)
            low_rank(n_g2, "rwkv_g2_2", 0, 0, P)
            low_rank(n_g2 + 1, "rwkv_g2_2", 0, P, 32)
            Steps(dve_step, dve_names).wait(sp, "S_1", NCH - 1)
            for c in range(4):
                for m, q in enumerate((2, 3, 0, 1)):
                    if c == 0 and m == 1:
                        sp.wait_ge(bonus_ready, 4)
                    src = a["w_out_2"][0][q * PK * P:(q + 1) * PK * P, c * CH:(c + 1) * CH]
                    load(n_wo2 + PIECES * c + m, src.rearrange("(k p) n -> p k n", p=P), CH)
            with sp.Fori(0, FF // CH) as i:
                for j, w in enumerate(("ffn_w_gate_2", "ffn_w_up_2")):
                    chunk(n_gu + PIECES * j, a[w][0], i * CH, CH, shift=i * (2 * PIECES))
            wd = a["ffn_w_down_2"][0]
            with sp.Fori(0, FT // PK) as i:
                for c in range(4):
                    src = wd[ds(i * (PK * P), PK * P), c * CH:(c + 1) * CH]
                    load(n_dn + c, src.rearrange("(k p) n -> p k n", p=P), CH, shift=i * PIECES)
            for s in range(2):
                for t in range(TT):
                    sp.wait_ge(fin_ready, TT * s + t + 1)
                    o = slice(s * D // 2, (s + 1) * D // 2)
                    sp.dma_start(out[0, t * P:(t + 1) * P, o], XN3[:, t, o]).then_inc(stored, 16)
            sp.wait_ge(stored, 16 * 2 * TT)

        @block.gpsimd
        def _(pool):
            own = Chain(pool, pool_chain)
            pool.memset(rows[:, :, :], 0.0).then_inc(rows_clear, 1)
            own.link(pool.memset(ident[:], 0.0))
            pool.affine_select(out=ident[:], in_=ident[:], compare_op=ALU.not_equal, fill=1.0, base=0,
                               pattern=[[-1, P]], channel_multiplier=1).then_inc(consts_set, 1)
            for t, (c0, w) in enumerate(((0, P), (P, L))):
                own.mark(pool.iota(causal_dist[:, c0:c0 + w], pattern=[[1, w]], base=-t * P,
                                   channel_multiplier=-1, allow_small_or_imprecise_dtypes=True))
            own.link(pool.memset(causal_mask, 0.0))
            for t, (c0, w) in enumerate(((0, P), (P, L))):
                for m in (causal_dist, causal_mask):
                    pool.affine_select(out=m[:, c0:c0 + w], in_=m[:, c0:c0 + w], compare_op=ALU.is_ge,
                                       fill=NEG, base=t * P, pattern=[[-1, w]],
                                       channel_multiplier=1).then_inc(consts_set, 1)
            for h in range(2 * HEADS):
                pool.memset(slope[:, h:h + 1], float(np.float32(2.0 ** (-8.0 * (h % HEADS + 1) / HEADS)))) \
                    .then_inc(consts_set, 1)
            pool.memset(KIX[:, :, :, :], 0.0).then_inc(consts_set, 1)

            def low(n, more=0):
                for s in range(1 if shared(n) else 2):
                    low_part(pool, n, s, more, lo_ready)

            def lows(first, end):
                with pool.Fori(0, (end - first) // PIECES) as i:
                    for q in range(PIECES):
                        low(first + q, i * PIECES)

            lows(n_ada, n_kw)
            low(n_kw)
            lows(n_qi, n_wag)
            for n in range(n_wag, n_low):
                low(n)
            own.link(pool.memset(masks[:, 0:3 * P], 0.0))
            own.link(pool.memset(masks[:, 768:1024], 1.0))
            own.link(pool.memset(level0T, 0.0))
            own.link(pool.memset(I2, 0.0))
            own.link(pool.memset(head_ones, 0.0))

            def level_mask(m):
                b = 1 << m
                v = level[m].rearrange("p (j two m) -> p j two m", two=2, m=b)[:, :, 0, :]
                nb = P // (2 * b)
                own.link(pool.memset(v, 1.0))
                own.link(pool.affine_select(out=v, in_=v, compare_op=ALU.is_ge, fill=0.0, base=-b,
                                            pattern=[[-2 * b, nb], [0, b]], channel_multiplier=1))
                own.link(pool.affine_select(out=v, in_=v, compare_op=ALU.is_ge, fill=0.0, base=2 * b - 1,
                                            pattern=[[2 * b, nb], [0, b]], channel_multiplier=-1))

            for m in range(3):
                level_mask(m)
            v = level0T.rearrange("p (j two) -> p j two", two=2)[:, :, 1]
            own.link(pool.affine_select(out=v, in_=v, compare_op=ALU.not_equal, fill=1.0, base=0,
                                        pattern=[[-2, P // 2]], channel_multiplier=1))
            own.link(pool.affine_select(out=below, in_=below, compare_op=ALU.is_gt, fill=0.0, base=0,
                                        pattern=[[1, P]], channel_multiplier=-1))
            own.link(pool.affine_select(out=upto_diag, in_=upto_diag, compare_op=ALU.is_ge, fill=0.0, base=0,
                                        pattern=[[1, P]], channel_multiplier=-1))
            own.link(pool.affine_select(out=I2, in_=I2, compare_op=ALU.not_equal, fill=1.0, base=0,
                                        pattern=[[-1, N]], channel_multiplier=1))
            own.link(pool.affine_select(out=I2, in_=I2, compare_op=ALU.not_equal, fill=1.0, base=-N,
                                        pattern=[[-1, N]], channel_multiplier=1))
            for h in range(2):
                own.link(pool.memset(head_ones[h * N:(h + 1) * N, h * N:(h + 1) * N], 1.0))
            own.link(pool.memset(chunk_start, 1.0))
            pool.memset(chunk_start.rearrange("p (c t) -> p c t", t=C)[:, :, 0], 0.0).then_inc(rw_masks, 1)
            R_, K_, V_ = RKV[:, 0:8], RKV[:, 8:16], RKV[:, 16:24]
            pool.wait_ge(rw_small_took, 16)
            pool.wait_ge(piece_done, n_low)
            pool.wait_ge(kk_raw, 1)
            for q in range(2):
                for f in range(4):
                    k = 4 * q + f
                    own.mark(pool.tensor_scalar(kfac[:, f, :], Bv[:, k, :], col("rwkv_k_a_2", k), one_ka[:, k:k + 1],
                                                ALU.mult, ALU.add))
                own.wait()
                own.mark(pool.tensor_tensor(K_[:, 4 * q:4 * q + 4, :], K_[:, 4 * q:4 * q + 4, :], kfac, ALU.mult))
                own.wait()
            pool.memset(small[:, 507:508], 0.0).then_inc(k_mod, 1)
            pool.wait_ge(piece_done, n_g2)
            own.mark(pool.tensor_tensor(RK, R_, K_, ALU.mult))
            own.wait()
            pool.memset(small[:, 501:502], 0.0).then_inc(rk_raw, 1)
            pool.wait_ge(piece_done, n_g2)
            pool.wait_ge(kk_ready, 1)
            own.link(pool.memset(pairs_zero[1], 0.0))
            own.link(pool.memset(spare[:, 0:1536 + 3 * P], 0.0))
            for m in range(3, LEVELS):
                level_mask(m)
            L_ = Steps(pool_step, pool_names)
            P_ = Steps(pe_step, pe_names)

            def pair_blocks(c, last=None):
                for i, (nm, dst, src, user) in enumerate((("b", b_bd, Bv, "BrT"), ("a", a_bd, KKn, "P1"),
                                                          ("k", k_bd, K_, "KrT"), ("v", v_bd, V_, "Vp"),
                                                          ("r", r_bd, R_, "Y"))):
                    if last is None and nm == "v":
                        L_.wait(pool, "k1_1", 0)
                        pool.wait_ge(masks_free, 1)
                        pool.memset(pairs_zero[0], 0.0).then_inc(pairs_cleared, 1)
                        pool.wait_ge(pairs_cleared, 1)
                    for s in range(2):
                        if last is None:
                            pool.wait_ge(ops_ready, i + 1)
                        else:
                            P_.wait(pool, f"{user}_{s}", last)
                        for h in range(2):
                            o = slice(h * N, (h + 1) * N)
                            cols_ = ds(c * C, C)
                            L_.mark(pool.tensor_copy(dst[s][o, :, o], src[o, 4 * s:4 * s + 4, cols_]), f"{nm}{h}_{s}")

            pair_blocks(0)
            L_.wait(pool, "r1_1", 0)
            for f in range(8):
                ins = pool.tensor_scalar(RK[:, f, :], RK[:, f, :], col("rwkv_r_k_2", f), None, ALU.mult)
            ins.then_inc(rk_ready, 1)
            pool.wait_ge(rk_ready, 1)
            with pool.Fori(1, NCH) as c:
                pair_blocks(c, c - 1)
            for g in range(4):
                k = slice(8 + 2 * g, 10 + 2 * g)
                pool.wait_ge(y_hi, g + 1)
                pool.tensor_tensor(HL[:, k, :], YMT[:, 2 * g:2 * g + 2, :], HH[:, k, :], ALU.subtract).then_inc(ht_ready, 1)
            lows(n_wo2, n_dn)
            lows(n_dn, n_end)
        CONSTS = 1 + 4 + 2 * HEADS + 1

        @block.tensor
        def _(pe):
            def split(n, k, more=0, pk=PK):
                by_pool, by_dve = lows_before(n)
                if k == pk // 2 and shared(n):
                    pe.wait_ge(lo_ready_dve, more + (by_dve + 1))
                elif k % (pk // 2) == 0:
                    pe.wait_ge(lo_ready, more * (1 if shared(n) else 2) + (by_pool + k // (pk // 2) + 1))

            def done(k, last, pk=PK):
                if k == pk // 2 - 1:
                    last.then_inc(half_done, 1)
                elif k == pk - 1:
                    last.then_inc(piece_done, 1)

            def arrived(n):
                pe.wait_ge(piece_in[n % NSLOT], 16 * (n // NSLOT + 1))

            def product(out, stat, mov, start, stop):
                pe.matmul(out, stat[0], mov[0], start=start, stop=False, skip_group_check=True)
                pe.matmul(out, stat[0], mov[1], start=False, stop=False, skip_group_check=True)
                return pe.matmul(out, stat[1], mov[0], start=False, stop=stop, skip_group_check=True)

            def tok_chunk(n, pair, width, more=0, begin=lambda kk: None, rot=0):
                for q in range(PIECES):
                    wh, wl = view(WH, nth(n + q) % 2, width), view(WL, (n + q) % NSLOT, width)
                    for k in range(PK):
                        kk = q * PK + k
                        begin(kk)
                        split(n + q, k, more)
                        for t in range(TT):
                            o = slice(t * P, (t + 1) * P)
                            last = product(BANK[2 * pair + t][:, 0:width], (HH[:, (kk + rot) % KT, o], HL[:, (kk + rot) % KT, o]),
                                           (wh[:, k, :], wl[:, k, :]), kk == 0, kk == KT - 1)
                        done(k, last)

            def feat_chunk(n, pair, width, more=0, begin=lambda kk: None, pk=PK):
                for q in range(KT // pk):
                    wh, wl = view(WH, nth(n + q) % 2, width, pk), view(WL, (n + q) % NSLOT, width, pk)
                    for k in range(pk):
                        kk = q * pk + k
                        begin(kk)
                        split(n + q, k, more, pk)
                        for f in range(width // P):
                            o = slice(f * P, (f + 1) * P)
                            last = product(BANK[2 * pair + f // 2][:, (f % 2) * L:(f % 2 + 1) * L],
                                           (wh[:, k, o], wl[:, k, o]), (HH[:, kk, :], HL[:, kk, :]),
                                           kk == 0 and f % 2 == 0, kk == KT - 1)
                        done(k, last, pk)

            def wide_chunk(n, first, width, more=0, begin=lambda kk: None):
                for q in range(PIECES):
                    wh, wl = view(WH, nth(n + q) % 2, width), view(WL, (n + q) % NSLOT, width)
                    for k in range(PK):
                        kk = q * PK + k
                        begin(kk)
                        split(n + q, k, more)
                        for f in range(width // P):
                            o = slice(f * P, (f + 1) * P)
                            bank = BANK[first + f]
                            pe.matmul(bank[:, :].rearrange("p (h n) -> p h n", h=2), wh[:, k, o], HX[:, :, kk, :],
                                      start=kk == 0, stop=False, skip_group_check=True)
                            last = pe.matmul(bank[:, 0:L], wl[:, k, o], HX[:, 0, kk, :], start=False, stop=kk == KT - 1,
                                             skip_group_check=True)
                        done(k, last)

            def ada_piece(n, q, bank, more=0):
                wh, wl = view(WH, nth(n + q) % 2, CH), view(WL, (n + q) % NSLOT, CH)
                for k in range(PK):
                    kk = q * PK + k
                    split(n + q, k, more)
                    last = product(bank, (CSH[:, kk, :], CSL[:, kk, :]), (wh[:, k, :], wl[:, k, :]),
                                   kk == 0, kk == KT - 1)
                    done(k, last)

            def ada_chunk(n, bank, more=0):
                for q in range(PIECES):
                    ada_piece(n, q, bank, more)

            def to_feature(src, g, first, base, scaled=False):
                bank = BANK[first + (base + g) % 2]
                if base + g >= 2:
                    pe.wait_ge(xT_taken, 2 * (base + g - 1))
                for f in range(2):
                    for t in range(TT):
                        o = bank[:, f * L + t * P:f * L + (t + 1) * P]
                        x = src[:, t, (2 * g + f) * P:(2 * g + f + 1) * P]
                        last = (pe.matmul(o, x, diag[:, t, :], start=True, stop=True) if scaled else
                                pe.transpose(o, x, ident[:]))
                last.then_inc(xT_ready, 1)

            def all_to_feature(src, kt, first, base):
                for g in range(kt // 2):
                    to_feature(src, g, first, base)

            def taken(ht, *turn):
                def begin(kk):
                    if kk % 2 == 0:
                        if turn and kk // 2 + 2 < 8:
                            turn[0](kk // 2 + 2)
                        pe.wait_ge(ht_ready, ht + kk // 2 + 1)
                return begin

            pe.wait_ge(consts_set, 1)
            pe.wait_ge(c_in, 16)
            pe.transpose(BANK[7][:, 0:KT], c_rows[0:KT, :], ident[0:KT, 0:KT]).then_inc(cT_ready, 1)
            pe.wait_ge(cs_split, 1)
            for j in range(2):
                ada_chunk(n_ada + PIECES * j, BANK[j][:, :])
            pe.wait_ge(params_in, PARAM_DMAS * 16)
            for g, r in enumerate(GROUP_ROWS):
                last = pe.transpose(BANK[6][:, g * P:g * P + r], rows[0:r, g, :], ident[0:r, 0:r])
            last.then_inc(colsT_ready, 1)
            pe.wait_ge(xn_ready, 2)
            for g in range(8):
                to_feature(X, g, 4, 0, scaled=True)
            with pe.Fori(1, NADA // 2) as i:
                for j in range(2):
                    pe.wait_ge(row_took, i * 2 + j - 1)
                    ada_chunk(n_ada + PIECES * j, BANK[j][:, :], more=i * (2 * PIECES))
            pe.wait_ge(row_took, NADA)
            feat_chunk(n_kw, 0, P, begin=taken(0), pk=KT)
            feat_chunk(n_qi, 1, CH)
            pe.wait_ge(kiT_taken, 1)
            for t in range(TT):
                last = pe.transpose(BANK[6][:, t * P:t * P + P], KIT[:, t * P:(t + 1) * P], ident[:])
            last.then_inc(ki_ready, 1)
            feat_chunk(n_qi + PIECES, 0, CH)
            pe.wait_ge(kix_ready, 4)
            for lo in range(2):
                for t in range(TT):
                    last = pe.transpose(BANK[6][:, lo * L + t * P:lo * L + (t + 1) * P], KIX[:, t, lo, :], ident[:])
            last.then_inc(kixT_ready, 1)
            pe.wait_ge(kb_ready, 1)
            pe.wait_ge(act_took, 6)
            for j in range(8):
                for t in range(TT):
                    s = 2 * j + t
                    w = (t + 1) * P
                    if s >= 2:
                        pe.wait_ge(relu_ready, s - 1)
                    pe.matmul(BANK[4 + t][:, 0:2 * w].rearrange("p (a n) -> p a n", a=2), QI[:, j, t * P:(t + 1) * P], KB[:, :, 0:w],
                              start=True, stop=True).then_inc(idx_ready, 1)
            with pe.Fori(0, 2) as b:
                for j in range(8):
                    pe.wait_ge(act_took, b * 16 + 6 + 2 * j - 2)
                    tok_chunk(n_br + PIECES * j, (j + 1) % 2, CH, more=b * (8 * PIECES))
                    if 1 <= j <= 4:
                        c = j - 1
                        pe.wait_ge(head_normed, b * 4 + c + 1)
                        for g in range(2):
                            for f in range(2):
                                for t in range(TT):
                                    h = 2 * g + f
                                    last = pe.transpose(BANK[4 + 2 * (c % 2) + g][:, f * L + t * P:f * L + (t + 1) * P],
                                                        stage[:, c % 2, t, h * P:(h + 1) * P], ident[:])
                        last.then_inc(headT_ready, 1)
            pe.wait_ge(cs_split, 2)
            pe.wait_ge(act_took, ACT_GATE)

            def gate_piece(h):
                c, q = h // PIECES, h % PIECES
                if q == 0 and c >= 2:
                    pe.wait_ge(act_took, ACT_GATE + c - 1)
                ada_piece(n_gate + PIECES * c, q, BANK[c % 2][:, :])

            attention_pe(pe, 2 * HEADS, 0,
                         lambda h, t: [(QT[:, h // HEADS, h % HEADS, t * P:(t + 1) * P],
                                        KTT[:, h // HEADS, h % HEADS, 0:(t + 1) * P])],
                         lambda h, k: V1[:, h // HEADS, k, (h % HEADS) * DH:(h % HEADS + 1) * DH], Pr, PTs,
                         gate_piece)
            pe.wait_ge(out_taken, 4 * HEADS)
            def turn_y(g):
                to_feature(Z1[:, g // 4], g % 4, 4, 8 + g // 4 * 4)

            turn_y(0)
            turn_y(1)
            pe.wait_ge(act_took, ACT_RKV)
            for c in range(4):
                if c >= 2:
                    pe.wait_ge(x_updated, 2 * (c - 1))
                tok_chunk(n_wo + PIECES * c, c % 2, CH, **(dict(begin=taken(8, turn_y)) if c == 0 else {}))
            pe.wait_ge(xn_ready, 4)
            turn_x = lambda g: to_feature(X, g, 4, 16, scaled=True)
            turn_x(0)
            turn_x(1)

            def rkv_chunk(i, j, **kw):
                if not isinstance(i, int):
                    pe.wait_ge(raw_taken, i * 8 + (4 * j - 4))
                wide_chunk(n_rkv + PIECES * j, 4 * j, CH, more=i * (2 * PIECES), **kw)

            rkv_chunk(0, 0, begin=taken(16, turn_x))
            rkv_chunk(0, 1)
            with pe.Fori(1, 3) as i:
                for j in range(2):
                    rkv_chunk(i, j)
            pe.wait_ge(raw_taken, 4 * 5)
            wide_chunk(n_wag, 0, 3 * P)
            for j in range(3):
                if j < 2:
                    pe.wait_ge(raw_taken, 4 * 6)
                else:
                    pe.wait_ge(act_took, ACT_RKV + 2)
                tok_chunk(n_c + PIECES * j, 2 + (1 + j) % 2, C_WIDTH[j])
            pe.wait_ge(rw_mid, 1)
            pe.wait_ge(raw_taken, RAW_C)
            for q in range(2):
                arrived(n_low + q)
                for g in range(4):
                    r = 4 * q + g
                    if r >= 4:
                        pe.wait_ge(rw_small_took, 2 * (r - 3))
                    p0 = 64 * q
                    for f in range(2):
                        last = pe.matmul(BANK[LOW_BANK[g]][:, f * L:(f + 1) * L],
                                         WR[p0:p0 + 64, (n_low + q) % NSLOT, (2 * g + f) * P:(2 * g + f + 1) * P],
                                         HWA[p0:p0 + 64, :], start=True, stop=True)
                    if g < 3:
                        last.then_inc(rw_small, 1)
                    else:
                        last.then_inc(piece_done, 1)
            pe.wait_ge(rw_small_took, 16)
            pe.wait_ge(kpx_ready, 4)
            all_to_feature(KPX.rearrange("p t a n -> p t (a n)"), 2, 4, 24)
            pe.wait_ge(c_normed, 2 * TT)
            for q in range(2):
                all_to_feature(CQ[:, 2 * q:2 * q + 2, :], 4, 4, 25 + 2 * q)
            pe.wait_ge(xT_taken, 2 * 29)
            for part, (n, stride) in enumerate(((n_uq, 192), (n_uq + 2, 192), (n_ukv, 256), (n_ukv + 2, 256))):
                c0 = 0 if part < 2 else 4
                if part == 2:
                    pe.wait_ge(rw_masks, 1)
                    pe.wait_ge(kk_sq, 1)
                    for g in range(4):
                        pe.matmul(BANK[4 + g][:, :], head_ones, sqk[:, 2 * g:2 * g + 2, :], start=True,
                                  stop=True).then_inc(kk_sum, 1)
                w = [view(WR, (n + m) % NSLOT, 2 * stride) for m in range(2)]
                pe.wait_ge(act_took, ACT_RKV + 2 * (2 + 2 * part))
                for h in range(4):
                    if h % 2 == 0:
                        arrived(n + h // 2)
                    for k in range(4):
                        last = pe.matmul(BANK[h // 2][:, (h % 2) * L:(h % 2 + 1) * L],
                                         w[h // 2][:, k, (h % 2) * stride:(h % 2) * stride + P], CT[:, c0 + k, :],
                                         start=(k == 0), stop=(k == 3))
                last.then_inc(lora_ready, 1)
                pe.wait_ge(act_took, ACT_RKV + 2 * (3 + 2 * part))
                width = stride - P
                for m in range(2):
                    for t in range(TT):
                        for k in range(4):
                            last = pe.matmul(BANK[2 + t][:, 2 * m * width:2 * (m + 1) * width].rearrange("p (h n) -> p h n", h=2),
                                             CT[:, c0 + k, t * P:(t + 1) * P],
                                             w[m][:, k, :].rearrange("p (h n) -> p h n", h=2)[:, :, P:stride],
                                             start=(k == 0), stop=(k == 3))
                    last.then_inc(piece_done, 1)
            pe.wait_ge(qpr_ready, 1)
            pe.wait_ge(kk_var, 1)
            all_to_feature(QPR, 4, 4, 29)
            pe.wait_ge(xT_taken, 2 * 31)
            pe.wait_ge(act_took, ACT_RKV + 22)
            attention_pe(pe, HEADS, 2 * HEADS,
                         lambda h, t: [(QN[:, h, t * P:(t + 1) * P], KN[:, h, 0:(t + 1) * P]),
                                       (QPT[:, h // 2, t * P:(t + 1) * P], KPT[:, h % 2, 0:(t + 1) * P])],
                         lambda h, k: VM[:, k, h * DH:(h + 1) * DH], Pr2, PT2)
            pe.wait_ge(out_taken, 6 * HEADS)
            all_to_feature(YM, 8, 4, 31)
            pe.wait_ge(xT_taken, 2 * 35)
            P_ = Steps(pe_step, pe_names)
            A_, D_, L_ = Steps(act_step, act_names), Steps(dve_step, dve_names), Steps(pool_step, pool_names)
            with pe.Fori(0, NCH) as it:
                def four(name, s, bank, width, *terms):
                    o = BANK[4 * s + bank][:, 0:4 * width].rearrange("p (q n) -> p q n", q=4)
                    for q in range(4):
                        for n, (x, y) in enumerate(terms):
                            last = pe.matmul(o[:, q, :], x[:, q, :], y[:, q, :] if len(y.shape) == 3 else y,
                                             start=(n == 0), stop=(n == len(terms) - 1))
                    P_.mark(last, f"{name}_{s}")

                for s in range(2):
                    L_.wait(pe, f"a1_{s}", it)
                    four("LT", s, 0, P, (b_bd[s], a_bd[s]))
                for s in range(2):
                    L_.wait(pe, f"k1_{s}", it)
                    for name, bank, src in (("btok", 2, b_bd), ("ktok", 3, k_bd)):
                        for q in range(4):
                            last = pe.transpose(BANK[4 * s + bank][:, q * P:(q + 1) * P], src[s][:, q, :], ident[:])
                        P_.mark(last, f"{name}_{s}")
                for s in range(2):
                    four("AkT", s, 1, P, (k_bd[s], a_bd[s]))
                for s in range(2):
                    D_.wait(pe, f"LT_{s}", it)
                    A_.wait(pe, f"ktok_{s}", it)
                    four("T0", s, 3, P, (LT[s], ident[:]))
                for s in range(2):
                    L_.wait(pe, f"v1_{s}", it)
                    four("Vp", s, 0, N, (v_bd[s], I2))
                for s in range(2):
                    L_.wait(pe, f"r1_{s}", it)
                    D_.wait(pe, f"AkT_{s}", it)
                    four("BrT", s, 1, P, (b_bd[s], r_bd[s]))
                for s in range(2):
                    four("KrT", s, 2, P, (k_bd[s], r_bd[s]))
                for m in range(1, LEVELS):
                    for s in range(2):
                        D_.wait(pe, f"X{m - 1}_{s}", it)
                        four(f"T{m}", s, 3, P, (LT[s], Xi[s]))
                    if m == 3:
                        for s in range(2):
                            D_.wait(pe, f"KrT_{s}", it)
                            A_.wait(pe, f"Vp_{s}", it)
                            four("P1", s, 2, N, (a_bd[s], ST[s]), (AkT[s], Vp[s]))
                    for s in range(2):
                        D_.wait(pe, f"T{m}_{s}", it)
                        if m == 1:
                            A_.wait(pe, f"Vp_{s}", it)
                            D_.wait(pe, f"BrT_{s}", it)
                        if m < LEVELS - 1:
                            four(f"X{m}", s, 0, P, (Zi[s], T2[s]))
                        four(f"Z{m}", s, 1, P, (T2[s], Zi[s]))
                for s in range(2):
                    D_.wait(pe, f"Z{LEVELS - 1}_{s}", it)
                    A_.wait(pe, f"P1_{s}", it)
                    four("U", s, 3, N, (Zi[s], P1[s]))
                for s in range(2):
                    A_.wait(pe, f"U_{s}", it)
                    four("Y", s, 0, N, (r_bd[s], ST[s]), (BrT[s], Us[s]), (KrT[s], Vp[s]))
                    four("S", s, 1, N, (b_tok[s], Us[s]), (k_tok[s], Vp[s]))
                for s in range(2):
                    A_.wait(pe, f"y1_{s}", it)
                    four("YT", s, 2, N, (y_bd[s], I2))
                A_.wait(pe, "YT_1", it)
                D_.wait(pe, "S_1", it)
            for g in range(4):
                pe.matmul(BANK[4 + g][:, :], head_ones, YR[:, 2 * g:2 * g + 2, :], start=True, stop=True) \
                    .then_inc(y_sum, 1)
            pe.wait_ge(rk_ready, 1)
            for g in range(4):
                pe.matmul(BANK[g][:, :], head_ones, RK[:, 2 * g:2 * g + 2, :], start=True, stop=True) \
                    .then_inc(bonus_ready, 1)
            for g in range(4):
                pe.wait_ge(y_sq, g + 1)
                for f in (2 * g, 2 * g + 1):
                    for t in range(TT):
                        c0 = 2 * NP_ * t + 2 * f
                        last = pe.matmul(BANK[4][:, c0:c0 + 2], YQ[:, f, t * P:(t + 1) * P], head_cols, start=True, stop=True)
                last.then_inc(y_sum, 1)
            pe.wait_ge(y_rstd_sq, 1)
            for g in range(4):
                for f in range(2):
                    for t in range(TT):
                        last = pe.matmul(BANK[4 + g][:, f * L + t * P:f * L + (t + 1) * P], y_wide[:, t, 2 * g + f, :], ident[:],
                                         start=True, stop=True)
                last.then_inc(y_sum, 1)
            arrived(n_g2)
            arrived(n_g2 + 1)
            for g in range(4):
                pe.wait_ge(bonus_took, g + 1)
                for f in range(2):
                    for n, h in enumerate((HG0, HG1)):
                        r = (P, 32)[n]
                        last = pe.matmul(BANK[g][:, f * L:(f + 1) * L],
                                         WR[0:r, (n_g2 + n) % NSLOT, (2 * g + f) * P:(2 * g + f + 1) * P],
                                         h[0:r, :], start=(n == 0), stop=(n == 1))
                if g < 3:
                    last.then_inc(g_ready, 1)
                else:
                    last.then_inc(piece_done, 2)
            pe.wait_ge(y_normed, 4)
            pe.wait_ge(ht_ready, 28)

            def y_split(kk):
                if kk >= 8 and kk % 2 == 0:
                    pe.wait_ge(g_took, kk - 6)

            for c in range(4):
                if c >= 2:
                    pe.wait_ge(x_updated, 8 + 2 * (c - 1))
                tok_chunk(n_wo2 + PIECES * c, 2 + c % 2, CH, rot=8, **(dict(begin=y_split) if c == 0 else {}))
            pe.wait_ge(xn_ready, 6)
            turn_x = lambda g: to_feature(X, g, 4, 35, scaled=True)
            turn_x(0)
            turn_x(1)

            def gate_up(i, **kw):
                pe.wait_ge(raw_taken, i * 4 + RAW_C)
                wide_chunk(n_gu, 0, CH, more=i * (2 * PIECES), **kw)
                pe.wait_ge(up_taken, i * 4 + 1)
                wide_chunk(n_gu + PIECES, 4, CH, more=i * (2 * PIECES))

            gate_up(0, begin=taken(28, turn_x))
            with pe.Fori(1, FF // CH) as i:
                gate_up(i)

            def down(g, first, final, more=0):
                pe.wait_ge(a_ready, more + (g + 1))
                for c in range(4):
                    if first and c % 2 == 0:
                        pe.wait_ge(*((raw_taken, RAW_C + FT) if c == 0 else (up_taken, FT + 1)))
                    n = n_dn + 4 * g + c
                    wh, wl = view(WH, nth(n) % 2, CH), view(WL, n % NSLOT, CH)
                    for k in range(PK):
                        split(n, k, more * PIECES)
                        for t in range(TT):
                            o = slice(t * P, (t + 1) * P)
                            last = product(BANK[2 * c + t][:, :], (AH[:, g % 2, k, o], AL[:, g % 2, k, o]),
                                           (wh[:, k, :], wl[:, k, :]), first and k == 0, final and k == PK - 1)
                        done(k, last)

            down(0, True, False)
            with pe.Fori(0, 4) as i:
                down(1, False, False, more=i * 2)
                down(2, False, False, more=i * 2)
            down(9, False, False)
            down(10, False, True)

        @block.scalar
        def _(act):
            own = Chain(act, act_chain_s)
            act.dma_start(c_rows[0:KT, :], a["c"][0].rearrange("(a n) -> a n", n=P)).then_inc(c_in, 16)
            for t in range(TT):
                act.dma_start(X[:, t, :], a["x"][0, t * P:(t + 1) * P, :]).then_inc(x_in, 16)
            def high(n, more=0):
                act.wait_ge(piece_in[n % NSLOT], more * (16 // NSLOT) + 16 * (n // NSLOT + 1))
                for s in range(2):
                    if nth(n) >= 2 or not isinstance(more, int):
                        if s == 0:
                            act.wait_ge(half_done, more + (nth(n) - 1))
                        else:
                            act.wait_ge(piece_done, more + (n - 1 if not n_wo2 <= n < n_wo2 + 2 else n_low + n - n_wo2 - 1))
                    w = (s, width_of(n), tiles_of(n))
                    act.activation(half(WH, nth(n) % 2, *w), half(WR, n % NSLOT, *w), ACT.Copy).then_inc(hi_ready, 1)

            def rest_then_next(n, more=0, following=True, rest=True):
                for q in (2, 3, 4, 5)[0 if rest else 2:4 if following else 2]:
                    high(n + q, more)

            def sqrt_of(dst, src):
                return act.activation(dst, src, ACT.Sqrt)

            def read_chunk(n, pair, dsts, func=ACT.Copy, more=0, width=CH, parts=P):
                act.wait_ge(piece_done, more + (n + PIECES))
                for t, dst in enumerate(dsts):
                    act.activation(dst, BANK[2 * pair + t][0:parts, 0:width], func).then_inc(act_took, 1)

            act.wait_ge(cT_ready, 1)
            act.activation(cs, BANK[7][:, 0:KT], ACT.Silu).then_inc(cs_ready, 1)
            high(0)
            high(1)
            act.wait_ge(x_in, 32)
            for t in range(TT):
                act.activation(XN[:, t, :], X[:, t, :], ACT.Square, accum_out=ss[:, t:t + 1]).then_inc(ssq_ready, 1)
            rest_then_next(0)
            act.wait_ge(var_ready, 1)
            sqrt_of(rstd, rstd).then_inc(rstd_ready, 1)
            rest_then_next(PIECES)
            for g in range(8):
                act.wait_ge(xT_ready, g + 1)
                act.activation(xT[:, 2 * g:2 * g + 2, :].rearrange("p f n -> p (f n)"), BANK[4 + g % 2][:, :],
                               ACT.Copy).then_inc(xT_taken, 2)
            with act.Fori(2, NADA - 1) as i:
                rest_then_next(0, more=i * PIECES)
            rest_then_next(n_kw - PIECES)

            def take_feature(dsts, base, gains=None):
                for g in range(len(dsts) // 2):
                    act.wait_ge(xT_ready, base + g + 1)
                    for f in range(2):
                        k = 2 * g + f
                        act.activation(dsts[k], BANK[4 + (base + g) % 2][:, f * L:(f + 1) * L], ACT.Copy,
                                       scale=gains[k] if gains else 1.0).then_inc(xT_taken, 1)

            def take_split(hf, groups, base, ht, n, gains=None, biases=None):
                for g in range(groups):
                    if g == 6:
                        high(n + 2)
                    act.wait_ge(xT_ready, base + g + 1)
                    if g >= 2:
                        act.wait_ge(ht_ready, ht + g - 1)
                    for f in range(2):
                        k = 2 * g + f
                        src = BANK[4 + (base + g) % 2][:, f * L:(f + 1) * L]
                        if biases:
                            ins = act.activation(hf[:, g % 2, f, :], src, ACT.Identity, bias=biases[k], scale=gains[k])
                        else:
                            ins = act.activation(hf[:, g % 2, f, :], src, ACT.Copy, scale=gains[k] if gains else 1.0)
                        ins.then_inc(xT_taken, 1)
                high(n + 3)

            act.wait_ge(mod_ready, 1)
            for k in range(KT):
                act.activation(xT[:, k, :], xT[:, k, :], ACT.Identity, bias=mod[:, k:k + 1],
                               scale=gs[:, k:k + 1]).then_inc(x_scaled, 1)
            high(n_qi + 1)
            act.wait_ge(piece_done, n_kw + 1)
            act.activation(KIT, BANK[0][:, 0:L], ACT.Copy).then_inc(kiT_taken, 1)
            rest_then_next(n_qi)
            act.wait_ge(ki_ready, 1)
            for t in range(TT):
                act.activation(KI[:, t, :], BANK[6][:, t * P:t * P + KW], ACT.Copy).then_inc(act_took, 1)
            for j in range(2):
                if j == 1:
                    high(n_qi + PIECES + 2)
                    act.wait_ge(ki_var, 1)
                    sqrt_of(krstd, krstd).then_inc(ki_rstd, 1)
                    for q in (3, 4, 5):
                        high(n_qi + PIECES + q)
                read_chunk(n_qi + PIECES * j, (1 + j) % 2, [QI[:, 4 * j + 2 * t:4 * j + 2 * t + 2, :].rearrange(
                    "p a n -> p (a n)") for t in range(TT)])
            act.wait_ge(kixT_ready, 1)
            act.activation(KB.rearrange("p a n -> p (a n)"), BANK[6][:, :], ACT.Copy).then_inc(kb_ready, 1)
            for s in range(16):
                t = s % 2
                w = (t + 1) * 2 * P
                act.wait_ge(idx_ready, s + 1)
                if s >= 2:
                    act.wait_ge(relu_used, s - 1)
                act.activation(relu[:, t, 0:w], BANK[4 + t][:, 0:w], ACT.Relu).then_inc(relu_ready, 1)
            with act.Fori(0, 2) as b:
                more = b * (8 * PIECES)
                for j in range(8):
                    n, pair = n_br + PIECES * j, (j + 1) % 2
                    high(n + 2, more)
                    high(n + 3, more)
                    if 1 <= j <= 4:
                        act.wait_ge(head_var, b * 4 + j)
                        hr = hrstd[:, 8 * ((j - 1) % 2):8 * ((j - 1) % 2) + 8]
                        sqrt_of(hr, hr).then_inc(head_rstd, 1)
                    high(n + 4, more)
                    high(n + 5, more)
                    if j < 4:
                        if j >= 2:
                            act.wait_ge(headT_ready, b * 4 + (j - 1))
                        read_chunk(n, pair, [stage[:, j % 2, t, :] for t in range(TT)], more=more)
                    elif j < 6:
                        read_chunk(n, pair, [V1[:, ds(b, 1), t, (j - 4) * CH:(j - 3) * CH].rearrange("p o n -> p (o n)")
                                             for t in range(TT)], more=more)
                    else:
                        read_chunk(n, pair, [Z1[:, ds(b, 1), t, (j - 6) * CH:(j - 5) * CH].rearrange("p o n -> p (o n)")
                                             for t in range(TT)], func=ACT.Silu, more=more)
                    if 1 <= j <= 4:
                        c = j - 1
                        act.wait_ge(headT_ready, b * 4 + c + 1)
                        dst = QT if c < 2 else KTT
                        for g in range(2):
                            h = 4 * (c % 2) + 2 * g
                            act.activation(dst[:, ds(b, 1), h:h + 2, :].rearrange("p o a n -> p (o a n)"),
                                           BANK[4 + 2 * (c % 2) + g][:, :], ACT.Copy,
                                           scale=qgain[:, ds(b + (0 if c < 2 else 2), 1)]).then_inc(headT_taken, 1)
            act.wait_ge(piece_done, n_gate)
            act.dma_start(bgate_row, a["b_ada"][0:1, 2 * D:3 * D].to_broadcast([P, D])).then_inc(bgate_in, 16)

            def gate_high(h):
                high(n_gate + 2 + h)
                if h % PIECES == PIECES - 1:
                    c = h // PIECES
                    act.wait_ge(piece_done, n_gate + PIECES * (c + 1))
                    act.activation(gate_row[:, c * CH:(c + 1) * CH], BANK[c % 2][:, :], ACT.Copy).then_inc(act_took, 1)

            attention_act(act, 2 * HEADS, 0, S_sb, Pr, PTs, gate_high)
            take_split(hf1, 8, 8, 8, n_wo)
            def squares(c, junk, base):
                for t in range(TT):
                    act.wait_ge(x_updated, base + 2 * c + t + 1)
                    act.activation(junk[:, t, c * CH:(c + 1) * CH], X[:, t, c * CH:(c + 1) * CH], ACT.Square,
                                   accum_out=sq4[:, 4 * t + c:4 * t + c + 1]).then_inc(ssq_ready, 1)

            def norm_act(q):
                act.wait_ge(var_ready, q + 1)
                sqrt_of(rstd, rstd).then_inc(rstd_ready, 1)

            for c in range(4):
                rest_then_next(n_wo + PIECES * c, rest=c > 0)
                if c >= 1:
                    squares(c - 1, XN2, 0)
            squares(3, XN2, 0)
            for t in range(TT):
                act.dma_start(pos_i[:, t:t + 1], a["positions_2"][0, t * P:(t + 1) * P].rearrange("(p o) -> p o", o=1)) \
                   .then_inc(pos_in, 16)
            norm_act(1)
            take_split(hf2, 8, 16, 16, n_rkv, [col("attn_norm_g_2", k) for k in range(KT)])
            act.wait_ge(ang_ready, 1)
            act.activation(ang.rearrange("p s t n -> p (s t n)"), turns.rearrange("p s t n -> p (s t n)"),
                           ACT.Sin).then_inc(trig_ready, 1)
            for c in range(6):
                rest_then_next(n_rkv + PIECES * c, rest=c > 0)
            rest_then_next(n_wag)
            for j in range(3):
                rest_then_next(n_c + PIECES * j, following=j < 2)
                act.wait_ge(piece_done, n_c + PIECES * (j + 1))
                for t in range(TT):
                    for (b0, b1), which, (c0, c1) in C_PARTS[j]:
                        dst = KPE[:, t, :] if which == 2 else CQ[:, 2 * which + t, c0:c1]
                        ins = act.activation(dst, BANK[4 + 2 * ((1 + j) % 2) + t][:, b0:b1], ACT.Copy)
                    ins.then_inc(act_took, 1)
                if j == 0:
                    act.wait_ge(wag_ready, 3)
                    act.activation(HWA[0:64, :], HWA[0:64, :], ACT.Tanh).then_inc(rw_mid, 1)
            for j in range(4):
                act.wait_ge(act_took, ACT_RKV + 6)
                act.activation(XN2[:, j // 2, (j % 2) * CH:(j % 2 + 1) * CH], CQ[:, j, :], ACT.Square,
                               accum_out=cstat[:, j:j + 1]).then_inc(c_sq, 1)

            def low_rank_out(r):
                if r % 4 < 3:
                    act.wait_ge(rw_small, r + 1 - r // 4)
                else:
                    act.wait_ge(piece_done, n_low + r // 4 + 1)
                dst, bias = ((Lw, "rwkv_w0_2"), (Bv, "rwkv_a0_2"))[r // 4]
                for f in range(2):
                    k = 2 * (r % 4) + f
                    act.activation(dst[:, k, :], BANK[LOW_BANK[r % 4]][:, f * L:(f + 1) * L], ACT.Sigmoid,
                                   bias=col(bias, k)).then_inc(rw_small_took, 1)

            for r in range(4):
                low_rank_out(r)
            act.wait_ge(c_var, 1)
            sqrt_of(crstd, crstd).then_inc(c_rstd, 1)
            for r in range(4, 8):
                low_rank_out(r)
            take_feature([KPT[:, k, :] for k in range(2)], 24)
            for q, name in enumerate(("mla_q_norm_g_2", "mla_kv_norm_g_2")):
                take_feature([CT[:, 4 * q + k, :] for k in range(4)], 25 + 2 * q, [col(name, k) for k in range(4)])
            scale = float(DH + ROPE) ** -0.5
            for part in range(4):
                dst, o = (QN, KN)[part // 2], 4 * (part % 2)
                act.wait_ge(lora_ready, part + 1)
                for t in range(TT):
                    act.activation(dst[:, o + 2 * t:o + 2 * t + 2, :].rearrange("p a n -> p (a n)"), BANK[t][:, :],
                                   ACT.Copy, scale=scale if part < 2 else 1.0).then_inc(act_took, 1)
                act.wait_ge(piece_done, n_uq + 2 * (part + 1))
                for t in range(TT):
                    if part < 2:
                        act.activation(QPE[:, t, part * 256:(part + 1) * 256], BANK[2 + t][:, 0:256], ACT.Copy,
                                       scale=scale).then_inc(act_took, 1)
                    else:
                        act.activation(VM[:, t, (part - 2) * CH:(part - 1) * CH], BANK[2 + t][:, :],
                                       ACT.Copy).then_inc(act_took, 1)
                if part == 0:
                    act.wait_ge(kk_raw, 1)
                    act.activation(sqk, KKn[:, :, :], ACT.Square).then_inc(kk_sq, 1)
                elif part == 1:
                    act.wait_ge(fac_raw, 1)
                    act.activation(small[:, 328:360], small[:, 328:360], ACT.Exp, scale=-DECAY).then_inc(fac_ready, 1)
                    act.wait_ge(decay_summed, 1)
                    act.activation(Lw[:, :, :], Lw[:, :, :], ACT.Exp, scale=-DECAY).then_inc(exc_ready, 1)
                elif part == 2:
                    act.wait_ge(kk_var, 1)
                    act.activation(sqk, sqk, ACT.Sqrt).then_inc(kk_rstd, 1)
                    act.wait_ge(k_mod, 1)
                    act.activation(EXr, El, ACT.Exp, scale=-DECAY).then_inc(ex_ready, 1)
                    act.wait_ge(ex_ready, 1)
                    act.activation(El, El, ACT.Exp, scale=DECAY).then_inc(en_ready, 1)
            take_feature([QPT[:, k, :] for k in range(4)], 29)
            attention_act(act, HEADS, 2 * HEADS, S2, Pr2, PT2)
            for g in range(4):
                act.wait_ge(xT_ready, 31 + g + 1)
                act.activation(YMT[:, 2 * g:2 * g + 2, :].rearrange("p f n -> p (f n)"), BANK[4 + (31 + g) % 2][:, :],
                               ACT.Copy).then_inc(xT_taken, 2)
            act.activation(HG0, HG0, ACT.Sigmoid).then_inc(rw_mid, 1)
            act.activation(HG1[0:32, :], HG1[0:32, :], ACT.Sigmoid).then_inc(rw_mid, 1)
            P_ = Steps(pe_step, pe_names)
            A_, D_ = Steps(act_step, act_names), Steps(dve_step, dve_names)
            with act.Fori(0, NCH) as it:
                def take(name, s, bank, dst, w):
                    P_.wait(act, f"{name}_{s}", it)
                    A_.mark(act.activation(dst[s].rearrange("p q n -> p (q n)"), BANK[4 * s + bank][:, 0:4 * w],
                                           ACT.Copy), f"{name}_{s}")

                for s in range(2):
                    take("btok", s, 2, b_tok, P)
                    take("ktok", s, 3, k_tok, P)
                for name, bank, dst in (("Vp", 0, Vp), ("P1", 2, P1), ("U", 3, Us)):
                    for s in range(2):
                        take(name, s, bank, dst, N)
                for s in range(2):
                    P_.wait(act, f"Y_{s}", it)
                    for h in range(2):
                        o = slice(h * N, (h + 1) * N)
                        A_.mark(act.activation(y_bd[s][o, :, o], BANK[4 * s][o, 0:4 * N].rearrange(
                            "p (q n) -> p q n", q=4), ACT.Copy), f"y{h}_{s}")
                for s in range(2):
                    P_.wait(act, f"YT_{s}", it)
                    A_.mark(act.activation(YR[:, 4 * s:4 * s + 4, ds(it * C, C)],
                                           BANK[4 * s + 2][:, 0:4 * N].rearrange("p (q n) -> p q n", q=4), ACT.Copy),
                            f"YT_{s}")
            for g in range(4):
                act.activation(HH[:, 8 + 2 * g:10 + 2 * g, :], YMT[:, 2 * g:2 * g + 2, :], ACT.Copy).then_inc(y_hi, 1)
            for g in range(4):
                act.wait_ge(y_centred, g + 1)
                act.activation(YQ[:, 2 * g:2 * g + 2, :], YR[:, 2 * g:2 * g + 2, :], ACT.Square).then_inc(y_sq, 1)
            high(n_wo2)
            act.wait_ge(y_var, 1)
            sqrt_of(y_wide.rearrange("p t f (h m) -> p (t f h) m", h=2),
                    y_scale.unsqueeze(2).to_broadcast([P, 4 * NP_, N])).then_inc(y_rstd_sq, 1)
            high(n_wo2 + 1)
            for g in range(4):
                act.wait_ge(y_normed, g + 1)
                for k in (2 * g, 2 * g + 1):
                    act.activation(YR[:, k, :], YR[:, k, :], ACT.Identity, bias=col("rwkv_gn_b_2", k),
                                   scale=col("rwkv_gn_w_2", k)).then_inc(y_scaled, 1)
            for c in range(4):
                rest_then_next(n_wo2 + PIECES * c)
                if c >= 1:
                    squares(c - 1, XN3, 8)
            squares(3, XN3, 8)
            norm_act(2)
            act.dma_start(fg_row, a["final_norm_g_2"].rearrange("(o n) -> o n", o=1).to_broadcast([P, D])).then_inc(fg_in, 16)
            take_split(hf4, 8, 35, 28, n_gu, [col("ffn_norm_g_2", k) for k in range(KT)])
            def gate_up(i, rest=True):
                more = i * (2 * PIECES)
                rest_then_next(n_gu, more, rest=rest)
                rest_then_next(n_gu + PIECES, more)
                act.wait_ge(conv_ready, i + 1)
                act.activation(CV.rearrange("p f n -> p (f n)"), CV.rearrange("p f n -> p (f n)"),
                               ACT.Silu).then_inc(gate_act, 1)

            gate_up(0, rest=False)
            with act.Fori(1, FF // CH) as i:
                gate_up(i)
            with act.Fori(0, FT // PK - 1) as i:
                rest_then_next(n_dn, i * PIECES)
            rest_then_next(n_dn + PIECES * (FT // PK - 1), following=False)
            for c in range(4):
                squares(c, XN3, 16)
            norm_act(3)

        @block.vector
        def _(dve):
            own = Chain(dve, dve_chain_s)

            def inverse_mean(dst, src, width, eps=EPS):
                own.link(dve.tensor_scalar(dst, src, 1.0 / width, eps, ALU.mult, ALU.add))
                return dve.reciprocal(dst, dst)

            def norm_dve(q):
                if q:
                    dve.wait_ge(ssq_ready, 2 + 8 * q)
                    own.link(dve.tensor_reduce(ss, sq4.rearrange("p (t c) -> p t c", t=TT), AX_X, ALU.add))
                else:
                    dve.wait_ge(ssq_ready, 2)
                inverse_mean(rstd, ss, D).then_inc(var_ready, 1)

            def make_diag(q):
                dve.wait_ge(rstd_ready, q + 1)
                for t in range(TT):
                    dve.tensor_scalar(diag[:, t, :], ident[:], rstd[:, t:t + 1], None, ALU.mult).then_inc(xn_ready, 1)

            def ht_split(hf, groups, base, first):
                for g in range(groups):
                    k = slice(first + 2 * g, first + 2 * g + 2)
                    dve.wait_ge(xT_taken, 2 * (base + g + 1))
                    own.link(dve.tensor_copy(HH[:, k, :], hf[:, g % 2]))
                    dve.tensor_tensor(HL[:, k, :], hf[:, g % 2], HH[:, k, :], ALU.subtract).then_inc(ht_ready, 1)

            def split_c():
                wide = cs.unsqueeze(2).to_broadcast([P, KT, P])
                own.link(dve.tensor_copy(CSH[:, :, :], wide))
                dve.tensor_tensor(CSL[:, :, :], wide, CSH[:, :, :], ALU.subtract).then_inc(cs_split, 1)

            def take_mod(c, j, at_col):
                dve.wait_ge(piece_done, c * PIECES + PIECES)
                own.link(dve.tensor_tensor(square[:, 0, :].rearrange("p (k n) -> p k n", k=4),
                                           BANK[j][:, :].rearrange("p (k n) -> p k n", k=4),
                                           ident[:].unsqueeze(1).to_broadcast([P, 4, P]), ALU.mult))
                dve.tensor_reduce(at_col, square[:, 0, :].rearrange("p (k n) -> p k n", k=4), AX_X,
                                  ALU.add).then_inc(row_took, 1)
                dve.wait_ge(row_took, c + 1)

            def ada_lows(c, between=None):
                for q in range(PIECES):
                    if q == 2 and between:
                        between()
                    low_part(dve, n_ada + q, 1, c * PIECES, lo_ready_dve)

            dve.wait_ge(consts_set, 1)
            dve.wait_ge(cs_ready, 1)
            split_c()
            ada_lows(0, lambda: norm_dve(0))
            ada_lows(1, lambda: make_diag(0))
            dve.wait_ge(colsT_ready, 1)
            for g, r in enumerate(GROUP_ROWS):
                last = dve.tensor_copy(cols[:, g * P:g * P + r], BANK[6][:, g * P:g * P + r])
            last.then_inc(cols_ready, 1)
            dve.wait_ge(cols_ready, 1)
            for b in range(2):
                own.mark(dve.tensor_scalar(qgain[:, b:b + 1], col(("q_norm_a", "q_norm_b")[b]), float(DH) ** -0.5, None, ALU.mult))
                own.mark(dve.tensor_copy(qgain[:, 2 + b:3 + b], col(("k_norm_a", "k_norm_b")[b])))
            take_mod(0, 0, mod[:, 0:4])
            with dve.Fori(1, NADA // 2) as i:
                own.enter(i - 1, 2)
                for j in range(2):
                    c = i * 2 + j
                    ada_lows(c, lambda: take_mod(c - 1, 1 - j, small[:, ds(c * 4 - 4, 4)]))
                own.leave(NADA // 2 - 1)
            take_mod(NADA - 1, 1, mod[:, 4 * NADA - 4:4 * NADA])
            own.link(dve.tensor_tensor(mod[:, 0:32], mod[:, 0:32], col("b_ada", 0, 32), ALU.add))
            own.link(dve.tensor_scalar(gs, mod[:, 16:32], 1.0, None, ALU.add))
            dve.tensor_tensor(gs, gs, col("g_norm", 0, 16), ALU.mult).then_inc(mod_ready, 1)
            for g in range(8):
                k = slice(2 * g, 2 * g + 2)
                dve.wait_ge(x_scaled, 2 * (g + 1))
                own.link(dve.tensor_copy(HH[:, k, :], xT[:, k, :]))
                dve.tensor_tensor(HL[:, k, :], xT[:, k, :], HH[:, k, :], ALU.subtract).then_inc(ht_ready, 1)
            dve.wait_ge(act_took, 2)
            for t in range(TT):
                own.link(dve.tensor_tensor(square[:, t, 0:IDX_DIM], KI[:, t, 0:IDX_DIM], KI[:, t, 0:IDX_DIM], ALU.mult))
                own.link(dve.tensor_reduce(kss[:, t:t + 1], square[:, t, 0:IDX_DIM], AX_X, ALU.add))
            inverse_mean(krstd, kss, IDX_DIM).then_inc(ki_var, 1)
            dve.wait_ge(ki_rstd, 1)
            dve.wait_ge(consts_set, CONSTS)
            for t in range(TT):
                for lo in range(2):
                    dve.scalar_tensor_tensor(out=KIX[:, t, lo, lo * IDX_DIM:(lo + 1) * IDX_DIM], in0=KI[:, t, 0:IDX_DIM],
                                             scalar=krstd[:, t:t + 1], in1=kin_g, op0=ALU.mult,
                                             op1=ALU.mult).then_inc(kix_ready, 1)
            for s in range(16):
                j, t = s // 2, s % 2
                w = (t + 1) * P
                sc = score[:, 0:P] if t == 0 else score[:, P:SPAN]
                dve.wait_ge(relu_ready, s + 1)
                for f in range(2):
                    wt = KI[:, t, IDX_DIM + 2 * j + f:IDX_DIM + 2 * j + f + 1]
                    r = relu[:, t, f * w:(f + 1) * w]
                    if j == 0 and f == 0:
                        own.link(dve.tensor_scalar(sc, r, wt, None, ALU.mult))
                    else:
                        ins = dve.scalar_tensor_tensor(out=sc, in0=r, scalar=wt, in1=sc, op0=ALU.mult, op1=ALU.add)
                        if f == 1:
                            ins.then_inc(relu_used, 1)
                            dve.wait_ge(relu_used, s + 1)
                        else:
                            own.link(ins)
            own.link(dve.tensor_tensor(score, score, causal_mask, ALU.add))
            own.link(dve.tensor_copy(work, score))
            halves = [(0, P), (P, L)]
            for r in range(TOPK // 8):
                for t, (c0, w) in enumerate(halves):
                    own.mark(dve.max(top8[:, t, :], work[:, c0:c0 + w]))
                own.wait()
                if r < TOPK // 8 - 1:
                    for t, (c0, w) in enumerate(halves):
                        own.mark(dve.match_replace(work[:, c0:c0 + w], top8[:, t, :], work[:, c0:c0 + w], -3e38))
                    own.wait()
            for t, (c0, w) in enumerate(halves):
                thr = top8[:, t, 7:8]
                sc, wk, gt = score[:, c0:c0 + w], work[:, c0:c0 + w], bias_a[:, c0:c0 + w]
                eq, run = square[:, t, 0:w], relu[:, t, 0:w]
                own.link(dve.tensor_scalar(gt, sc, thr, None, ALU.is_gt, ALU.add, accum_out=cnt[:, t:t + 1]))
                own.link(dve.tensor_scalar(need[:, t:t + 1], cnt[:, t:t + 1], -1.0, float(TOPK), ALU.mult, ALU.add))
                own.link(dve.tensor_scalar(eq, sc, thr, None, ALU.is_equal))
                own.link(dve.memset(wk, 1.0))
                own.link(dve.tensor_tensor_scan(run, wk, eq, 0.0, ALU.mult, ALU.add))
                own.link(dve.scalar_tensor_tensor(out=eq, in0=run, scalar=need[:, t:t + 1], in1=eq,
                                                  op0=ALU.is_le, op1=ALU.mult))
                own.link(dve.tensor_tensor(gt, gt, eq, ALU.add))
                own.link(dve.tensor_scalar(gt, gt, -1.0, -NEG, ALU.add, ALU.mult))
                own.link(dve.tensor_tensor(gt, gt, causal_dist[:, c0:c0 + w], ALU.add))
            with dve.Fori(0, 2) as b:
                own.enter(b, 12)
                for j in range(4):
                    s = stage[:, j % 2]
                    flat = s.rearrange("p t n -> p (t n)")
                    sq = square.rearrange("p t n -> p (t n)")
                    dve.wait_ge(act_took, b * 16 + 6 + 2 * (j + 1))
                    own.link(dve.tensor_tensor(sq, flat, flat, ALU.mult))
                    hs, hr = hss[:, 8 * (j % 2):8 * (j % 2) + 8], hrstd[:, 8 * (j % 2):8 * (j % 2) + 8]
                    own.link(dve.tensor_reduce(hs, sq.rearrange("p (g n) -> p g n", n=DH), AX_X, ALU.add))
                    inverse_mean(hr, hs, DH).then_inc(head_var, 1)
                    dve.wait_ge(head_rstd, b * 4 + j + 1)
                    for g in range(8):
                        v = s[:, g // 4, (g % 4) * DH:(g % 4 + 1) * DH]
                        last = dve.tensor_scalar(v, v, hr[:, g:g + 1], None, ALU.mult)
                    last.then_inc(head_normed, 1)
                own.leave(2)

            dve.wait_ge(piece_done, n_gate)
            split_c()

            def emit(h, t, o, inv):
                b, hh = h // HEADS, h % HEADS
                z = Z1[:, b, t, hh * DH:(hh + 1) * DH]
                return dve.scalar_tensor_tensor(out=z, in0=o, scalar=inv, in1=z, op0=ALU.mult, op1=ALU.mult)

            attention_dve(dve, own, 2 * HEADS, 0,
                          lambda h: bias_a if h < HEADS else causal_dist,
                          lambda h: slope[:, h:h + 1], emit, S_sb)
            dve.wait_ge(bgate_in, 16)
            dve.wait_ge(act_took, ACT_RKV - 1)
            own.link(dve.tensor_tensor(gate_row[:, 0:3 * CH], gate_row[:, 0:3 * CH], bgate_row[:, 0:3 * CH], ALU.add))
            dve.wait_ge(act_took, ACT_RKV)
            own.link(dve.tensor_tensor(gate_row[:, 3 * CH:D], gate_row[:, 3 * CH:D], bgate_row[:, 3 * CH:D], ALU.add))
            ht_split(hf1, 8, 8, 0)
            for c in range(4):
                dve.wait_ge(piece_done, n_wo + PIECES * (c + 1))
                for t in range(TT):
                    xc = X[:, t, c * CH:(c + 1) * CH]
                    own.link(dve.tensor_tensor(wo_tmp[:, t, :], BANK[2 * (c % 2) + t][:, :],
                                               gate_row[:, c * CH:(c + 1) * CH], ALU.mult))
                    dve.tensor_tensor(xc, xc, wo_tmp[:, t, :], ALU.add).then_inc(x_updated, 1)
            norm_dve(1)
            make_diag(1)
            for j in range(32):
                own.mark(dve.memset(inv_freq[:, j:j + 1], float(np.float32(10000.0) ** np.float32(-j / 32.0))))
            dve.wait_ge(pos_in, 32)
            own.mark(dve.tensor_copy(pos, pos_i))
            own.wait()
            flat = lambda v: v.rearrange("p t n -> p (t n)")
            two_pi = 2 * np.pi
            c1 = 6.28125
            c2 = float(np.float32(int((two_pi - c1) * 2 ** 21) / 2 ** 21))
            c3 = float(two_pi - c1 - c2)
            magic = 1.5 * 2 ** 23
            for part in range(2):
                th, nt = ang[:, part], turns[:, part]
                for t in range(TT):
                    own.mark(dve.tensor_scalar(th[:, t, :], inv_freq, pos[:, t:t + 1], None, ALU.mult))
                own.wait()
                own.link(dve.tensor_scalar(flat(nt), flat(th), float(1 / two_pi), 0.25 * part, ALU.mult, ALU.add))
                own.link(dve.tensor_scalar(flat(nt), flat(nt), magic, -magic, ALU.add, ALU.add))
                for cc in (c1, c2, c3):
                    own.link(dve.scalar_tensor_tensor(out=flat(th), in0=flat(nt), scalar=-cc, in1=flat(th),
                                                      op0=ALU.mult, op1=ALU.add))
                own.link(dve.tensor_scalar(flat(th), flat(th), float(np.pi / 2) * part, None, ALU.add))
                lim = float(np.nextafter(np.float32(np.pi), np.float32(0)))
                own.link(dve.tensor_scalar(flat(nt), flat(th), lim, -lim, ALU.min, ALU.max))
            dve.tensor_copy(small[:, 510:511], pos[:, 0:1]).then_inc(ang_ready, 1)
            ht_split(hf2, 8, 16, 0)
            own.link(dve.memset(RAW[:, :, 0:1], 0.0))
            gm, rm, _ = VEC["rwkv_mu_2"]
            mu0 = gm * P + rm

            def add_halves(dst, bank, ready):
                dve.tensor_reduce(dst, BANK[bank][:, :].rearrange("p (h n) -> p n h", h=2), AX_X, ALU.add).then_inc(ready, 1)

            with dve.Fori(0, 3) as i:
                own.enter(i, 4)
                for j in range(2):
                    dve.wait_ge(piece_done, i * (2 * PIECES) + (n_rkv + PIECES * (j + 1)))
                    for f in range(4):
                        add_halves(RAW[:, f, 1:L + 1], 4 * j + f, raw_taken)
                    dve.wait_ge(raw_taken, i * 8 + 4 * (j + 1))
                    own.link(dve.tensor_tensor(SH, RAW[:, :, 0:L], RAW[:, :, 1:L + 1], ALU.subtract))
                    for f in range(4):
                        last = dve.scalar_tensor_tensor(out=RKV[:, ds(8 * i + (4 * j + f), 1), :].rearrange("p o n -> p (o n)"),
                                                        in0=SH[:, f, :], scalar=cols[:, ds(8 * i + (mu0 + 4 * j + f), 1)],
                                                        in1=RAW[:, f, 1:L + 1], op0=ALU.mult, op1=ALU.add)
                    own.link(last)
                own.leave(3)
            dve.wait_ge(piece_done, n_wag + PIECES)
            for f in range(3):
                add_halves(RAW[:, f, 1:L + 1], f, raw_taken)
            dve.wait_ge(raw_taken, RAW_C)
            own.link(dve.tensor_tensor(SH[:, 0:3, :], RAW[:, 0:3, 0:L], RAW[:, 0:3, 1:L + 1], ALU.subtract))
            for f, (dst, m) in enumerate(((HWA, P), (HG0, P), (HG1, 32))):
                dve.scalar_tensor_tensor(out=dst[0:m, :], in0=SH[0:m, f, :], scalar=cols[0:m, mu0 + 24 + f:mu0 + 25 + f],
                                         in1=RAW[0:m, f, 1:L + 1], op0=ALU.mult, op1=ALU.add).then_inc(wag_ready, 1)
            own.link(dve.memset(KPX, 0.0))
            dve.wait_ge(act_took, ACT_RKV + 6)
            dve.wait_ge(trig_ready, 1)

            def rotate(dst, src, t, heads, emit=None):
                sn = ang[:, 0, t, :].unsqueeze(1).to_broadcast([P, heads, 32])
                cn = ang[:, 1, t, :].unsqueeze(1).to_broadcast([P, heads, 32])
                tmp = [rope_tmp[:, i, 0:heads * 32].rearrange("p (h n) -> p h n", n=32) for i in range(4)]
                lo, hi = src[:, :, 0:32], src[:, :, 32:64]
                for d, x, y in ((0, lo, cn), (1, hi, sn), (2, hi, cn), (3, lo, sn)):
                    own.mark(dve.tensor_tensor(tmp[d], x, y, ALU.mult))
                own.wait()
                return (dve.tensor_tensor(dst[:, :, 0:32], tmp[0], tmp[1], ALU.subtract),
                        dve.tensor_tensor(dst[:, :, 32:64], tmp[2], tmp[3], ALU.add))

            for t in range(TT):
                x, y = rotate(KPX[:, t, 0:1, 0:ROPE], KPE[:, t:t + 1, :], t, 1)
                own.mark(x)
                own.mark(y)
                own.wait()
                dve.tensor_copy(KPX[:, t, 1, ROPE:2 * ROPE], KPX[:, t, 0, 0:ROPE]).then_inc(kpx_ready, 2)
            dve.wait_ge(c_sq, 4)
            inverse_mean(crstd, cstat, LORA).then_inc(c_var, 1)
            dve.wait_ge(c_rstd, 1)
            for j in range(4):
                dve.tensor_scalar(CQ[:, j, :], CQ[:, j, :], crstd[:, j:j + 1], None, ALU.mult).then_inc(c_normed, 1)
            R_, K_, V_ = RKV[:, 0:8], RKV[:, 8:16], RKV[:, 16:24]
            fl = lambda v: v.rearrange("p f n -> p (f n)")
            own.link(dve.tensor_scalar(one_ka, col("rwkv_k_a_2", 0, 8), -1.0, 1.0, ALU.mult, ALU.add))
            dve.wait_ge(piece_done, n_low)
            for f in range(8):
                ins = dve.tensor_scalar(KKn[:, f, :], K_[:, f, :], col("rwkv_k_k_2", f), None, ALU.mult)
            ins.then_inc(kk_raw, 1)
            dve.wait_ge(rw_small_took, 8)
            dve.wait_ge(rw_masks, 1)
            for f in range(8):
                own.mark(dve.tensor_tensor_scan(El[:, f, :], chunk_start, Lw[:, f, :], 0.0, ALU.mult, ALU.add))
            own.wait()
            e4 = fl(El).rearrange("p (g t) -> p g t", t=C)
            own.mark(dve.tensor_copy(small[:, 264:296], e4[:, :, C - 1]))
            own.mark(dve.tensor_copy(small[:, 296:328], e4[:, :, C // 2 - 1]))
            own.wait()
            own.link(dve.tensor_tensor(e4, e4, small[:, 296:328].unsqueeze(2).to_broadcast([P, 32, C]), ALU.subtract))
            own.link(dve.tensor_tensor(fac, end_s, mid_s, ALU.subtract))
            own.link(dve.tensor_tensor(fac[:, :, 0:NCH - 1], fac[:, :, 0:NCH - 1], mid_s[:, :, 1:NCH], ALU.add))
            dve.tensor_copy(small[:, 505:506], small[:, 328:329]).then_inc(fac_raw, 1)
            dve.tensor_tensor(fl(Lw[:, :, :]), fl(El), fl(Lw[:, :, :]), ALU.subtract).then_inc(decay_summed, 1)
            dve.wait_ge(act_took, ACT_RKV + 14)
            for t in range(TT):
                x, y = rotate(QPR[:, t, :].rearrange("p (h n) -> p h n", n=ROPE),
                              QPE[:, t, :].rearrange("p (h n) -> p h n", n=ROPE), t, HEADS)
                own.mark(x)
                if t == 0:
                    own.mark(y)
                    own.wait()
                else:
                    y.then_inc(qpr_ready, 1)

            for g in range(4):
                dve.wait_ge(kk_sum, g + 1)
                own.mark(dve.tensor_scalar(fl(sqk[:, 2 * g:2 * g + 2]), BANK[4 + g][:, :], 1e-24, None, ALU.max))
            own.wait()
            dve.reciprocal(fl(sqk), fl(sqk)).then_inc(kk_var, 1)
            dve.wait_ge(kk_rstd, 1)
            own.link(dve.tensor_tensor(fl(KKn[:, :, :]), fl(KKn[:, :, :]), fl(sqk), ALU.mult))
            dve.wait_ge(k_mod, 1)
            own.link(dve.scalar_tensor_tensor(out=fl(Bv[:, :, :]), in0=fl(Bv[:, :, :]), scalar=-1.0, in1=fl(KKn[:, :, :]), op0=ALU.mult, op1=ALU.mult))
            dve.tensor_copy(small[:, 504:505], small[:, 328:329]).then_inc(kk_ready, 1)
            dve.wait_ge(en_ready, 1)
            dve.tensor_tensor(fl(Bv[:, :, :]), fl(Bv[:, :, :]), fl(El), ALU.mult).then_inc(ops_ready, 1)
            dve.wait_ge(exc_ready, 1)
            dve.tensor_tensor(fl(KKn[:, :, :]), fl(KKn[:, :, :]), fl(Lw[:, :, :]), ALU.mult).then_inc(ops_ready, 1)

            def decayed(h):
                if h == 3:
                    dve.wait_ge(rk_raw, 1)
                    dve.tensor_tensor(fl(K_), fl(K_), fl(El), ALU.mult).then_inc(ops_ready, 2)
                elif h == 4:
                    dve.wait_ge(ex_ready, 1)
                    dve.tensor_tensor(fl(R_), fl(R_), fl(EXr), ALU.mult).then_inc(ops_ready, 1)

            def emit2(h, t, o, inv):
                return dve.tensor_scalar(YM[:, t, h * DH:(h + 1) * DH], o, inv, None, ALU.mult)

            attention_dve(dve, own, HEADS, 2 * HEADS, lambda h: causal_mask, lambda h: 1.0, emit2, S2,
                          decayed)
            dve.memset(small[:, 506:507], 0.0).then_inc(masks_free, 1)
            for s in range(2):
                own.mark(dve.memset(ST[s], 0.0))
            own.wait()
            dve.wait_ge(fac_ready, 1)
            P_ = Steps(pe_step, pe_names)
            D_ = Steps(dve_step, dve_names)
            four = lambda m: m.unsqueeze(1).to_broadcast([P, 4, P])
            with dve.Fori(0, NCH) as it:
                bank4 = lambda s, b, w: BANK[4 * s + b][:, 0:4 * w].rearrange("p (q n) -> p q n", q=4)

                def masked(name, s, dst, bank, mask):
                    P_.wait(dve, f"{name}_{s}", it)
                    D_.mark(dve.tensor_tensor(dst[s], bank4(s, bank, P), four(mask), ALU.mult), f"{name}_{s}")

                def added(name, s, dst, bank):
                    P_.wait(dve, f"{name}_{s}", it)
                    D_.mark(dve.tensor_tensor(dst[s], dst[s], bank4(s, bank, P), ALU.add), f"{name}_{s}")

                for s in range(2):
                    masked("LT", s, LT, 0, below)
                for s in range(2):
                    masked("AkT", s, AkT, 1, below)
                for s in range(2):
                    masked("T0", s, T2, 3, level[0])
                    D_.wait(dve, f"T0_{s}", it)
                    D_.mark(dve.tensor_tensor(Xi[s], T2[s], four(ident[:]), ALU.add), f"X0_{s}")
                    D_.mark(dve.tensor_tensor(Zi[s], LT[s], four(level0T), ALU.mult), f"Zm_{s}")
                    D_.wait(dve, f"Zm_{s}", it)
                    D_.mark(dve.tensor_tensor(Zi[s], Zi[s], four(ident[:]), ALU.add), f"Z0_{s}")
                for s in range(2):
                    masked("BrT", s, BrT, 1, upto_diag)
                for s in range(2):
                    masked("KrT", s, KrT, 2, upto_diag)
                for m in range(1, LEVELS):
                    for s in range(2):
                        masked(f"T{m}", s, T2, 3, level[m])
                    for s in range(2):
                        if m < LEVELS - 1:
                            added(f"X{m}", s, Xi, 0)
                        added(f"Z{m}", s, Zi, 1)
                for s in range(2):
                    P_.wait(dve, f"S_{s}", it)
                    D_.mark(dve.tensor_tensor(ST[s], ST[s], bank4(s, 1, N), ALU.add), f"Ssum_{s}")
                    D_.wait(dve, f"Ssum_{s}", it)
                    D_.mark(dve.tensor_tensor(ST[s], ST[s], fac[:, 4 * s:4 * s + 4, ds(it, 1)].to_broadcast([P, 4, N]),
                                              ALU.mult), f"S_{s}")
                    D_.wait(dve, f"S_{s}", it)
            def two(v, g):
                return fl(v[:, 2 * g:2 * g + 2, :])

            for g in range(4):
                dve.wait_ge(y_sum, g + 1)
                dve.scalar_tensor_tensor(out=two(YR, g), in0=BANK[4 + g][:, :], scalar=-1.0 / N, in1=two(YR, g),
                                         op0=ALU.mult, op1=ALU.add).then_inc(y_centred, 1)
            for g in range(4):
                dve.wait_ge(bonus_ready, g + 1)
                dve.tensor_tensor(two(BV, g), BANK[g][:, :], two(V_, g), ALU.mult).then_inc(bonus_took, 1)
            dve.wait_ge(y_sum, 8)
            own.link(dve.tensor_scalar(y_scale, BANK[4][:, 0:4 * NP_], 1.0 / N, GN_EPS, ALU.mult, ALU.add))
            dve.reciprocal(y_scale, y_scale).then_inc(y_var, 1)
            for g in range(4):
                dve.wait_ge(y_sum, 8 + g + 1)
                dve.tensor_tensor(two(YR, g), two(YR, g), BANK[4 + g][:, :], ALU.mult).then_inc(y_normed, 1)
            dve.wait_ge(bonus_took, 4)
            for g in range(4):
                dve.wait_ge(y_scaled, 2 * (g + 1))
                own.link(dve.tensor_tensor(two(YR, g), two(YR, g), two(BV, g), ALU.add))
                if g < 3:
                    dve.wait_ge(g_ready, g + 1)
                else:
                    dve.wait_ge(piece_done, n_wo2)
                k = slice(2 * g, 2 * g + 2)
                own.link(dve.tensor_tensor(two(YR, g), two(YR, g), BANK[g][:, :], ALU.mult))
                own.link(dve.tensor_copy(HH[:, k, :], YR[:, k, :]))
                dve.tensor_tensor(HL[:, k, :], YR[:, k, :], HH[:, k, :], ALU.subtract).then_inc(g_took, 2)
            for c in range(4):
                dve.wait_ge(piece_done, n_wo2 + PIECES * (c + 1))
                for t in range(TT):
                    xc = X[:, t, c * CH:(c + 1) * CH]
                    dve.tensor_tensor(xc, xc, BANK[4 + 2 * (c % 2) + t][:, :], ALU.add).then_inc(x_updated, 1)
            norm_dve(2)
            make_diag(2)
            ht_split(hf4, 8, 35, 0)
            own.link(dve.memset(RAWF[:, :, 0:2], 0.0))
            dve.memset(small[:, 502:503], 0.0).then_inc(up_taken, 1)
            tap = [VEC[f"conv{t}"][0] * P + VEC[f"conv{t}"][1] for t in range(3)]
            cb = VEC["ffn_conv_b_2"][0] * P + VEC["ffn_conv_b_2"][1]
            def split_hidden(g, dyn=None):
                tile = AC[:, PK * g:PK * (g + 1), :] if dyn is None else AC[:, ds(dyn * (2 * PK) + PK * g, PK), :]
                own.link(dve.tensor_copy(AH[:, g % 2], tile))
                dve.tensor_tensor(AL[:, g % 2], tile, AH[:, g % 2], ALU.subtract).then_inc(a_ready, 1)

            own.wait()
            def down_low(g, c, more=0):
                low_part(dve, n_dn + 4 * g + c, 1, more * PIECES, lo_ready_dve)

            def down_lows(g, more=0):
                for c in range(4):
                    down_low(g, c, more)

            def gate_up(i):
                dve.wait_ge(piece_done, i * (2 * PIECES) + (n_gu + PIECES))
                for f in range(4):
                    add_halves(RAWF[:, f, 2:L + 2], f, raw_taken)
                dve.wait_ge(raw_taken, i * 4 + (RAW_C + 4))
                for f in range(4):
                    w = lambda t: cols[:, ds(4 * i + (tap[t] + f), 1)]
                    own.mark(dve.tensor_scalar(CV[:, f, :], RAWF[:, f, 2:L + 2], w(2), cols[:, ds(4 * i + (cb + f), 1)],
                                               ALU.mult, ALU.add))
                own.wait()
                for f in range(4):
                    w = lambda t: cols[:, ds(4 * i + (tap[t] + f), 1)]
                    own.mark(dve.scalar_tensor_tensor(out=CV[:, f, :], in0=RAWF[:, f, 1:L + 1], scalar=w(1), in1=CV[:, f, :],
                                                      op0=ALU.mult, op1=ALU.add))
                own.wait()
                for f in range(4):
                    w = lambda t: cols[:, ds(4 * i + (tap[t] + f), 1)]
                    last = dve.scalar_tensor_tensor(out=CV[:, f, :], in0=RAWF[:, f, 0:L], scalar=w(0), in1=CV[:, f, :],
                                                    op0=ALU.mult, op1=ALU.add)
                last.then_inc(conv_ready, 1)
                if isinstance(i, int):
                    down_low(0, 0)
                    down_low(0, 1)
                dve.wait_ge(piece_done, i * (2 * PIECES) + (n_gu + 2 * PIECES))
                for f in range(4):
                    add_halves(UPS[:, f, :], 4 + f, up_taken)
                dve.wait_ge(up_taken, i * 4 + 5)
                dve.wait_ge(gate_act, i + 1)
                own.link(dve.tensor_tensor(AC[:, ds(4 * i, 4), :], CV, UPS, ALU.mult))

            with dve.Fori(0, FF // CH - 1) as i:
                own.enter(i, 9)
                gate_up(i)
                own.leave(FF // CH - 1)
            split_hidden(0)
            split_hidden(1)
            gate_up(FF // CH - 1)
            down_low(0, 2)
            down_low(0, 3)
            with dve.Fori(0, 4) as i:
                own.enter(i, 2)
                for g in (2, 3):
                    down_lows(g - 1, i * 2)
                    dve.wait_ge(piece_done, i * (2 * PIECES) + (n_dn + PIECES * (g - 1)))
                    split_hidden(g, i)
                own.leave(4)
            down_lows(9)
            dve.wait_ge(piece_done, n_dn + PIECES * 9)
            split_hidden(10)
            down_lows(10)
            for c in range(4):
                dve.wait_ge(piece_done, n_end - 3 + c)
                for t in range(TT):
                    xc = X[:, t, c * CH:(c + 1) * CH]
                    dve.tensor_tensor(xc, xc, BANK[2 * c + t][:, :], ALU.add).then_inc(x_updated, 1)
            norm_dve(3)
            dve.wait_ge(rstd_ready, 4)
            dve.wait_ge(fg_in, 16)
            for s in range(2):
                for t in range(TT):
                    o = slice(s * D // 2, (s + 1) * D // 2)
                    dve.scalar_tensor_tensor(out=XN3[:, t, o], in0=X[:, t, o], scalar=rstd[:, t:t + 1], in1=fg_row[:, o],
                                             op0=ALU.mult, op1=ALU.mult).then_inc(fin_ready, 1)


_INS = ["x", "c", "w_ada", "b_ada", "g_norm", "w_in", "q_norm_a", "k_norm_a", "k_norm_idx", "q_norm_b",
        "k_norm_b", "w_out", "positions_2", "attn_norm_g_2", "w_in_2", "rwkv_mu_2", "rwkv_w0_2", "rwkv_w2_2",
        "rwkv_a0_2", "rwkv_a2_2", "rwkv_g2_2", "rwkv_k_k_2", "rwkv_k_a_2", "rwkv_r_k_2", "rwkv_gn_w_2",
        "rwkv_gn_b_2", "mla_q_norm_g_2", "mla_w_uq_2", "mla_kv_norm_g_2", "mla_w_ukv_2", "w_out_2",
        "ffn_norm_g_2", "ffn_w_gate_2", "ffn_w_up_2", "ffn_conv_w_2", "ffn_conv_b_2", "ffn_w_down_2",
        "final_norm_g_2"]
_OUT = (1, L, D)


def kernel(**inputs):
    import concourse.bacc as bacc
    from concourse.bass_utils import run_bass_kernel_spmd

    nc = bacc.Bacc("TRN2", target_bir_lowering=False, num_devices=1)
    arrays, args = {}, {}
    for name in _INS:
        v = np.ascontiguousarray(inputs[name])
        arrays[f"in_{name}"] = v
        args[name] = nc.dram_tensor(f"in_{name}", v.shape, mybir.dt.from_np(v.dtype), kind="ExternalInput").ap()
    out = nc.dram_tensor("out", _OUT, F32, kind="ExternalOutput").ap()
    build(nc, args, out)
    return run_bass_kernel_spmd(nc, [arrays], core_ids=[0]).results[0]["out"]
```
